# Optimizing a Trainium2 kernel written in Bass

```python
import jax, jax.numpy as jnp
from jax import lax
import numpy as np

D_MODEL = 1024
BATCH = 1
SEQ = 256
DEPTH = 1

D_MIX = D_MODEL
HG_WIDTH = D_MIX // 2
HG_DK = 128
HG_DV = 128
HG_HEADS = HG_WIDTH // HG_DV
HG_CHUNK = 64
NSA_WIDTH = D_MIX - HG_WIDTH
NSA_DH = 64
NSA_HEADS = NSA_WIDTH // NSA_DH
NSA_KV_HEADS = 2
NSA_GROUP = NSA_HEADS // NSA_KV_HEADS
CMP_LEN = 32
CMP_STRIDE = 16
SLC_LEN = 64
SLC_TOPK = 16
WIN = 512
Q_BLOCK = 128
PLE_DIM = 256
PEER_HEADS = 8
PEER_NKEYS = 128
PEER_N = PEER_NKEYS * PEER_NKEYS
PEER_DKEY = 256
PEER_TOPK = 16
PEER_TOKEN_BLOCK = 128
EPS = 1e-6

KV_WIDTH = NSA_KV_HEADS * NSA_DH
SPLIT_SIZES = (HG_WIDTH, HG_WIDTH, HG_WIDTH, HG_WIDTH, NSA_WIDTH,
               KV_WIDTH, KV_WIDTH, KV_WIDTH, KV_WIDTH, KV_WIDTH, KV_WIDTH, 3 * NSA_HEADS)
SPLIT_POINTS = tuple(int(v) for v in np.cumsum(SPLIT_SIZES)[:-1])
D_IN = int(sum(SPLIT_SIZES))


def rmsnorm(x, g):
    x32 = x.astype(jnp.float32)
    y = x32 * lax.rsqrt(jnp.mean(x32 * x32, axis=-1, keepdims=True) + EPS)
    return (y * g.astype(jnp.float32)).astype(x.dtype)

def alibi_slopes(n_heads):
    return jnp.asarray(2.0 ** (-8.0 * np.arange(1, n_heads + 1) / n_heads), dtype=jnp.float32)

def masked_softmax(s, mask):
    s = jnp.where(mask, s, -jnp.inf)
    m = jnp.max(s, axis=-1, keepdims=True)
    m = jnp.where(jnp.isfinite(m), m, 0.0)
    e = jnp.where(mask, jnp.exp(s - m), 0.0)
    return e / jnp.maximum(jnp.sum(e, axis=-1, keepdims=True), 1e-30)

def hgrn2_mixer(q, f_logit, i_val, g, lb, out_gain):
    B, T, _ = q.shape
    f32 = jnp.float32
    C = HG_CHUNK
    n_chunk = T // C
    forget = lb + (1.0 - lb) * jax.nn.sigmoid(f_logit.astype(f32))
    log_f = jnp.log(forget)
    key = 1.0 - forget
    query = jax.nn.silu(q.astype(f32)) * HG_DK ** -0.5

    def chunks(a, d):
        return a.reshape(B, n_chunk, C, HG_HEADS, d).transpose(0, 3, 1, 2, 4)

    qc = chunks(query, HG_DK)
    kc = chunks(key, HG_DK)
    vc = chunks(i_val.astype(f32), HG_DV)
    G = jnp.cumsum(chunks(log_f, HG_DK), axis=3)
    G_ref = G[:, :, :, C // 2 - 1:C // 2]
    G_last = G[:, :, :, C - 1:C]
    causal = jnp.tril(jnp.ones((C, C), dtype=bool))
    a = jnp.einsum('bhntk,bhnsk->bhnts', qc * jnp.exp(G - G_ref), kc * jnp.exp(G_ref - G))
    o_intra = jnp.einsum('bhnts,bhnsv->bhntv', jnp.where(causal, a, 0.0), vc)
    q_in = jnp.moveaxis(qc * jnp.exp(G), 2, 0)
    k_in = jnp.moveaxis(kc * jnp.exp(G_last - G), 2, 0)
    v_in = jnp.moveaxis(vc, 2, 0)
    d_in = jnp.moveaxis(jnp.exp(G_last[:, :, :, 0]), 2, 0)

    def step(S, xs):
        q_t, k_t, v_t, d_t = xs
        o_t = jnp.einsum('bhtk,bhkv->bhtv', q_t, S)
        S = d_t[..., None] * S + jnp.einsum('bhtk,bhtv->bhkv', k_t, v_t)
        return S, o_t

    S0 = jnp.zeros((B, HG_HEADS, HG_DK, HG_DV), f32)
    _, o_inter = lax.scan(step, S0, (q_in, k_in, v_in, d_in))
    o = o_intra + jnp.moveaxis(o_inter, 0, 2)
    o = o.transpose(0, 2, 3, 1, 4).reshape(B, T, HG_HEADS, HG_DV)
    gate = jax.nn.silu(g.astype(f32)).reshape(B, T, HG_HEADS, HG_DV)
    return (rmsnorm(o, out_gain.reshape(HG_HEADS, HG_DV)) * gate).reshape(B, T, HG_WIDTH)

def cmp_to_slc(imp, n_slc):
    ratio = SLC_LEN // CMP_STRIDE
    span = CMP_LEN // CMP_STRIDE
    weights = np.convolve(np.ones(ratio), np.ones(span))
    n_cmp = imp.shape[-1]
    pad = n_slc * ratio + ratio + span - n_cmp
    padded = jnp.pad(imp, [(0, 0)] * (imp.ndim - 1) + [(0, pad)])
    out = float(weights[0]) * padded[..., 0:n_slc * ratio:ratio]
    for o in range(1, len(weights)):
        out = out + float(weights[o]) * padded[..., o:o + n_slc * ratio:ratio]
    return out

def nsa_mixer(q, k_cmp, v_cmp, k_slc, v_slc, k_win, v_win, gate_logit,
              q_gain, k_gain, cmp_pe, cmp_w1, cmp_w2, out_gain):
    B, T, _ = q.shape
    f32 = jnp.float32
    G, R = NSA_KV_HEADS, NSA_GROUP

    def heads(a, n):
        return a.astype(f32).reshape(B, T, n, NSA_DH).transpose(0, 2, 1, 3)

    qh = rmsnorm(heads(q, NSA_HEADS), q_gain) * NSA_DH ** -0.5
    qg = qh.reshape(B, G, R, T, NSA_DH)
    n_cmp = (T - CMP_LEN) // CMP_STRIDE + 1

    def compress(a, pe, w1, w2):
        c = a.reshape(B, G, T // CMP_STRIDE, CMP_STRIDE, NSA_DH)
        blk = jnp.concatenate([c[:, :, j:j + n_cmp] for j in range(CMP_LEN // CMP_STRIDE)], axis=3)
        blk = (blk + pe).reshape(B, G, n_cmp, CMP_LEN * NSA_DH)
        return jax.nn.gelu(blk @ w1) @ w2

    kc = rmsnorm(compress(heads(k_cmp, G), cmp_pe[0], cmp_w1[0], cmp_w2[0]), k_gain[0])
    vc = compress(heads(v_cmp, G), cmp_pe[1], cmp_w1[1], cmp_w2[1])
    cmp_end = jnp.arange(n_cmp) * CMP_STRIDE + CMP_LEN - 1
    n_slc = T // SLC_LEN
    top_n = min(SLC_TOPK, n_slc)
    k_sb = rmsnorm(heads(k_slc, G), k_gain[1]).reshape(B, G, n_slc, SLC_LEN, NSA_DH)
    v_sb = heads(v_slc, G).reshape(B, G, n_slc, SLC_LEN, NSA_DH)
    pad_w = ((0, 0), (0, 0), (WIN, 0), (0, 0))
    k_wp = jnp.pad(rmsnorm(heads(k_win, G), k_gain[2]), pad_w)
    v_wp = jnp.pad(heads(v_win, G), pad_w)
    gates = jax.nn.sigmoid(gate_logit.astype(f32)).reshape(B, T, NSA_HEADS, 3).transpose(0, 2, 1, 3)
    gates = gates.reshape(B, G, R, T, 3)
    slopes = alibi_slopes(NSA_HEADS).reshape(1, G, R, 1, 1)
    gather_blocks = jax.vmap(jax.vmap(lambda blocks, ix: blocks[ix]))

    def query_block(b):
        t0 = b * Q_BLOCK
        qb = lax.dynamic_slice_in_dim(qg, t0, Q_BLOCK, axis=3)
        gb = lax.dynamic_slice_in_dim(gates, t0, Q_BLOCK, axis=3)
        t = t0 + jnp.arange(Q_BLOCK)
        dist_c = t[:, None] - cmp_end[None, :]
        s_c = jnp.einsum('bgrtd,bgnd->bgrtn', qb, kc) - slopes * dist_c
        p_c = masked_softmax(s_c, dist_c >= 0)
        o_c = jnp.einsum('bgrtn,bgnd->bgrtd', p_c, vc)
        imp = cmp_to_slc(jnp.sum(p_c, axis=2), n_slc)
        blk_id = jnp.arange(n_slc)[None, :]
        cur = (t // SLC_LEN)[:, None]
        forced = (blk_id == 0) | (blk_id == cur) | (blk_id == cur - 1)
        imp = jnp.where(forced, jnp.inf, jnp.where(blk_id <= cur, imp, -jnp.inf))
        _, sel = lax.top_k(imp, top_n)
        ks = gather_blocks(k_sb, sel).reshape(B, G, Q_BLOCK, top_n * SLC_LEN, NSA_DH)
        vs = gather_blocks(v_sb, sel).reshape(B, G, Q_BLOCK, top_n * SLC_LEN, NSA_DH)
        pos = (sel[..., None] * SLC_LEN + jnp.arange(SLC_LEN)).reshape(B, G, Q_BLOCK, top_n * SLC_LEN)
        dist_s = (t[:, None] - pos)[:, :, None]
        s_s = jnp.einsum('bgrtd,bgtmd->bgrtm', qb, ks) - slopes * dist_s
        p_s = masked_softmax(s_s, dist_s >= 0)
        o_s = jnp.einsum('bgrtm,bgtmd->bgrtd', p_s, vs)
        kw = lax.dynamic_slice_in_dim(k_wp, t0, WIN + Q_BLOCK, axis=2)
        vw = lax.dynamic_slice_in_dim(v_wp, t0, WIN + Q_BLOCK, axis=2)
        pos_w = t0 - WIN + jnp.arange(WIN + Q_BLOCK)
        dist_w = t[:, None] - pos_w[None, :]
        valid_w = (dist_w >= 0) & (dist_w < WIN) & (pos_w[None, :] >= 0)
        s_w = jnp.einsum('bgrtd,bgsd->bgrts', qb, kw) - slopes * dist_w
        p_w = masked_softmax(s_w, valid_w)
        o_w = jnp.einsum('bgrts,bgsd->bgrtd', p_w, vw)
        return gb[..., 0:1] * o_c + gb[..., 1:2] * o_s + gb[..., 2:3] * o_w

    o = lax.map(query_block, jnp.arange(T // Q_BLOCK))
    o = o.transpose(1, 0, 4, 2, 3, 5).reshape(B, T, NSA_HEADS, NSA_DH)
    return rmsnorm(o, out_gain.reshape(NSA_HEADS, NSA_DH)).reshape(B, T, NSA_WIDTH)

def peer_ffn(h, wq, sub_keys, u, v):
    B, T, D = h.shape
    f32 = jnp.float32
    tokens = h.reshape(-1, PEER_TOKEN_BLOCK, D)

    def token_block(xt):
        q = (xt @ wq).astype(f32).reshape(PEER_TOKEN_BLOCK, PEER_HEADS, 2, PEER_DKEY // 2)
        s = jnp.einsum('thcd,hckd->thck', q, sub_keys.astype(f32))
        top_s, top_i = lax.top_k(s, PEER_TOPK)
        cand = top_s[:, :, 0, :, None] + top_s[:, :, 1, None, :]
        best_s, best_c = lax.top_k(cand.reshape(PEER_TOKEN_BLOCK, PEER_HEADS, PEER_TOPK * PEER_TOPK), PEER_TOPK)
        i1 = jnp.take_along_axis(top_i[:, :, 0], best_c // PEER_TOPK, axis=-1)
        i2 = jnp.take_along_axis(top_i[:, :, 1], best_c % PEER_TOPK, axis=-1)
        expert = i1 * PEER_NKEYS + i2
        w = jax.nn.softmax(best_s, axis=-1)
        act = jax.nn.gelu(jnp.einsum('thkd,td->thk', u[expert].astype(f32), xt.astype(f32)))
        return jnp.einsum('thk,thkd->td', w * act, v[expert].astype(f32))

    return lax.map(token_block, tokens).reshape(B, T, D).astype(h.dtype)

def first_inputs(seed: int = 0) -> dict:
    key = jax.random.key(seed)
    ks = jax.random.split(key, 21)
    n = jax.random.normal
    f32 = jnp.float32

    def gain(k, shape):
        return 1.0 + 0.02 * n(k, shape, f32)

    return {
        'x': n(ks[0], (BATCH, SEQ, D_MODEL), f32),
        'p': n(ks[1], (DEPTH, BATCH, SEQ, PLE_DIM), f32),
        'mix_norm': gain(ks[2], (DEPTH, D_MODEL)),
        'w_in': n(ks[3], (DEPTH, D_MODEL, D_IN), f32) * D_MODEL ** -0.5,
        'hg_lb_logits': 0.1 * n(ks[4], (DEPTH + 1, HG_WIDTH), f32),
        'hg_out_norm': gain(ks[5], (DEPTH, HG_WIDTH)),
        'nsa_q_norm': gain(ks[6], (DEPTH, NSA_DH)),
        'nsa_k_norm': gain(ks[7], (DEPTH, 3, NSA_DH)),
        'cmp_pe': 0.02 * n(ks[8], (DEPTH, 2, CMP_LEN, NSA_DH), f32),
        'cmp_w1': n(ks[9], (DEPTH, 2, CMP_LEN * NSA_DH, NSA_DH), f32) * (CMP_LEN * NSA_DH) ** -0.5,
        'cmp_w2': n(ks[10], (DEPTH, 2, NSA_DH, NSA_DH), f32) * NSA_DH ** -0.5,
        'nsa_out_norm': gain(ks[11], (DEPTH, NSA_WIDTH)),
        'w_out': n(ks[12], (DEPTH, D_MIX, D_MODEL), f32) * D_MIX ** -0.5,
        'ffn_norm': gain(ks[13], (DEPTH, D_MODEL)),
        'peer_wq': n(ks[14], (DEPTH, D_MODEL, PEER_HEADS * PEER_DKEY), f32) * D_MODEL ** -0.5,
        'peer_keys': n(ks[15], (DEPTH, PEER_HEADS, 2, PEER_NKEYS, PEER_DKEY // 2), f32) * (PEER_DKEY // 2) ** -0.5,
        'peer_u': n(ks[16], (DEPTH, PEER_N, D_MODEL), f32) * D_MODEL ** -0.5,
        'peer_v': n(ks[17], (DEPTH, PEER_N, D_MODEL), f32) * PEER_HEADS ** -0.5,
        'ple_proj': n(ks[18], (DEPTH, PLE_DIM, D_MODEL), f32) * PLE_DIM ** -0.5,
        'ple_gate_norm': gain(ks[19], (DEPTH, D_MODEL)),
        'ple_gate_w': n(ks[20], (DEPTH, D_MODEL, D_MODEL), f32) * D_MODEL ** -0.5,
    }

def first_block(x, p, mix_norm, w_in, hg_lb_logits, hg_out_norm, nsa_q_norm, nsa_k_norm,
              cmp_pe, cmp_w1, cmp_w2, nsa_out_norm, w_out, ffn_norm, peer_wq, peer_keys,
              peer_u, peer_v, ple_proj, ple_gate_norm, ple_gate_w):
    lb_table = jnp.cumsum(jax.nn.softmax(hg_lb_logits.astype(jnp.float32), axis=0), axis=0)
    h = x
    for i in range(DEPTH):
        a = rmsnorm(h, mix_norm[i])
        proj = a @ w_in[i]
        (hg_q, hg_f, hg_i, hg_g, n_q, n_kc, n_vc, n_ks, n_vs, n_kw, n_vw, n_gate) = jnp.split(proj, SPLIT_POINTS, axis=-1)
        o_hg = hgrn2_mixer(hg_q, hg_f, hg_i, hg_g, lb_table[i], hg_out_norm[i])
        o_nsa = nsa_mixer(n_q, n_kc, n_vc, n_ks, n_vs, n_kw, n_vw, n_gate,
                          nsa_q_norm[i], nsa_k_norm[i], cmp_pe[i], cmp_w1[i], cmp_w2[i], nsa_out_norm[i])
        mixed = jnp.concatenate([o_hg, o_nsa], axis=-1).astype(h.dtype)
        h = h + mixed @ w_out[i]
        h = h + peer_ffn(rmsnorm(h, ffn_norm[i]), peer_wq[i], peer_keys[i], peer_u[i], peer_v[i])
        gate = jax.nn.sigmoid(rmsnorm(h, ple_gate_norm[i]) @ ple_gate_w[i])
        h = h + (p[i] @ ple_proj[i]) * gate
    return h


DEPTH_2 = 2

GRID_W = 64
CTX_LEN = 256
N_MIXERS = 4
HEAD_DIM = 64
ROPE_THETA = 10000.0
NA_HEADS = 16
NA_WIN_H = 8
NA_WIN_W = 16
GQA_HEADS = 16
GQA_KV_HEADS = 4
SWA_HEADS = 16
SWA_KV_HEADS = 2
SWA_WINDOW = 128
LRU_WIDTH = D_MODEL
LRU_BLOCKS = 16
LRU_BLOCK_DIM = LRU_WIDTH // LRU_BLOCKS
CONV_WIDTH = 4
LRU_C = 8.0
FFN_HIDDEN = ((8 * D_MODEL + 2) // 3 + 255) // 256 * 256
N_MOD = 6
MASK_VALUE = -1e30
N_NA_LAYERS = (DEPTH_2 + 3) // N_MIXERS
N_GQA_LAYERS = (DEPTH_2 + 2) // N_MIXERS
N_SWA_LAYERS = (DEPTH_2 + 1) // N_MIXERS
N_LRU_LAYERS = DEPTH_2 // N_MIXERS


def rms_norm(x, g):
    xf = x.astype(jnp.float32)
    y = xf * lax.rsqrt(jnp.mean(xf * xf, axis=-1, keepdims=True) + EPS)
    return (y * g.astype(jnp.float32)).astype(x.dtype)

def ada_norm(x, g, shift, scale):
    return rms_norm(x, g) * (1.0 + scale) + shift

def axial_angles(n_tokens):
    t = jnp.arange(n_tokens, dtype=jnp.int32)
    row = (t // GRID_W).astype(jnp.float32)
    col = (t % GRID_W).astype(jnp.float32)
    half = HEAD_DIM // 2
    inv_freq = 1.0 / (ROPE_THETA ** (jnp.arange(0, half, 2, dtype=jnp.float32) / half))
    return row[:, None] * inv_freq, col[:, None] * inv_freq

def _rotate(x, ang):
    cos = jnp.cos(ang)[None, :, None, :].astype(x.dtype)
    sin = jnp.sin(ang)[None, :, None, :].astype(x.dtype)
    x1, x2 = jnp.split(x, 2, axis=-1)
    return jnp.concatenate([x1 * cos - x2 * sin, x1 * sin + x2 * cos], axis=-1)

def axial_rope(x, ang_row, ang_col):
    xr, xc = jnp.split(x, 2, axis=-1)
    return jnp.concatenate([_rotate(xr, ang_row), _rotate(xc, ang_col)], axis=-1)

def project_qkv(h, w_qkv, n_q, n_kv):
    b, t, _ = h.shape
    qkv = h @ w_qkv
    q, k, v = jnp.split(qkv, [n_q * HEAD_DIM, (n_q + n_kv) * HEAD_DIM], axis=-1)
    return (q.reshape(b, t, n_q, HEAD_DIM), k.reshape(b, t, n_kv, HEAD_DIM), v.reshape(b, t, n_kv, HEAD_DIM))

def attn_probs(s, sink=None):
    if sink is None:
        return jax.nn.softmax(s, axis=-1)
    sk = sink.astype(jnp.float32)[None, :, :, None, None]
    m = jnp.maximum(jnp.max(s, axis=-1, keepdims=True), sk)
    e = jnp.exp(s - m)
    return e / (jnp.sum(e, axis=-1, keepdims=True) + jnp.exp(sk - m))

def context_attention(q, k, v, sink=None):
    b, t, n_q, dh = q.shape
    n_kv = k.shape[2]
    qg = q.reshape(b, t, n_kv, n_q // n_kv, dh)
    s = jnp.einsum('bqhgd,bshd->bhgqs', qg, k).astype(jnp.float32) * dh ** -0.5
    p = attn_probs(s, sink).astype(v.dtype)
    o = jnp.einsum('bhgqs,bshd->bqhgd', p, v)
    return o.reshape(b, t, n_q * dh)

def neighbourhood_attention_mixer(h_lat, h_ctx, w_qkv, rpb, w_o, with_ctx_out):
    b, s_len, _ = h_lat.shape
    rows = s_len // GRID_W
    kh = min(NA_WIN_H, rows)
    scale = HEAD_DIM ** -0.5
    q, k, v = project_qkv(h_lat, w_qkv, NA_HEADS, NA_HEADS)
    qc, kc, vc = project_qkv(h_ctx, w_qkv, NA_HEADS, NA_HEADS)
    k_grid = k.reshape(b, rows, GRID_W, NA_HEADS, HEAD_DIM)
    v_grid = v.reshape(b, rows, GRID_W, NA_HEADS, HEAD_DIM)
    q_rows = jnp.moveaxis(q.reshape(b, rows, GRID_W, NA_HEADS, HEAD_DIM), 1, 0)
    qcol = jnp.arange(GRID_W, dtype=jnp.int32)
    kcol = jnp.arange(GRID_W, dtype=jnp.int32)
    col_start = jnp.clip(qcol - NA_WIN_W // 2, 0, GRID_W - NA_WIN_W)
    col_in = (kcol[None, :] >= col_start[:, None]) & (kcol[None, :] < col_start[:, None] + NA_WIN_W)
    dcol = jnp.clip(kcol[None, :] - qcol[:, None] + NA_WIN_W - 1, 0, 2 * NA_WIN_W - 2)
    n_nb = kh * GRID_W

    def row_block(args):
        r, q_r = args
        r0 = jnp.clip(r - kh // 2, 0, rows - kh)
        k_b = lax.dynamic_slice_in_dim(k_grid, r0, kh, axis=1)
        v_b = lax.dynamic_slice_in_dim(v_grid, r0, kh, axis=1).reshape(b, n_nb, NA_HEADS, HEAD_DIM)
        drow = r0 + jnp.arange(kh, dtype=jnp.int32) - r + NA_WIN_H - 1
        bias = rpb[:, drow[None, :, None], dcol[:, None, :]]
        s_nb = jnp.einsum('bqhd,biwhd->bhqiw', q_r, k_b).astype(jnp.float32) * scale + bias.astype(jnp.float32)[None]
        s_nb = jnp.where(col_in[None, None, :, None, :], s_nb, MASK_VALUE).reshape(b, NA_HEADS, GRID_W, n_nb)
        s_cx = jnp.einsum('bqhd,bshd->bhqs', q_r, kc).astype(jnp.float32) * scale
        p = jax.nn.softmax(jnp.concatenate([s_nb, s_cx], axis=-1), axis=-1).astype(v.dtype)
        return (jnp.einsum('bhqn,bnhd->bqhd', p[..., :n_nb], v_b)
                + jnp.einsum('bhqs,bshd->bqhd', p[..., n_nb:], vc))

    o = lax.map(row_block, (jnp.arange(rows, dtype=jnp.int32), q_rows))
    y_lat = jnp.moveaxis(o, 0, 1).reshape(b, s_len, NA_HEADS * HEAD_DIM) @ w_o
    y_ctx = context_attention(qc, kc, vc) @ w_o if with_ctx_out else None
    return y_lat, y_ctx

def qknorm_gqa_mixer(h_lat, h_ctx, w_qkv, q_gain, k_gain, w_o, ang_row, ang_col, with_ctx_out):
    b, s_len, _ = h_lat.shape
    g = GQA_HEADS // GQA_KV_HEADS
    scale = HEAD_DIM ** -0.5
    q, k, v = project_qkv(h_lat, w_qkv, GQA_HEADS, GQA_KV_HEADS)
    qc, kc, vc = project_qkv(h_ctx, w_qkv, GQA_HEADS, GQA_KV_HEADS)
    q = axial_rope(rms_norm(q, q_gain), ang_row, ang_col)
    k = axial_rope(rms_norm(k, k_gain), ang_row, ang_col)
    qc = rms_norm(qc, q_gain)
    kc = rms_norm(kc, k_gain)
    k_all = jnp.concatenate([kc, k], axis=1)
    v_all = jnp.concatenate([vc, v], axis=1)
    nb = s_len // Q_BLOCK
    q_blocks = jnp.moveaxis(q.reshape(b, nb, Q_BLOCK, GQA_KV_HEADS, g, HEAD_DIM), 1, 0)

    def block(q_b):
        s = jnp.einsum('bqhgd,bshd->bhgqs', q_b, k_all).astype(jnp.float32) * scale
        p = jax.nn.softmax(s, axis=-1).astype(v_all.dtype)
        return jnp.einsum('bhgqs,bshd->bqhgd', p, v_all)

    o = lax.map(block, q_blocks)
    y_lat = jnp.moveaxis(o, 0, 1).reshape(b, s_len, GQA_HEADS * HEAD_DIM) @ w_o
    y_ctx = context_attention(qc, kc, vc) @ w_o if with_ctx_out else None
    return y_lat, y_ctx

def sliding_window_mixer(h_lat, h_ctx, w_qkv, sinks, w_o, ang_row, ang_col, with_ctx_out):
    b, s_len, _ = h_lat.shape
    g = SWA_HEADS // SWA_KV_HEADS
    scale = HEAD_DIM ** -0.5
    q, k, v = project_qkv(h_lat, w_qkv, SWA_HEADS, SWA_KV_HEADS)
    qc, kc, vc = project_qkv(h_ctx, w_qkv, SWA_HEADS, SWA_KV_HEADS)
    q = axial_rope(q, ang_row, ang_col)
    k = axial_rope(k, ang_row, ang_col)
    sink = sinks.reshape(SWA_KV_HEADS, g)
    band = Q_BLOCK + 2 * SWA_WINDOW
    pad = ((0, 0), (SWA_WINDOW, SWA_WINDOW), (0, 0), (0, 0))
    k_pad = jnp.pad(k, pad)
    v_pad = jnp.pad(v, pad)
    nb = s_len // Q_BLOCK
    q_blocks = jnp.moveaxis(q.reshape(b, nb, Q_BLOCK, SWA_KV_HEADS, g, HEAD_DIM), 1, 0)

    def block(args):
        j, q_b = args
        start = j * Q_BLOCK
        k_b = lax.dynamic_slice_in_dim(k_pad, start, band, axis=1)
        v_b = lax.dynamic_slice_in_dim(v_pad, start, band, axis=1)
        qpos = start + jnp.arange(Q_BLOCK, dtype=jnp.int32)
        kpos = start - SWA_WINDOW + jnp.arange(band, dtype=jnp.int32)
        valid = ((jnp.abs(qpos[:, None] - kpos[None, :]) <= SWA_WINDOW)
                 & (kpos[None, :] >= 0) & (kpos[None, :] < s_len))
        s_loc = jnp.einsum('bqhgd,bshd->bhgqs', q_b, k_b).astype(jnp.float32) * scale
        s_loc = jnp.where(valid, s_loc, MASK_VALUE)
        s_cx = jnp.einsum('bqhgd,bshd->bhgqs', q_b, kc).astype(jnp.float32) * scale
        p = attn_probs(jnp.concatenate([s_loc, s_cx], axis=-1), sink).astype(v.dtype)
        return (jnp.einsum('bhgqs,bshd->bqhgd', p[..., :band], v_b)
                + jnp.einsum('bhgqs,bshd->bqhgd', p[..., band:], vc))

    o = lax.map(block, (jnp.arange(nb, dtype=jnp.int32), q_blocks))
    y_lat = jnp.moveaxis(o, 0, 1).reshape(b, s_len, SWA_HEADS * HEAD_DIM) @ w_o
    y_ctx = context_attention(qc, kc, vc, sink) @ w_o if with_ctx_out else None
    return y_lat, y_ctx

def centred_depthwise_conv(x, w, bias):
    t = x.shape[1]
    left = CONV_WIDTH // 2
    xp = jnp.pad(x, ((0, 0), (left, CONV_WIDTH - 1 - left), (0, 0)))
    return sum(xp[:, kk:kk + t] * w[kk] for kk in range(CONV_WIDTH)) + bias

def rglru_coeffs(x, w_a, b_a, w_x, b_x, lam):
    b, t, _ = x.shape
    xf = x.astype(jnp.float32)
    xb = xf.reshape(b, t, LRU_BLOCKS, LRU_BLOCK_DIM)
    r = jax.nn.sigmoid(jnp.einsum('btnd,nde->btne', xb, w_a.astype(jnp.float32)).reshape(b, t, LRU_WIDTH) + b_a.astype(jnp.float32))
    ig = jax.nn.sigmoid(jnp.einsum('btnd,nde->btne', xb, w_x.astype(jnp.float32)).reshape(b, t, LRU_WIDTH) + b_x.astype(jnp.float32))
    log_a = -LRU_C * r * jax.nn.softplus(-lam.astype(jnp.float32))
    return jnp.exp(log_a), jnp.sqrt(-jnp.expm1(2.0 * log_a)) * (ig * xf)

def linear_scan(a, bx, h0):
    def combine(left, right):
        a_l, b_l = left
        a_r, b_r = right
        return a_r * a_l, a_r * b_l + b_r
    a_cum, b_cum = lax.associative_scan(combine, (a, bx), axis=1)
    return a_cum * h0[:, None, :] + b_cum

def rglru_mixer(h_lat, h_ctx, w_in, conv_w, conv_b, w_a, b_a, w_x, b_x, lam, w_out, with_ctx_out):
    def branches(h):
        xr, gate = jnp.split(h @ w_in, 2, axis=-1)
        return centred_depthwise_conv(xr, conv_w, conv_b), jax.nn.gelu(gate, approximate=True)

    xc, gc = branches(h_ctx)
    xl, gl = branches(h_lat)
    hc_sum = jnp.zeros(xc.shape, jnp.float32)
    hl_sum = jnp.zeros(xl.shape, jnp.float32)
    for d in range(2):
        ac, bc = rglru_coeffs(xc, w_a[d], b_a[d], w_x[d], b_x[d], lam[d])
        al, bl = rglru_coeffs(xl, w_a[d], b_a[d], w_x[d], b_x[d], lam[d])
        if d == 1:
            ac, bc, al, bl = jnp.flip(ac, 1), jnp.flip(bc, 1), jnp.flip(al, 1), jnp.flip(bl, 1)
        hc = linear_scan(ac, bc, jnp.zeros_like(bc[:, 0]))
        hl = linear_scan(al, bl, hc[:, -1])
        if d == 1:
            hc, hl = jnp.flip(hc, 1), jnp.flip(hl, 1)
        hc_sum = hc_sum + hc
        hl_sum = hl_sum + hl
    y_lat = (hl_sum.astype(h_lat.dtype) * gl) @ w_out
    y_ctx = (hc_sum.astype(h_ctx.dtype) * gc) @ w_out if with_ctx_out else None
    return y_lat, y_ctx

def swiglu_ffn(h, w_in, w_out):
    a, g = jnp.split(h @ w_in, 2, axis=-1)
    return (jax.nn.silu(a) * g) @ w_out

def second_inputs(seed: int = 0) -> dict:
    key = jax.random.key(seed)
    ks = jax.random.split(key, 32)

    def nrm(k, shape, scale):
        return jax.random.normal(k, shape, jnp.float32) * scale

    def gain(k, shape):
        return 1.0 + 0.02 * jax.random.normal(k, shape, jnp.float32)

    d = D_MODEL
    a0 = jnp.sqrt(jax.random.uniform(ks[26], (N_LRU_LAYERS, 2, LRU_WIDTH), jnp.float32, 0.81, 0.998))
    return {
        'x': nrm(ks[0], (BATCH, SEQ, d), 1.0),
        'c': nrm(ks[1], (BATCH, d), 1.0),
        'ctx': nrm(ks[2], (BATCH, CTX_LEN, d), 1.0),
        'c_ctx': nrm(ks[3], (d,), 1.0),
        'ada_w': nrm(ks[4], (DEPTH_2, d, N_MOD * d), 0.5 * d ** -0.5),
        'ada_b': nrm(ks[5], (DEPTH_2, N_MOD * d), 0.02),
        'norm_mix': gain(ks[6], (DEPTH_2, d)),
        'norm_ffn': gain(ks[7], (DEPTH_2, d)),
        'norm_final': gain(ks[8], (d,)),
        'ffn_w_in': nrm(ks[9], (DEPTH_2, d, 2 * FFN_HIDDEN), d ** -0.5),
        'ffn_w_out': nrm(ks[10], (DEPTH_2, FFN_HIDDEN, d), FFN_HIDDEN ** -0.5),
        'na_w_qkv': nrm(ks[11], (N_NA_LAYERS, d, 3 * NA_HEADS * HEAD_DIM), d ** -0.5),
        'na_rpb': nrm(ks[12], (N_NA_LAYERS, NA_HEADS, 2 * NA_WIN_H - 1, 2 * NA_WIN_W - 1), 0.1),
        'na_w_o': nrm(ks[13], (N_NA_LAYERS, NA_HEADS * HEAD_DIM, d), (NA_HEADS * HEAD_DIM) ** -0.5),
        'gqa_w_qkv': nrm(ks[14], (N_GQA_LAYERS, d, (GQA_HEADS + 2 * GQA_KV_HEADS) * HEAD_DIM), d ** -0.5),
        'gqa_q_gain': gain(ks[15], (N_GQA_LAYERS, HEAD_DIM)),
        'gqa_k_gain': gain(ks[16], (N_GQA_LAYERS, HEAD_DIM)),
        'gqa_w_o': nrm(ks[17], (N_GQA_LAYERS, GQA_HEADS * HEAD_DIM, d), (GQA_HEADS * HEAD_DIM) ** -0.5),
        'swa_w_qkv': nrm(ks[18], (N_SWA_LAYERS, d, (SWA_HEADS + 2 * SWA_KV_HEADS) * HEAD_DIM), d ** -0.5),
        'swa_sinks': nrm(ks[19], (N_SWA_LAYERS, SWA_HEADS), 0.5),
        'swa_w_o': nrm(ks[20], (N_SWA_LAYERS, SWA_HEADS * HEAD_DIM, d), (SWA_HEADS * HEAD_DIM) ** -0.5),
        'lru_w_in': nrm(ks[21], (N_LRU_LAYERS, d, 2 * LRU_WIDTH), d ** -0.5),
        'lru_conv_w': nrm(ks[22], (N_LRU_LAYERS, CONV_WIDTH, LRU_WIDTH), CONV_WIDTH ** -0.5),
        'lru_conv_b': nrm(ks[23], (N_LRU_LAYERS, LRU_WIDTH), 0.02),
        'lru_w_a': nrm(ks[24], (N_LRU_LAYERS, 2, LRU_BLOCKS, LRU_BLOCK_DIM, LRU_BLOCK_DIM), LRU_BLOCK_DIM ** -0.5),
        'lru_b_a': nrm(ks[25], (N_LRU_LAYERS, 2, LRU_WIDTH), 0.02),
        'lru_w_x': nrm(ks[27], (N_LRU_LAYERS, 2, LRU_BLOCKS, LRU_BLOCK_DIM, LRU_BLOCK_DIM), LRU_BLOCK_DIM ** -0.5),
        'lru_b_x': nrm(ks[28], (N_LRU_LAYERS, 2, LRU_WIDTH), 0.02),
        'lru_lam': jnp.log(a0) - jnp.log1p(-a0),
        'lru_w_out': nrm(ks[29], (N_LRU_LAYERS, LRU_WIDTH, d), LRU_WIDTH ** -0.5),
    }

def second_block(x, c, ctx, c_ctx, ada_w, ada_b, norm_mix, norm_ffn, norm_final, ffn_w_in, ffn_w_out,
              na_w_qkv, na_rpb, na_w_o, gqa_w_qkv, gqa_q_gain, gqa_k_gain, gqa_w_o,
              swa_w_qkv, swa_sinks, swa_w_o, lru_w_in, lru_conv_w, lru_conv_b, lru_w_a, lru_b_a,
              lru_w_x, lru_b_x, lru_lam, lru_w_out):
    s_len = x.shape[1]
    ang_row, ang_col = axial_angles(s_len)
    silu_c = jax.nn.silu(c)
    silu_cc = jax.nn.silu(c_ctx)
    h = x
    hc = ctx
    for i in range(DEPTH_2):
        kind = i % N_MIXERS
        slot = i // N_MIXERS
        ctx_out = i < DEPTH_2 - 1
        mod_l = (silu_c @ ada_w[i] + ada_b[i])[:, None, :]
        mod_c = (silu_cc @ ada_w[i] + ada_b[i])[None, None, :]
        sh1_l, sc1_l, g1_l, sh2_l, sc2_l, g2_l = jnp.split(mod_l, N_MOD, axis=-1)
        sh1_c, sc1_c, g1_c, sh2_c, sc2_c, g2_c = jnp.split(mod_c, N_MOD, axis=-1)
        a_l = ada_norm(h, norm_mix[i], sh1_l, sc1_l)
        a_c = ada_norm(hc, norm_mix[i], sh1_c, sc1_c)
        if kind == 0:
            y_l, y_c = neighbourhood_attention_mixer(a_l, a_c, na_w_qkv[slot], na_rpb[slot], na_w_o[slot], ctx_out)
        elif kind == 1:
            y_l, y_c = qknorm_gqa_mixer(a_l, a_c, gqa_w_qkv[slot], gqa_q_gain[slot], gqa_k_gain[slot],
                                        gqa_w_o[slot], ang_row, ang_col, ctx_out)
        elif kind == 2:
            y_l, y_c = sliding_window_mixer(a_l, a_c, swa_w_qkv[slot], swa_sinks[slot], swa_w_o[slot],
                                            ang_row, ang_col, ctx_out)
        else:
            y_l, y_c = rglru_mixer(a_l, a_c, lru_w_in[slot], lru_conv_w[slot], lru_conv_b[slot],
                                   lru_w_a[slot], lru_b_a[slot], lru_w_x[slot], lru_b_x[slot],
                                   lru_lam[slot], lru_w_out[slot], ctx_out)
        h = h + g1_l * y_l
        h = h + g2_l * swiglu_ffn(ada_norm(h, norm_ffn[i], sh2_l, sc2_l), ffn_w_in[i], ffn_w_out[i])
        if ctx_out:
            hc = hc + g1_c * y_c
            hc = hc + g2_c * swiglu_ffn(ada_norm(hc, norm_ffn[i], sh2_c, sc2_c), ffn_w_in[i], ffn_w_out[i])
    return rms_norm(h, norm_final)


def setup_inputs(seed=0):
    out = dict(first_inputs(seed))
    for name, value in second_inputs(seed + 1).items():
        if name != "x":
            out[name + "_2"] = value
    return out


def reference(
    x, p, mix_norm, w_in, hg_lb_logits, hg_out_norm, nsa_q_norm, nsa_k_norm, cmp_pe, cmp_w1,
    cmp_w2, nsa_out_norm, w_out, ffn_norm, peer_wq, peer_keys, peer_u, peer_v, ple_proj,
    ple_gate_norm, ple_gate_w, c_2, ctx_2, c_ctx_2, ada_w_2, ada_b_2, norm_mix_2, norm_ffn_2,
    norm_final_2, ffn_w_in_2, ffn_w_out_2, na_w_qkv_2, na_rpb_2, na_w_o_2, gqa_w_qkv_2,
    gqa_q_gain_2, gqa_k_gain_2, gqa_w_o_2, swa_w_qkv_2, swa_sinks_2, swa_w_o_2, lru_w_in_2,
    lru_conv_w_2, lru_conv_b_2, lru_w_a_2, lru_b_a_2, lru_w_x_2, lru_b_x_2, lru_lam_2,
    lru_w_out_2,
):
    x = first_block(
        x, p, mix_norm, w_in, hg_lb_logits, hg_out_norm, nsa_q_norm, nsa_k_norm, cmp_pe, cmp_w1,
        cmp_w2, nsa_out_norm, w_out, ffn_norm, peer_wq, peer_keys, peer_u, peer_v, ple_proj,
        ple_gate_norm, ple_gate_w,
    )
    return second_block(
        x, c_2, ctx_2, c_ctx_2, ada_w_2, ada_b_2, norm_mix_2, norm_ffn_2, norm_final_2,
        ffn_w_in_2, ffn_w_out_2, na_w_qkv_2, na_rpb_2, na_w_o_2, gqa_w_qkv_2, gqa_q_gain_2,
        gqa_k_gain_2, gqa_w_o_2, swa_w_qkv_2, swa_sinks_2, swa_w_o_2, lru_w_in_2, lru_conv_w_2,
        lru_conv_b_2, lru_w_a_2, lru_b_a_2, lru_w_x_2, lru_b_x_2, lru_lam_2, lru_w_out_2,
    )


_drawn_inputs = setup_inputs


def setup_inputs(seed=0):
    import zlib

    import numpy as np

    out = dict(_drawn_inputs(seed))
    spreads = {}
    factors = {'hg_lb_logits': 5.987,
     'hg_out_norm': 4.235,
     'nsa_q_norm': 3.884,
     'nsa_k_norm': 4.191,
     'cmp_pe': 2.918,
     'nsa_out_norm': 3.095,
     'ffn_norm': 2.823,
     'ple_gate_norm': 8.0,
     'ada_b_2': 3.045,
     'norm_mix_2': 8.0,
     'norm_ffn_2': 8.0,
     'norm_final_2': 2.718,
     'na_rpb_2': 8.0,
     'gqa_q_gain_2': 8.0,
     'gqa_k_gain_2': 8.0}
    for name, (base, spread) in spreads.items():
        noise = np.random.default_rng([zlib.crc32(name.encode()), seed]).standard_normal(out[name].shape)
        drawn = base * np.exp(spread * noise) if base else spread * noise
        out[name] = __import__('jax').numpy.asarray(drawn.astype(out[name].dtype))
    for name, factor in factors.items():
        out[name] = (out[name] * factor).astype(out[name].dtype)
    return out
```

```python
from contextlib import ExitStack

import numpy as np

import concourse.bass as bass
from concourse import mybir

F32 = mybir.dt.float32
F32R = mybir.dt.float32r
I32 = mybir.dt.int32
U32 = mybir.dt.uint32
ACT = mybir.ActivationFunctionType
ALU = mybir.AluOpType
AX = mybir.AxisListType

P = 128
D = 1024
C = D // P
T = 256
TB = T // P
TC = 256
EPS = 1e-6
NEG = -1e30
LOWEST = -3e38

HG_HEADS, HG_CHUNK = 4, 64
HG_N = T // HG_CHUNK
NSA_HEADS, NSA_KV, NSA_DH = 8, 2, 64
NSA_G = NSA_HEADS // NSA_KV
CMP_LEN, CMP_STRIDE = 32, 16
N_CMP = (T - CMP_LEN) // CMP_STRIDE + 1
SLC_LEN, SLC_TOPK, WIN = 64, 16, 512
assert T // SLC_LEN <= SLC_TOPK and T <= WIN
PK_HEADS, PK_KEYS, PK_TOP = 8, 128, 16
PK_SETS = 2 * PK_HEADS
PK_HK = PK_HEADS * PK_TOP
HEADS, DH = 16, 64
GQA_KV = 4
GRID_W, NA_WIN_W, NA_WIN_H = 64, 16, 8
FFN = 2816
FC = FFN // P
N_MOD = 6
LAYERS = 2
ROPE_THETA = 10000.0
TT = T + TC

ADA_TILES = LAYERS * N_MOD * D // 512
ADA = (3, 5, ADA_TILES)
PIECE = 1024
RAW = 4
SPLIT = 3

NSA_ORDER = [h for c in range(NSA_G) for h in (c, NSA_G + c)]
GQA_ORDER = [h for k in (0, 2) for c in range(4) for h in (4 * k + c, 4 * k + 4 + c)]

VECS = [("mix_norm", C), ("lb0", 4), ("lb1", 4), ("hg_out", 4), ("nsa_q", 1), ("nsa_k", 3), ("nsa_out", 4),
        ("ffn_norm", C), ("ple_norm", C), ("mix2", LAYERS * C), ("ffn2", LAYERS * C), ("final", C),
        ("ada_b", LAYERS * N_MOD * C), ("gqa_q", 1), ("gqa_k", 1), ("cond", 2 * C)]
VEC_AT, NV = {}, 0
for _n, _w in VECS:
    VEC_AT[_n] = NV
    NV += _w

CONSTS = [("ident", P), ("ones", P), ("ones64", P), ("iota", P), ("swap", P)]
MIX_CONSTS = [("hg_mask", P), ("dist", TB * T), ("cdist", TB * N_CMP), ("cmask", TB * N_CMP)]
CONST_AT, NCONST = {}, 0
for _n, _w in CONSTS:
    CONST_AT[_n] = NCONST
    NCONST += _w
MIX_AT, NMIX = {}, 0
for _n, _w in MIX_CONSTS:
    MIX_AT[_n] = NMIX
    NMIX += _w


def const_tables():
    t = {}
    i = np.arange(P)
    t["ident"] = np.eye(P)
    t["ones"] = np.ones((P, P))
    t["ones64"] = (i[:, None] // 64 == i[None, :] // 64) * 1.0
    t["iota"] = np.broadcast_to(i, (P, P))
    s = np.zeros((P, P))
    for m in range(P):
        k = m + 16 if m % 32 < 16 else m - 16
        s[k, m] = -1.0 if m % 32 < 16 else 1.0
    t["swap"] = s
    t["hg_mask"] = ((i[:, None] <= i[None, :]) & (i[:, None] // HG_CHUNK == i[None, :] // HG_CHUNK)) * 1.0
    pos = np.arange(T)
    dist = (pos[:, None] - pos[None, :]).astype(np.float64)
    t["dist"] = np.where(dist >= 0, -dist, NEG).reshape(TB, P, T).transpose(1, 0, 2).reshape(P, -1)
    end = np.arange(N_CMP) * CMP_STRIDE + CMP_LEN - 1
    cd = (pos[:, None] - end[None, :]).astype(np.float64)
    t["cdist"] = np.where(cd >= 0, -cd, NEG).reshape(TB, P, N_CMP).transpose(1, 0, 2).reshape(P, -1)
    t["cmask"] = ((cd >= 0) * 1.0).reshape(TB, P, N_CMP).transpose(1, 0, 2).reshape(P, -1)
    half = DH // 2
    inv = (1.0 / (np.float32(ROPE_THETA) ** (np.arange(0, half, 2, dtype=np.float32) / np.float32(half)))).astype(np.float32)
    row = (pos // GRID_W).astype(np.float32)
    col = (pos % GRID_W).astype(np.float32)
    ang = np.concatenate([np.tile((row[:, None] * inv).T, (2, 1)), np.tile((col[:, None] * inv).T, (2, 1))])
    t["cos"] = np.tile(np.cos(ang), (2, 1))
    t["sin"] = np.tile(np.sin(ang), (2, 1))
    t["rope"] = np.concatenate([t["cos"], t["sin"]], axis=1)

    def table(names):
        return np.ascontiguousarray(np.concatenate([t[n] for n in names], axis=1).astype(np.float32))
    return table([n for n, _ in CONSTS]), table([n for n, _ in MIX_CONSTS]), table(["rope"])


class Signal:

    def __init__(self, handle):
        self.h, self.base = handle, 0

    def at(self, n):
        return self.base + n

    def advance(self, n):
        self.base += n


def build(nc, dr):
    ctx = ExitStack()
    with ctx:
        def sem(name):
            return ctx.enter_context(nc.semaphore(name))

        def signal(name):
            return Signal(sem(name))

        used = []

        def numbered(name):
            used.append(name)
            return f"{name}{used.count(name)}"

        raw = ctx.enter_context(nc.sbuf_tensor("raw", [P, RAW, PIECE], F32))
        whi = ctx.enter_context(nc.sbuf_tensor("whi", [P, SPLIT, PIECE], F32R))
        wlo = ctx.enter_context(nc.sbuf_tensor("wlo", [P, SPLIT, PIECE], F32R))
        vec = ctx.enter_context(nc.sbuf_tensor("vec", [P, NV], F32))
        kon = ctx.enter_context(nc.sbuf_tensor("kon", [P, NCONST], F32))
        eps = ctx.enter_context(nc.sbuf_tensor("eps", [P, 1], F32))
        mod = ctx.enter_context(nc.sbuf_tensor("mod", [P, LAYERS, N_MOD * C, 2], F32))
        gs1 = ctx.enter_context(nc.sbuf_tensor("gs1", [P, LAYERS, C, 2], F32))
        gs2 = ctx.enter_context(nc.sbuf_tensor("gs2", [P, LAYERS, C, 2], F32))
        hT = ctx.enter_context(nc.sbuf_tensor("hT", [P, C, T], F32))
        ps = ctx.enter_context(nc.psum_tensor("ps", [P, 8, 512], F32))

        def v(name, i=0, n=1):
            return vec[:, VEC_AT[name] + i:VEC_AT[name] + i + n]

        def k(name, a=0, b=None):
            w = dict(CONSTS)[name]
            return kon[:, CONST_AT[name] + a:CONST_AT[name] + (w if b is None else b)]

        raw_loaded = [sem(f"raw_loaded{i}") for i in range(RAW)]
        hi_done, lo_done = sem("hi_done"), sem("lo_done")
        piece_used, raw_used = sem("piece_used"), sem("raw_used")
        start_loaded = sem("start_loaded")
        product_done = signal("product_done")
        act_evacuated = signal("act_evacuated")
        dve_evacuated = signal("dve_evacuated")
        squares_done = signal("squares_done")
        sums_done = signal("sums_done")
        root_done = signal("root_done")
        rstd_done = signal("rstd_done")
        scaled_done = signal("scaled_done")
        normed_done = signal("normed_done")
        rounded_done = signal("rounded_done")
        out_stored = sem("out_stored")

        pieces = []
        count = {True: 0, False: 0}

        own_end = {}

        def add_pieces(name, split=True, a=0, b=None, end=None):
            first = len(pieces)
            for x in dr[name] if isinstance(dr[name], list) else [dr[name]]:
                for i in range(a, x.shape[0] if b is None else b):
                    if end:
                        own_end[len(pieces)] = end(i)
                    pieces.append((x[i], x.shape[2], split, count[split]))
                    count[split] += not end
            return first

        top_pe = sem("top_pe_step")
        at_in = add_pieces("w_in_t")
        at_ada = [add_pieces("ada_t", False, 0, 4 * ADA[0])]
        at_cmp = add_pieces("cmp_w1_t", split=False)
        at_ada.append(add_pieces("ada_t", False, 4 * ADA[0], 4 * ADA[1]))
        at_wout = add_pieces("w_out_t")
        at_wq = add_pieces("peer_wq_t")
        at_keys = add_pieces("peer_keys_t", split=False, end=lambda i: (top_pe, 4 * i + 4))
        at_ada.append(add_pieces("ada_t", False, 4 * ADA[1], 4 * ADA[2]))
        at_experts = add_pieces("experts_t")
        at_plep = add_pieces("ple_proj_t")
        at_plew = add_pieces("ple_gate_t")
        at_qkv = [None] * LAYERS
        at_o = [None] * LAYERS
        at_f1 = [None] * LAYERS
        at_f2 = [None] * LAYERS
        for i in range(LAYERS):
            at_qkv[i] = add_pieces(f"qkv{i}_t")
            at_o[i] = add_pieces(f"o{i}_t")
            at_f1[i] = add_pieces(f"ffn_in{i}_t")
            at_f2[i] = add_pieces(f"ffn_out{i}_t")
        n_pieces = len(pieces)
        next_load = [0]

        def loads(sp, upto):
            for g in range(next_load[0], min(upto, n_pieces)):
                if g >= RAW:
                    _, _, split, n = pieces[g - RAW]
                    if g - RAW in own_end:
                        sp.wait_ge(*own_end[g - RAW])
                    else:
                        sp.wait_ge(lo_done if split else raw_used, n + 1)
                src, w, _, _ = pieces[g]
                sp.dma_start(raw[:, g % RAW, 0:w], src).then_inc(raw_loaded[g % RAW], 16)
            next_load[0] = max(next_load[0], min(upto, n_pieces))

        def piece_loaded(eng, g):
            eng.wait_ge(raw_loaded[g % RAW], 16 * (g // RAW + 1))

        def split_hi(act, g):
            _, w, _, n = pieces[g]
            piece_loaded(act, g)
            if n >= SPLIT:
                act.wait_ge(piece_used, n - SPLIT + 1)
            act.activation(whi[:, n % SPLIT, 0:w], raw[:, g % RAW, 0:w], ACT.Copy).then_inc(hi_done, 1)

        def split_lo(dve, g):
            _, w, _, n = pieces[g]
            dve.wait_ge(hi_done, n + 1)
            dve.tensor_tensor(wlo[:, n % SPLIT, 0:w], raw[:, g % RAW, 0:w], whi[:, n % SPLIT, 0:w].bitcast(F32),
                              ALU.subtract).then_inc(lo_done, 1)

        split_upto = [0]

        def ahead(g):
            n = 0
            while n < SPLIT - 1 and g + n < n_pieces and pieces[g + n][2]:
                n += 1
            return list(range(g, g + n))

        def norm_stage(src, dst, n, gain, shift=None, segs=1, parts=None):
            w = n // segs
            with ExitStack() as own, nc.Block() as block:
                root = own.enter_context(nc.sbuf_tensor(numbered("root"), [P, n], F32))
                rstd = own.enter_context(nc.sbuf_tensor(numbered("rstd"), [P, n], F32))
                plain = shift is None

                @block.scalar
                def _(act):
                    for c in range(C):
                        act.activation(dst[:, c, :], src[:, c, :], ACT.Square).then_inc(squares_done.h, 1)
                    act.wait_ge(sums_done.h, sums_done.at(1))
                    act.activation(root[:, :], ps[:, 0, 0:n], ACT.Sqrt, bias=eps[:, :], scale=1.0 / D).then_inc(root_done.h, 1)
                    for c in range(C):
                        act.wait_ge(scaled_done.h, scaled_done.at(c + 1))
                        if not plain:
                            for s in range(segs):
                                o = dst[:, c, s * w:s * w + w]
                                ins = act.activation(o, o, ACT.Identity, bias=shift(c, s), scale=gain(c, s))
                            ins.then_inc(normed_done.h, 1)
                            act.wait_ge(normed_done.h, normed_done.at(c + 1))
                        if parts:
                            act.activation(parts[0][:, c, :], dst[:, c, :], ACT.Copy).then_inc(rounded_done.h, 1)

                @block.tensor
                def _(pe):
                    for c in range(C):
                        pe.wait_ge(squares_done.h, squares_done.at(c + 1))
                        mm = pe.matmul(ps[:, 0, 0:n], k("ones"), dst[:, c, :], start=(c == 0), stop=(c == C - 1))
                    mm.then_inc(sums_done.h, 1)

                @block.vector
                def _(dve):
                    dve.wait_ge(root_done.h, root_done.at(1))
                    dve.reciprocal(rstd[:, :], root[:, :]).then_inc(rstd_done.h, 1)
                    dve.wait_ge(rstd_done.h, rstd_done.at(1))
                    for c in range(C + 2):
                        if c < C and plain:
                            dve.scalar_tensor_tensor(out=dst[:, c, :], in0=src[:, c, :], scalar=gain(c, 0), in1=rstd[:, :],
                                                     op0=ALU.mult, op1=ALU.mult).then_inc(scaled_done.h, 1)
                        elif c < C:
                            dve.tensor_tensor(dst[:, c, :], src[:, c, :], rstd[:, :], ALU.mult).then_inc(scaled_done.h, 1)
                        if parts and c >= 2:
                            dve.wait_ge(rounded_done.h, rounded_done.at(c - 1))
                            dve.tensor_tensor(parts[1][:, c - 2, :], dst[:, c - 2, :], parts[0][:, c - 2, :].bitcast(F32), ALU.subtract)
            squares_done.advance(C)
            sums_done.advance(1)
            root_done.advance(1)
            rstd_done.advance(1)
            scaled_done.advance(C)
            if parts:
                rounded_done.advance(C)
            if not plain:
                normed_done.advance(C)

        def split_stage(src, parts, chunks):
            with nc.Block() as block:
                @block.scalar
                def _(act):
                    for c in range(chunks):
                        act.activation(parts[0][:, c, :], src[:, c, :], ACT.Copy).then_inc(rounded_done.h, 1)

                @block.vector
                def _(dve):
                    for c in range(chunks):
                        dve.wait_ge(rounded_done.h, rounded_done.at(c + 1))
                        dve.tensor_tensor(parts[1][:, c, :], src[:, c, :], parts[0][:, c, :].bitcast(F32), ALU.subtract)
            rounded_done.advance(chunks)

        def products(pe, place, stationary, moving, start, stop):
            (wh, wl), (xh, xl) = stationary, moving
            pe.matmul(place, wh, xh, start=start, stop=False)
            pe.matmul(place, wh, xl, start=False, stop=False)
            return pe.matmul(place, wl, xh, start=False, stop=stop)

        def product_stage(first, x, tiles):
            at, a_n, d_n, spans = first, 0, 0, []
            for n_pc, per, width, jobs in tiles:
                outs = []
                for j in jobs:
                    a_n += j[3] is not None
                    d_n += j[4] is not None
                    outs.append((a_n, d_n))
                spans.append((at, outs))
                at += n_pc
            after = ahead(at)

            def place(t, j):
                kind, a, b, _, _ = tiles[t][3][j]
                n = (b.stop - b.start) if kind == "wide" else a.stop - a.start
                return ps[:, 4 * (t % 2) + j, 0:n]

            with nc.Block() as block:
                @block.sync
                def _(sp):
                    loads(sp, at + RAW)

                @block.tensor
                def _(pe):
                    for t, (n_pc, per, width, jobs) in enumerate(tiles):
                        g0, _ = spans[t]
                        if t >= 2:
                            a_out, d_out = spans[t - 2][1][-1]
                            if a_out:
                                pe.wait_ge(act_evacuated.h, act_evacuated.at(a_out))
                            if d_out:
                                pe.wait_ge(dve_evacuated.h, dve_evacuated.at(d_out))
                        for g in range(g0, g0 + n_pc):
                            _, _, _, n = pieces[g]
                            pe.wait_ge(lo_done, n + 1)
                            wp = [w[:, n % SPLIT, 0:per * width].rearrange("p (c n) -> p c n", n=width) for w in (whi, wlo)]
                            for i in range(per):
                                c = (g - g0) * per + i
                                first_c, last_c = c == 0, c == n_pc * per - 1
                                for j, (kind, a, b, _, _) in enumerate(jobs):
                                    if kind == "wide":
                                        w, y = [v_[:, i, a:a + P] for v_ in wp], [v_[:, c, b] for v_ in x]
                                    else:
                                        w, y = [v_[:, c, b:b + P] for v_ in x], [v_[:, i, a] for v_ in wp]
                                    mm = products(pe, place(t, j), w, y, first_c, last_c)
                            mm.then_inc(piece_used, 1)

                @block.scalar
                def _(act):
                    def take_out(t):
                        g0, _ = spans[t]
                        act.wait_ge(piece_used, pieces[g0 + tiles[t][0] - 1][3] + 1)
                        for j, job in enumerate(tiles[t][3]):
                            if job[3] is not None:
                                job[3](act, place(t, j)).then_inc(act_evacuated.h, 1)
                    for t, (n_pc, _, _, _) in enumerate(tiles):
                        for i in range(n_pc):
                            if spans[t][0] + i >= split_upto[0]:
                                split_hi(act, spans[t][0] + i)
                            if t >= 1 and i == min(1, n_pc - 1):
                                take_out(t - 1)
                    for g in after:
                        split_hi(act, g)
                    take_out(len(tiles) - 1)

                @block.vector
                def _(dve):
                    def take_out(t):
                        g0, outs = spans[t]
                        dve.wait_ge(piece_used, pieces[g0 + tiles[t][0] - 1][3] + 1)
                        for j, job in enumerate(tiles[t][3]):
                            if job[4] is not None:
                                if job[3] is not None:
                                    dve.wait_ge(act_evacuated.h, act_evacuated.at(outs[j][0]))
                                job[4](dve, place(t, j)).then_inc(dve_evacuated.h, 1)
                    for t, (n_pc, _, _, _) in enumerate(tiles):
                        for i in range(n_pc):
                            if spans[t][0] + i >= split_upto[0]:
                                split_lo(dve, spans[t][0] + i)
                            if t >= 1 and i == min(1, n_pc - 1):
                                take_out(t - 1)
                    for g in after:
                        split_lo(dve, g)
                    take_out(len(tiles) - 1)
            split_upto[0] = at + len(after)
            act_evacuated.advance(a_n)
            dve_evacuated.advance(d_n)

        def wide_tiles(n, w, out, x0=0):
            return [(4, 2, 512, [("wide", j * P, slice(x0, x0 + w), *out(4 * t + j)) for j in range(4)]) for t in range(n // 4)]

        def copied(n, dst, scale=None):
            if n % 2 == 0:
                return (lambda act, place: act.activation(dst, place, ACT.Copy, scale=1.0 if scale is None else scale)), None
            if scale is None:
                return None, lambda dve, place: dve.tensor_copy(dst, place)
            return None, lambda dve, place: dve.tensor_scalar(dst, place, scale, None, ALU.mult)

        def head_norm_stage(x, n, gain):
            flat = x.rearrange("p n t -> p (n t)")
            groups = n * T // 512
            with ExitStack() as own, nc.Block() as block:
                sq = own.enter_context(nc.sbuf_tensor(numbered("head_squares"), [P, n * T], F32))
                rstd = own.enter_context(nc.sbuf_tensor(numbered("head_rstd"), [P, n, T], F32))

                @block.scalar
                def _(act):
                    act.activation(sq[:, :], flat, ACT.Square).then_inc(squares_done.h, 1)
                    act.wait_ge(sums_done.h, sums_done.at(1))
                    act.activation(sq[:, :], ps[:, 0:groups, :].rearrange("p g t -> p (g t)"), ACT.Sqrt,
                                   bias=eps[:, :], scale=1.0 / 64).then_inc(root_done.h, 1)

                @block.tensor
                def _(pe):
                    pe.wait_ge(squares_done.h, squares_done.at(1))
                    for g in range(groups):
                        mm = pe.matmul(ps[:, g, :], k("ones64"), sq[:, g * 512:g * 512 + 512], start=True, stop=True)
                    mm.then_inc(sums_done.h, 1)

                @block.vector
                def _(dve):
                    dve.wait_ge(root_done.h, root_done.at(1))
                    dve.reciprocal(rstd[:, :, :].rearrange("p n t -> p (n t)"), sq[:, :]).then_inc(rstd_done.h, 1)
                    dve.wait_ge(rstd_done.h, rstd_done.at(1))
                    for c in range(n):
                        dve.scalar_tensor_tensor(out=x[:, c, :], in0=x[:, c, :], scalar=gain(c), in1=rstd[:, c, :],
                                                 op0=ALU.mult, op1=ALU.mult)
            for s in (squares_done, sums_done, root_done, rstd_done):
                s.advance(1)

        ada_rows_out, ada_turned = sem("ada_rows_out"), sem("ada_turned")
        cond = ctx.enter_context(nc.sbuf_tensor("cond", [P, C, 2], F32))
        lots = ctx.enter_context(ExitStack())
        ada_row = lots.enter_context(nc.sbuf_tensor("ada_row", [2, 2, 512], F32, side="right"))

        def ada_whole(t):
            lot = next(i for i, n in enumerate(ADA) if t < n)
            g = at_ada[lot] + 4 * (t - (ADA[lot - 1] if lot else 0)) + 3
            return g, pieces[g][3] + 1

        def ada_tiles_pe(pe, a, b, bank0):
            def turn(t):
                pe.wait_ge(ada_rows_out, t + 1)
                for j in range(4):
                    n = 4 * (t - a) + j
                    mm = pe.transpose(ps[:, bank0 + 2, 2 * n:2 * n + 2], ada_row[:, t % 2, j * P:j * P + P], k("ident")[0:2, 0:2])
                mm.then_inc(ada_turned, 1)
            for t in range(a, b):
                if t >= a + 2:
                    pe.wait_ge(ada_rows_out, t - 1)
                for g in range(ada_whole(t)[0] - 3, ada_whole(t)[0] + 1):
                    piece_loaded(pe, g)
                    for i in range(2):
                        c = 2 * (g - ada_whole(t)[0] + 3) + i
                        mm = pe.matmul(ps[0:2, bank0 + t % 2, :], cond[:, c, :], raw[:, g % RAW, i * 512:i * 512 + 512], start=(c == 0), stop=(c == C - 1))
                    mm.then_inc(raw_used, 1)
                if t > a:
                    turn(t - 1)
            turn(b - 1)

        def ada_tiles_act(act, a, b, bank0):
            for t in range(a, b):
                act.wait_ge(raw_used, ada_whole(t)[1])
                if t >= 2:
                    act.wait_ge(ada_turned, t - 1)
                act.activation(ada_row[:, t % 2, :], ps[0:2, bank0 + t % 2, :], ACT.Copy).then_inc(ada_rows_out, 1)
            act.wait_ge(ada_turned, b)
            act.activation(mod[:, :, :, :].rearrange("p l j s -> p (l j s)")[:, 8 * a:8 * b], ps[:, bank0 + 2, 0:8 * (b - a)], ACT.Copy)

        mixer = ctx.enter_context(ExitStack())

        def mb(name, shape):
            return mixer.enter_context(nc.sbuf_tensor(name, shape, F32))

        aT = mb("aT", [P, C, T])
        aH = [mixer.enter_context(nc.sbuf_tensor(n, [P, C, T], F32R)) for n in ("aT_hi", "aT_lo")]
        hgT = mb("hgT", [P, 3, 4, T])
        nqk = mb("nqk", [P, 6, T])
        cin = mb("cin", [P, 2, T])
        hg_v = mb("hg_v", [P, TB, 512])
        nv = mb("nv", [P, TB, 280])
        mixT = mb("mixT", [P, C, T])
        mkon = mb("mkon", [P, NMIX])
        cmp_pe = mb("cmp_pe", [P, 2, CMP_LEN])
        cmp_w2 = mb("cmp_w2", [P, 2, P])

        def mk(name):
            return mkon[:, MIX_AT[name]:MIX_AT[name] + dict(MIX_CONSTS)[name]]

        with nc.Block() as block:
            @block.sync
            def _(sp):
                sp.dma_start(hT[:, :, :], dr["x_t"]).then_inc(start_loaded, 16)
                sp.dma_start(kon[:, :], dr["consts"]).then_inc(start_loaded, 16)
                sp.dma_start(vec[:, :], dr["vecs"]).then_inc(start_loaded, 16)
                loads(sp, RAW)
                sp.dma_start(mkon[:, :], dr["mix_consts"]).then_inc(start_loaded, 16)
                sp.dma_start(cmp_pe[:, :, :], dr["cmp_pe_t"]).then_inc(start_loaded, 16)
                sp.dma_start(cmp_w2[:, :, :], dr["cmp_w2_t"]).then_inc(start_loaded, 16)

            @block.scalar
            def _(act):
                act.wait_ge(start_loaded, 96)
                act.activation(cond[:, :, :].rearrange("p c s -> p (c s)"), v("cond", 0, 2 * C), ACT.Silu)

            @block.vector
            def _(dve):
                dve.memset(eps[:, :], EPS)
                dve.wait_ge(start_loaded, 96)
                dve.tensor_scalar(v("nsa_q"), v("nsa_q"), NSA_DH ** -0.5, None, ALU.mult)
                dve.tensor_scalar(v("gqa_q"), v("gqa_q"), DH ** -0.5, None, ALU.mult)

        norm_stage(hT, aT, T, lambda c, s: v("mix_norm", c), parts=aH)

        chunks = ([hgT[:, 0, j, :] for j in range(4)] + [hgT[:, 1, j, :] for j in range(4)] + [nqk[:, j, :] for j in range(4)]
                  + [cin[:, 0, :], cin[:, 1, :], nqk[:, 4, :], nqk[:, 5, :]] + [hgT[:, 2, j, :] for j in range(4)])
        product_stage(at_in, aH, wide_tiles(len(chunks), T, lambda n: copied(n, chunks[n]))
                      + [(4, 2, 512, [("tall", slice(0, 512), b * P, *copied(b, hg_v[:, b, :])) for b in range(TB)]),
                         (4, 2, 280, [("tall", slice(0, 280), b * P, *copied(b, nv[:, b, :])) for b in range(TB)])])

        hg_act, hg_dve, hg_pe = sem("hg_act_step"), sem("hg_dve_step"), sem("hg_pe_step")
        with ExitStack() as own, nc.Block() as block:
            def ob(name, shape):
                return own.enter_context(nc.sbuf_tensor(name, shape, F32))

            H4 = [P, HG_HEADS, T]
            lb, lbd, oml = ob("lb", [P, 4]), ob("lbd", [P, 4]), ob("oml", [P, 4])
            keep, sig, forget, key, logf, G = (ob(n, H4) for n in ("keep", "sig", "forget", "key", "logf", "G"))
            d1, d4, e1, e2, e3, e4 = (ob(n, H4) for n in ("d1", "d4", "e1", "e2", "e3", "e4"))
            qs, gate, qa, ka, qi, ki = (ob(n, H4) for n in ("qs", "gate", "qa", "ka", "qi", "ki"))
            am = ob("am", [P, TB, 512])
            kiT = ob("kiT", [P, TB, 512])
            S = ob("S", [P, 3, 512])
            osq, on, rstd = am, sig, kiT

            def fl(x):
                return x[:, :, :].rearrange("p h t -> p (h t)")

            def ch(x):
                return fl(x).rearrange("p (n s) -> p n s", s=HG_CHUNK)

            def at_end(x, i):
                return ch(x)[:, :, i:i + 1].broadcast_to([P, HG_HEADS * HG_N, HG_CHUNK])

            @block.scalar
            def _(act):
                act.activation(fl(sig), hgT[:, 0, :, :].rearrange("p h t -> p (h t)"), ACT.Sigmoid).then_inc(hg_act, 1)
                act.wait_ge(hg_dve, 1)
                act.activation(lb[:, :], lbd[:, :], ACT.Sigmoid).then_inc(hg_act, 1)
                act.activation(fl(qs), hgT[:, 1, :, :].rearrange("p h t -> p (h t)"), ACT.Silu).then_inc(hg_act, 1)
                act.activation(fl(gate), hgT[:, 2, :, :].rearrange("p h t -> p (h t)"), ACT.Silu).then_inc(hg_act, 1)
                ada_tiles_act(act, 0, ADA[0], 4)
                act.wait_ge(hg_dve, 9)
                act.activation(fl(logf), fl(forget), ACT.Ln).then_inc(hg_act, 1)
                act.wait_ge(hg_dve, 13)
                act.activation(fl(e1), fl(d1), ACT.Exp).then_inc(hg_act, 1)
                act.activation(fl(e2), fl(d1), ACT.Exp, scale=-1.0).then_inc(hg_act, 1)
                act.activation(fl(e3), fl(G), ACT.Exp).then_inc(hg_act, 1)
                act.activation(fl(e4), fl(d4), ACT.Exp).then_inc(hg_act, 1)
                for b in range(TB):
                    act.wait_ge(hg_pe, 3 + b)
                    act.activation(kiT[:, b, :], ps[:, 2 + b, :], ACT.Copy).then_inc(hg_act, 1)
                for b in range(TB):
                    act.wait_ge(hg_pe, 8 + b)
                    act.activation(osq[:, b, :], ps[:, b, :], ACT.Square).then_inc(hg_act, 1)
                act.wait_ge(hg_pe, 10)
                act.activation(osq[:, :, :].rearrange("p b n -> p (b n)"), ps[:, 2:4, :].rearrange("p b n -> p (b n)"),
                               ACT.Sqrt, bias=eps[:, :], scale=1.0 / P).then_inc(hg_act, 1)

            @block.vector
            def _(dve):
                dve.tensor_tensor(lbd[:, :], v("lb0", 0, 4), v("lb1", 0, 4), ALU.subtract).then_inc(hg_dve, 1)
                dve.memset(keep[:, :, :], 1.0).then_inc(hg_dve, 1)
                dve.wait_ge(hg_dve, 2)
                dve.memset(ch(keep)[:, :, 0:1], 0.0).then_inc(hg_dve, 1)
                dve.memset(am[:, :, :], 0.0).then_inc(hg_dve, 1)
                dve.wait_ge(hg_act, 2)
                dve.tensor_scalar(oml[:, :], lb[:, :], -1.0, 1.0, ALU.mult, ALU.add).then_inc(hg_dve, 1)
                dve.wait_ge(hg_dve, 5)
                for h in range(4):
                    dve.tensor_scalar(forget[:, h, :], sig[:, h, :], oml[:, h:h + 1], lb[:, h:h + 1], ALU.mult, ALU.add).then_inc(hg_dve, 1)
                dve.wait_ge(hg_dve, 9)
                dve.tensor_scalar(fl(key), fl(forget), -1.0, 1.0, ALU.mult, ALU.add).then_inc(hg_dve, 1)
                dve.wait_ge(hg_act, 5)
                dve.tensor_tensor_scan(fl(G), fl(keep), fl(logf), 0.0, ALU.mult, ALU.add).then_inc(hg_dve, 1)
                dve.wait_ge(hg_dve, 11)
                dve.tensor_tensor(ch(d1), ch(G), at_end(G, HG_CHUNK // 2 - 1), ALU.subtract).then_inc(hg_dve, 1)
                dve.tensor_tensor(ch(d4), at_end(G, HG_CHUNK - 1), ch(G), ALU.subtract).then_inc(hg_dve, 1)
                dve.wait_ge(hg_act, 6)
                dve.scalar_tensor_tensor(out=fl(qa), in0=fl(qs), scalar=P ** -0.5, in1=fl(e1), op0=ALU.mult, op1=ALU.mult).then_inc(hg_dve, 1)
                dve.wait_ge(hg_act, 7)
                dve.tensor_tensor(fl(ka), fl(key), fl(e2), ALU.mult).then_inc(hg_dve, 1)
                dve.wait_ge(hg_act, 8)
                dve.scalar_tensor_tensor(out=fl(qi), in0=fl(qs), scalar=P ** -0.5, in1=fl(e3), op0=ALU.mult, op1=ALU.mult).then_inc(hg_dve, 1)
                dve.wait_ge(hg_act, 9)
                dve.tensor_tensor(fl(ki), fl(key), fl(e4), ALU.mult).then_inc(hg_dve, 1)
                mask = mk("hg_mask").bitcast(I32).unsqueeze(1).broadcast_to([P, HG_HEADS, P])
                for b in range(TB):
                    dve.wait_ge(hg_pe, 1 + b)
                    dve.copy_predicated(am[:, b, :].rearrange("p (h t) -> p h t", t=P), mask,
                                        ps[:, b, :].rearrange("p (h t) -> p h t", t=P)).then_inc(hg_dve, 1)
                dve.wait_ge(hg_pe, 5)
                dve.tensor_copy(S[:, 0, :], ps[:, 4, :]).then_inc(hg_dve, 1)
                for n in range(1, 3):
                    dve.wait_ge(hg_dve, 16 + 4 * n)
                    dve.wait_ge(hg_pe, 5 + n)
                    for h in range(4):
                        end = n * HG_CHUNK + HG_CHUNK - 1
                        o = slice(h * P, h * P + P)
                        dve.scalar_tensor_tensor(out=S[:, n, o], in0=S[:, n - 1, o], scalar=e3[:, h, end:end + 1], in1=ps[:, 4 + n, o],
                                                 op0=ALU.mult, op1=ALU.add).then_inc(hg_dve, 1)
                dve.wait_ge(hg_act, 14)
                dve.reciprocal(rstd[:, :, :].rearrange("p b n -> p (b n)"), osq[:, :, :].rearrange("p b n -> p (b n)")).then_inc(hg_dve, 1)
                dve.wait_ge(hg_dve, 29)
                for b in range(TB):
                    for h in range(4):
                        o = slice(h * P, h * P + P)
                        dve.scalar_tensor_tensor(out=on[:, h, b * P:b * P + P], in0=ps[:, b, o], scalar=v("hg_out", h), in1=rstd[:, b, o],
                                                 op0=ALU.mult, op1=ALU.mult).then_inc(hg_dve, 1)
                dve.wait_ge(hg_dve, 37)
                dve.tensor_tensor(mixT[:, 0:4, :].rearrange("p h t -> p (h t)"), fl(on), fl(gate), ALU.mult)

            @block.sync
            def _(sp):
                loads(sp, at_cmp + RAW)

            @block.tensor
            def _(pe):
                ada_tiles_pe(pe, 0, ADA[0], 4)
                pe.wait_ge(hg_dve, 15)
                for b in range(TB):
                    for h in range(4):
                        o, t = slice(h * P, h * P + P), slice(b * P, b * P + P)
                        mm = pe.matmul(ps[:, b, o], ka[:, h, t], qa[:, h, t], start=True, stop=True)
                    mm.then_inc(hg_pe, 1)
                pe.wait_ge(hg_dve, 17)
                for b in range(TB):
                    for h in range(4):
                        o, t = slice(h * P, h * P + P), slice(b * P, b * P + P)
                        mm = pe.transpose(ps[:, 2 + b, o], ki[:, h, t], k("ident"))
                    mm.then_inc(hg_pe, 1)
                pe.wait_ge(hg_act, 5)
                for n in range(3):
                    b, r = n // 2, slice((n % 2) * HG_CHUNK, (n % 2) * HG_CHUNK + HG_CHUNK)
                    pe.wait_ge(hg_act, 10 + b)
                    for h in range(4):
                        o = slice(h * P, h * P + P)
                        mm = pe.matmul(ps[:, 4 + n, o], kiT[r, b, o], hg_v[r, b, o], start=True, stop=True)
                    mm.then_inc(hg_pe, 1)
                for b in range(TB):
                    pe.wait_ge(hg_dve, 19)
                    for h in range(4):
                        o = slice(h * P, h * P + P)
                        pe.matmul(ps[:, b, o], hg_v[:, b, o], am[:, b, o], start=(h == 0), stop=False, skip_group_check=True)
                    for n in range(max(1, 2 * b), 2 * b + 2):
                        pe.wait_ge(hg_dve, 16 + 4 * n)
                        for h in range(4):
                            at = h * P + (n % 2) * HG_CHUNK
                            mm = pe.matmul(ps[:, b, at:at + HG_CHUNK], S[:, n - 1, h * P:h * P + P], qi[:, h, n * HG_CHUNK:n * HG_CHUNK + HG_CHUNK],
                                           start=False, stop=True, skip_group_check=True)
                    mm.then_inc(hg_pe, 1)
                pe.wait_ge(hg_act, 13)
                for b in range(TB):
                    mm = pe.matmul(ps[:, 2 + b, :], k("ones"), osq[:, b, :], start=True, stop=True)
                mm.then_inc(hg_pe, 1)

        head_norm_stage(nqk, 6, lambda c: v("nsa_q") if c < 4 else v("nsa_k", c - 3))

        kcn = mb("kcn", [P, N_CMP])
        vcs = mb("vcs", [N_CMP, P])
        gates = mb("gates", [P, TB, 3 * NSA_HEADS])
        cmp_act, cmp_dve, cmp_pe_step = sem("cmp_act_step"), sem("cmp_dve_step"), sem("cmp_pe_step")
        with ExitStack() as own, nc.Block() as block:
            win = own.enter_context(nc.sbuf_tensor("win", [P, 2, CMP_LEN, N_CMP], F32))
            rows = own.enter_context(nc.sbuf_tensor("cmp_rows", [N_CMP, 2, P], F32))
            hid = own.enter_context(nc.sbuf_tensor("cmp_hid", [P, 2, N_CMP], F32))
            csq = own.enter_context(nc.sbuf_tensor("cmp_sq", [P, N_CMP], F32))
            crs = own.enter_context(nc.sbuf_tensor("cmp_rstd", [P, N_CMP], F32))
            c3 = cin[:, :, :].rearrange("p i (n l) -> p i l n", l=CMP_STRIDE)

            @block.sync
            def _(sp):
                loads(sp, at_wout + RAW)

            @block.vector
            def _(dve):
                for i in range(2):
                    for j in range(2):
                        l = slice(j * CMP_STRIDE, j * CMP_STRIDE + CMP_STRIDE)
                        dve.tensor_tensor(win[:, i, l, :], c3[:, i, :, j:j + N_CMP],
                                          cmp_pe[:, i, l].unsqueeze(2).broadcast_to([P, CMP_STRIDE, N_CMP]), ALU.add).then_inc(cmp_dve, 1)
                dve.wait_ge(cmp_act, 7)
                dve.reciprocal(crs[:, :], csq[:, :]).then_inc(cmp_dve, 1)
                dve.wait_ge(cmp_dve, 5)
                dve.scalar_tensor_tensor(out=kcn[:, :], in0=ps[:, 2, 0:N_CMP], scalar=v("nsa_k", 0), in1=crs[:, :], op0=ALU.mult, op1=ALU.mult)
                dve.tensor_copy(vcs[:, :], ps[0:N_CMP, 3, 0:P])

            @block.tensor
            def _(pe):
                for i in range(2):
                    pe.wait_ge(cmp_dve, 2 * i + 2)
                    per = PIECE // P
                    for l in range(CMP_LEN):
                        g = at_cmp + (i * CMP_LEN + l) // per
                        if l % per == 0:
                            piece_loaded(pe, g)
                        o = l % per * P
                        mm = pe.matmul(ps[0:N_CMP, i, 0:P], win[:, i, l, :], raw[:, g % RAW, o:o + P], start=(l == 0), stop=(l == CMP_LEN - 1))
                        if l % per == per - 1:
                            mm.then_inc(raw_used, 1)
                for i in range(2):
                    pe.wait_ge(cmp_act, 1 + i)
                    pe.transpose(ps[:, 5 + i, 0:N_CMP], rows[:, i, :], k("ident")[0:N_CMP, 0:N_CMP]).then_inc(cmp_pe_step, 1)
                pe.wait_ge(cmp_act, 4)
                pe.matmul(ps[:, 2, 0:N_CMP], cmp_w2[:, 0, :], hid[:, 0, :], start=True, stop=True).then_inc(cmp_pe_step, 1)
                pe.matmul(ps[0:N_CMP, 3, 0:P], hid[:, 1, :], cmp_w2[:, 1, :], start=True, stop=True).then_inc(cmp_pe_step, 1)
                ada_tiles_pe(pe, ADA[0], ADA[1], 5)
                pe.wait_ge(cmp_act, 6)
                pe.matmul(ps[:, 4, 0:N_CMP], k("ones64"), csq[:, :], start=True, stop=True).then_inc(cmp_pe_step, 1)

            @block.scalar
            def _(act):
                for i in range(2):
                    act.wait_ge(raw_used, pieces[at_cmp][3] + (i + 1) * CMP_LEN * P // PIECE)
                    act.activation(rows[:, i, :], ps[0:N_CMP, i, 0:P], ACT.Gelu_apprx_tanh).then_inc(cmp_act, 1)
                for i in range(2):
                    act.wait_ge(cmp_pe_step, 1 + i)
                    act.activation(hid[:, i, :], ps[:, 5 + i, 0:N_CMP], ACT.Copy).then_inc(cmp_act, 1)
                act.activation(gates[:, :, :], nv[:, :, 256:280], ACT.Sigmoid).then_inc(cmp_act, 1)
                act.wait_ge(cmp_pe_step, 4)
                act.activation(csq[:, :], ps[:, 2, 0:N_CMP], ACT.Square).then_inc(cmp_act, 1)
                ada_tiles_act(act, ADA[0], ADA[1], 5)
                act.wait_ge(cmp_pe_step, 5)
                act.activation(csq[:, :], ps[:, 4, 0:N_CMP], ACT.Sqrt, bias=eps[:, :], scale=1.0 / 64).then_inc(cmp_act, 1)

        scores_done, biased, max_done = signal("scores_done"), signal("biased"), signal("max_done")
        exp_done, probs_done, turned = signal("exp_done"), signal("probs_done"), signal("turned")
        turned_out, attended, attended_out = signal("turned_out"), signal("attended"), signal("attended_out")
        probs_link, output_hi = signal("probs_link"), signal("output_hi")
        with ExitStack() as own, nc.Block() as block:
            def ob(name, shape):
                return own.enter_context(nc.sbuf_tensor(name, shape, F32))

            W3 = 512 + N_CMP
            sc = ob("nsa_sc", [P, 2, W3])
            pr = ob("nsa_pr", [P, 3, W3])
            nm = ob("nsa_nm", [P, 3, 3])
            sums, coef = ob("nsa_sums", [P, 3, 3]), ob("nsa_coef", [P, 3, 3])
            pT = ob("nsa_pT", [P, 2, 512])
            cT = ob("nsa_cT", [N_CMP, 2, P])
            units = [(c, half, qb) for c in range(NSA_G) for half in range(2) for qb in range(TB)]
            N = len(units)
            dist = mk("dist").rearrange("p (b t) -> p b t", b=TB)
            cdist = mk("cdist").rearrange("p (b t) -> p b t", b=TB)
            cmask = mk("cmask").rearrange("p (b t) -> p b t", b=TB)

            def head_of(u):
                return units[u][0] + NSA_G * units[u][1]

            @block.tensor
            def _(pe):
                for i in range(N + 3):
                    if i < N:
                        c, half, qb = units[i]
                        r = slice(64 * half, 64 * half + 64)
                        q = nqk[r, c, qb * P:qb * P + P]
                        if i >= 2:
                            pe.wait_ge(max_done.h, max_done.at(i - 1))
                        pe.matmul(ps[:, i % 2, 0:256], q, nqk[r, 4, :], start=True, stop=True)
                        pe.matmul(ps[:, i % 2, 256:512], q, nqk[r, 5, :], start=True, stop=True)
                        if i >= 1:
                            pe.wait_ge(biased.h, biased.at(2 * i))
                        pe.matmul(ps[:, 2, 0:N_CMP], q, kcn[r, :], start=True, stop=True).then_inc(scores_done.h, 1)
                    if 0 <= i - 2 < N:
                        u = i - 2
                        pe.wait_ge(probs_done.h, probs_done.at(u + 1))
                        if u >= 2:
                            pe.wait_ge(turned_out.h, turned_out.at(u - 1))
                        for j in range(4):
                            pe.transpose(ps[:, 3 + u % 2, j * P:j * P + P], pr[:, u % 3, j * P:j * P + P], k("ident"))
                        if u >= 1:
                            pe.wait_ge(turned_out.h, turned_out.at(u))
                        pe.transpose(ps[0:N_CMP, 5, 0:P], pr[:, u % 3, 512:W3], k("ident")).then_inc(turned.h, 1)
                    if 0 <= i - 3 < N:
                        u = i - 3
                        _, half, _ = units[u]
                        vcol = slice(64 * half, 64 * half + 64)
                        wcol = slice(P + 64 * half, P + 64 * half + 64)
                        pe.wait_ge(turned_out.h, turned_out.at(u + 1))
                        if u >= 2:
                            pe.wait_ge(attended_out.h, attended_out.at(u - 1))
                        o = ps[64 * half:64 * half + 64, 6 + u % 2, 0:P]
                        pe.matmul(o, nv[:, 0, vcol], pT[:, u % 2, 0:P], start=True, stop=False)
                        pe.matmul(o, nv[:, 1, vcol], pT[:, u % 2, P:2 * P], start=False, stop=False)
                        pe.matmul(o, nv[:, 0, wcol], pT[:, u % 2, 2 * P:3 * P], start=False, stop=False)
                        pe.matmul(o, nv[:, 1, wcol], pT[:, u % 2, 3 * P:4 * P], start=False, stop=False)
                        pe.matmul(o, vcs[:, vcol], cT[:, u % 2, :], start=False, stop=True).then_inc(attended.h, 1)

            @block.vector
            def _(dve):
                for i in range(N + 4):
                    if i < N:
                        _, _, qb = units[i]
                        slope = float(2.0 ** (-8.0 * (head_of(i) + 1) / NSA_HEADS))
                        dve.wait_ge(scores_done.h, scores_done.at(i + 1))
                        if i >= 2:
                            dve.wait_ge(exp_done.h, exp_done.at(3 * (i - 1)))
                        dve.scalar_tensor_tensor(out=sc[:, i % 2, 0:512].rearrange("p (a t) -> p a t", a=2),
                                                 in0=dist[:, qb:qb + 1, :].broadcast_to([P, 2, T]), scalar=slope,
                                                 in1=ps[:, i % 2, :].rearrange("p (a t) -> p a t", a=2),
                                                 op0=ALU.mult, op1=ALU.add).then_inc(biased.h, 1)
                        dve.scalar_tensor_tensor(out=sc[:, i % 2, 512:W3], in0=cdist[:, qb, :], scalar=slope,
                                                 in1=ps[:, 2, 0:N_CMP], op0=ALU.mult, op1=ALU.add).then_inc(biased.h, 1)
                        dve.wait_ge(biased.h, biased.at(2 * i + 2))
                        dve.tensor_reduce(nm[:, i % 3, 0:2], sc[:, i % 2, 0:512].rearrange("p (a t) -> p a t", a=2), AX.X, ALU.max, negate=True)
                        dve.tensor_reduce(nm[:, i % 3, 2:3], sc[:, i % 2, 512:W3], AX.X, ALU.max, negate=True).then_inc(max_done.h, 1)
                    if 0 <= i - 1 < N:
                        u = i - 1
                        _, _, qb = units[u]
                        s3, h3 = u % 3, 3 * head_of(u)
                        dve.wait_ge(exp_done.h, exp_done.at(3 * u + 3))
                        dve.scalar_tensor_tensor(out=pr[:, s3, 512:W3], in0=pr[:, s3, 512:W3], scalar=1.0, in1=cmask[:, qb, :],
                                                 op0=ALU.mult, op1=ALU.mult, accum_out=sums[:, s3, 2:3]).then_inc(probs_link.h, 1)
                        dve.wait_ge(probs_link.h, probs_link.at(4 * u + 1))
                        dve.tensor_scalar(sums[:, s3, :], sums[:, s3, :], 1e-30, None, ALU.max).then_inc(probs_link.h, 1)
                        dve.wait_ge(probs_link.h, probs_link.at(4 * u + 2))
                        dve.reciprocal(coef[:, s3, :], sums[:, s3, :]).then_inc(probs_link.h, 1)
                        dve.wait_ge(probs_link.h, probs_link.at(4 * u + 3))
                        dve.tensor_tensor(coef[:, s3, 0:2], coef[:, s3, 0:2], gates[:, qb, h3 + 1:h3 + 3], ALU.mult)
                        dve.tensor_tensor(coef[:, s3, 2:3], coef[:, s3, 2:3], gates[:, qb, h3:h3 + 1], ALU.mult).then_inc(probs_link.h, 1)
                        dve.wait_ge(probs_link.h, probs_link.at(4 * u + 4))
                        dve.tensor_scalar(pr[:, s3, 0:256], pr[:, s3, 0:256], coef[:, s3, 0:1], None, ALU.mult)
                        dve.tensor_scalar(pr[:, s3, 256:512], pr[:, s3, 256:512], coef[:, s3, 1:2], None, ALU.mult)
                        dve.tensor_scalar(pr[:, s3, 512:W3], pr[:, s3, 512:W3], coef[:, s3, 2:3], None, ALU.mult).then_inc(probs_done.h, 1)
                    if 0 <= i - 4 < N:
                        u = i - 4
                        c, half, qb = units[u]
                        dve.wait_ge(attended.h, attended.at(u + 1))
                        r = slice(64 * half, 64 * half + 64)
                        dve.tensor_copy(mixT[r, 4 + c, qb * P:qb * P + P], ps[r, 6 + u % 2, 0:P]).then_inc(attended_out.h, 1)

            @block.scalar
            def _(act):
                for i in range(N + 2):
                    if i < N:
                        act.wait_ge(max_done.h, max_done.at(i + 1))
                        if i >= 3:
                            act.wait_ge(turned.h, turned.at(i - 2))
                        for j, (a, b) in enumerate(((0, 256), (256, 512), (512, W3))):
                            acc = {"accum_out": sums[:, i % 3, j:j + 1]} if j < 2 else {}
                            act.activation(pr[:, i % 3, a:b], sc[:, i % 2, a:b], ACT.Exp, bias=nm[:, i % 3, j:j + 1], **acc).then_inc(exp_done.h, 1)
                    if 0 <= i - 2 < N:
                        u = i - 2
                        act.wait_ge(turned.h, turned.at(u + 1))
                        if u >= 2:
                            act.wait_ge(attended.h, attended.at(u - 1))
                        act.activation(pT[:, u % 2, :], ps[:, 3 + u % 2, :], ACT.Copy)
                        act.activation(cT[:, u % 2, :], ps[0:N_CMP, 5, 0:P], ACT.Copy).then_inc(turned_out.h, 1)
        for s, n in ((scores_done, 1), (biased, 2), (max_done, 1), (exp_done, 3), (probs_link, 4), (probs_done, 1),
                     (turned, 1), (turned_out, 1), (attended, 1), (attended_out, 1)):
            s.advance(n * N)

        head_norm_stage(mixT[:, 4:8, :], 4, lambda c: v("nsa_out", c))

        def add_to_tokens(n):
            return None, lambda dve, place: dve.tensor_tensor(hT[:, n, :], hT[:, n, :], place, ALU.add)

        split_stage(mixT, aH, C)
        product_stage(at_wout, aH, wide_tiles(C, T, add_to_tokens))
        mixer.close()

        peer = ctx.enter_context(ExitStack())

        def pb(name, shape, dt=F32):
            return peer.enter_context(nc.sbuf_tensor(name, shape, dt))

        xH = [pb(n, [P, C, T], F32R) for n in ("xT_hi", "xT_lo")]
        i1T, i2T, wT = pb("i1T", [P, T]), pb("i2T", [P, T]), pb("wT", [P, T])
        with nc.sbuf_tensor("xT", [P, C, T], F32) as xT:
            norm_stage(hT, xT, T, lambda c, s: v("ffn_norm", c), parts=xH)

        top_act, top_dve, sel_step = sem("top_act_step"), sem("top_dve_step"), sem("sel_step")
        with ExitStack() as own:
            def ob(name, shape, dt=F32):
                return own.enter_context(nc.sbuf_tensor(name, shape, dt))

            qT = ob("qT", [P, PK_SETS, T])
            product_stage(at_wq, xH, wide_tiles(PK_SETS, T, lambda j: copied(j, qT[:, j, :])))
            ks = ob("key_scores", [P, TB, PK_SETS, PK_KEYS])
            top_s = ob("top_s", [P, TB, PK_HEADS, 2, PK_TOP])
            top_i = ob("top_i", [P, TB, PK_HEADS, 2, PK_TOP], U32)
            top_f = ob("top_f", [P, PK_HEADS, 2, PK_TOP])
            cand = ob("cand", [P, PK_HEADS, PK_TOP, PK_TOP])
            best_s = ob("best_s", [P, PK_HEADS, PK_TOP])
            best_c = ob("best_c", [P, PK_HEADS, PK_TOP], U32)
            half_u = ob("half_u", [P, 2, PK_HK], U32)
            half_f = ob("half_f", [P, 2, PK_HK])
            pick = ob("pick", [P, PK_HK, PK_TOP])
            expert = ob("expert", [P, TB, 3, PK_HK])
            shifted = ob("shifted", [P, PK_HEADS, PK_TOP])
            total = ob("total", [P, PK_HEADS])
            with nc.Block() as block:
                @block.sync
                def _(sp):
                    loads(sp, at_experts + RAW)

                @block.tensor
                def _(pe):
                    per = PIECE // PK_KEYS
                    for g in range(4):
                        w = at_keys + 4 * g // per
                        piece_loaded(pe, w)
                        for b in range(TB):
                            for j in range(4 * g, 4 * g + 4):
                                mm = pe.matmul(ps[:, 4 * b + g, j % 4 * P:j % 4 * P + P], qT[:, j, b * P:b * P + P],
                                               raw[:, w % RAW, j % per * PK_KEYS:j % per * PK_KEYS + PK_KEYS], start=True, stop=True)
                            mm.then_inc(top_pe, 1)
                    pe.wait_ge(top_act, 8)
                    ada_tiles_pe(pe, ADA[1], ADA[2], 4)
                    for b in range(TB):
                        pe.wait_ge(sel_step, 13 * b + 13)
                        for i in range(3):
                            mm = pe.transpose(ps[:, i, b * P:b * P + P], expert[:, b, i, :], k("ident"))
                    mm.then_inc(top_pe, 1)

                @block.scalar
                def _(act):
                    for n in range(8):
                        g, b = n // 2, n % 2
                        act.wait_ge(top_pe, n + 1)
                        act.activation(ks[:, b, 4 * g:4 * g + 4, :].rearrange("p j n -> p (j n)"), ps[:, 4 * b + g, :], ACT.Copy).then_inc(top_act, 1)
                    ada_tiles_act(act, ADA[1], ADA[2], 4)
                    for b in range(TB):
                        act.wait_ge(sel_step, 13 * b + 1)
                        act.activation(shifted[:, :, :], shifted[:, :, :], ACT.Exp).then_inc(top_act, 1)
                    act.wait_ge(top_pe, 9)
                    for i, dst in enumerate((i1T, i2T, wT)):
                        act.activation(dst[:, :], ps[:, i, 0:T], ACT.Copy)

                @block.vector
                def _(dve):
                    done = 0
                    for b in range(TB):
                        def best(n, values, s8, i8, load):
                            nonlocal done
                            for turn in range(2):
                                for j in range(n):
                                    if turn == 0:
                                        load(j)
                                    else:
                                        dve.wait_ge(top_dve, done - n + j + 1)
                                    dve.max(s8(j, turn), values(j)).then_inc(top_dve, 1)
                                done += n
                                for j in range(n):
                                    dve.wait_ge(top_dve, done - n + j + 1)
                                    dve.max_index(i8(j, turn), s8(j, turn), values(j)).then_inc(top_dve, 1)
                                done += n
                                if turn == 0:
                                    for j in range(n):
                                        dve.wait_ge(top_dve, done - n + j + 1)
                                        dve.match_replace(values(j), s8(j, 0), values(j), LOWEST).then_inc(top_dve, 1)
                                    done += n

                        def scored(j):
                            dve.wait_ge(top_act, 2 * (j // 4) + b + 1)

                        best(PK_SETS, lambda j: ks[:, b, j, :], lambda j, t: top_s[:, b, j // 2, j % 2, 8 * t:8 * t + 8],
                             lambda j, t: top_i[:, b, j // 2, j % 2, 8 * t:8 * t + 8], scored)
                        dve.wait_ge(top_dve, done)
                        dve.tensor_tensor(cand[:, :, :, :], top_s[:, b, :, 0, :].unsqueeze(3).broadcast_to([P, PK_HEADS, PK_TOP, PK_TOP]),
                                          top_s[:, b, :, 1, :].unsqueeze(2).broadcast_to([P, PK_HEADS, PK_TOP, PK_TOP]), ALU.add).then_inc(top_dve, 1)
                        done += 1
                        dve.wait_ge(top_dve, done)
                        best(PK_HEADS, lambda h: cand[:, h, :, :].rearrange("p a b -> p (a b)"), lambda h, t: best_s[:, h, 8 * t:8 * t + 8],
                             lambda h, t: best_c[:, h, 8 * t:8 * t + 8], lambda h: None)
                        dve.wait_ge(top_dve, done)
                        s0 = 13 * b
                        dve.tensor_tensor(shifted[:, :, :], best_s[:, :, :], best_s[:, :, 0:1].broadcast_to([P, PK_HEADS, PK_TOP]), ALU.subtract).then_inc(sel_step, 1)
                        flat_c = best_c[:, :, :].rearrange("p h k -> p (h k)")
                        dve.tensor_scalar(half_u[:, 0, :], flat_c, 4, None, ALU.logical_shift_right).then_inc(sel_step, 1)
                        dve.tensor_scalar(half_u[:, 1, :], flat_c, PK_TOP - 1, None, ALU.bitwise_and).then_inc(sel_step, 1)
                        dve.tensor_copy(top_f[:, :, :, :].rearrange("p h c k -> p (h c k)"), top_i[:, b, :, :, :].rearrange("p h c k -> p (h c k)")).then_inc(sel_step, 1)
                        dve.wait_ge(sel_step, s0 + 3)
                        dve.tensor_copy(half_f[:, :, :], half_u[:, :, :]).then_inc(sel_step, 1)
                        for i in range(2):
                            dve.wait_ge(sel_step, s0 + 5 + 3 * i)
                            dve.tensor_tensor(pick[:, :, :], half_f[:, i, :].unsqueeze(2).broadcast_to([P, PK_HK, PK_TOP]),
                                              k("iota", 0, PK_TOP).unsqueeze(1).broadcast_to([P, PK_HK, PK_TOP]), ALU.is_equal).then_inc(sel_step, 1)
                            dve.wait_ge(sel_step, s0 + 6 + 3 * i)
                            p4 = pick[:, :, :].rearrange("p (h k) j -> p h k j", h=PK_HEADS)
                            dve.tensor_tensor(p4, p4, top_f[:, :, i, :].unsqueeze(2).broadcast_to([P, PK_HEADS, PK_TOP, PK_TOP]), ALU.mult).then_inc(sel_step, 1)
                            dve.wait_ge(sel_step, s0 + 7 + 3 * i)
                            dve.tensor_reduce(expert[:, b, i, :], pick[:, :, :], AX.X, ALU.add).then_inc(sel_step, 1)
                        dve.wait_ge(top_act, 9 + b)
                        dve.tensor_reduce(total[:, :], shifted[:, :, :], AX.X, ALU.add).then_inc(sel_step, 1)
                        dve.wait_ge(sel_step, s0 + 12)
                        dve.reciprocal(total[:, :], total[:, :]).then_inc(top_dve, 1)
                        done += 1
                        dve.wait_ge(top_dve, done)
                        dve.tensor_tensor(expert[:, b, 2, :].rearrange("p (h k) -> p h k", h=PK_HEADS), shifted[:, :, :],
                                          total[:, :].unsqueeze(2).broadcast_to([P, PK_HEADS, PK_TOP]), ALU.mult).then_inc(sel_step, 1)
                        if b == 0:
                            dve.wait_ge(sel_step, 13)

        lots.close()
        route = pb("route", [P, T, PK_KEYS])
        BATCH = 4
        hot, route_mm, route_out = sem("hot"), sem("route_mm"), sem("route_out")
        with ExitStack() as own, nc.Block() as block:
            oh1 = own.enter_context(nc.sbuf_tensor("oh1", [P, 2, BATCH, PK_KEYS], F32))
            oh2 = own.enter_context(nc.sbuf_tensor("oh2", [P, 2, BATCH, PK_KEYS], F32))
            PAIRS = T // (2 * BATCH)

            @block.vector
            def _(dve):
                def pair(r, first):
                    for s in range(2):
                        if not first:
                            dve.wait_ge(route_mm, 2 * r + s - 1)
                        dve.tensor_tensor(oh1[:, s, :, :], k("iota").unsqueeze(1).broadcast_to([P, BATCH, PK_KEYS]),
                                          i1T[:, bass.ds((2 * r + s) * BATCH, BATCH)].unsqueeze(2).broadcast_to([P, BATCH, PK_KEYS]), ALU.is_equal)
                        for q in range(BATCH):
                            t = bass.ds((2 * r + s) * BATCH + q, 1)
                            ins = dve.tensor_scalar(oh2[:, s, q, :], k("iota"), i2T[:, t], wT[:, t], ALU.is_equal, ALU.mult)
                        ins.then_inc(hot, 1)
                pair(0, True)
                with dve.Fori(1, PAIRS) as r:
                    pair(r, False)

            @block.tensor
            def _(pe):
                def pair(r, first):
                    for s in range(2):
                        pe.wait_ge(hot, 2 * r + s + 1)
                        if not first:
                            pe.wait_ge(route_out, 2 * r + s - 1)
                        for q in range(BATCH):
                            mm = pe.matmul(ps[:, s, q * P:q * P + P], oh1[:, s, q, :], oh2[:, s, q, :], start=True, stop=True)
                        mm.then_inc(route_mm, 1)
                pair(0, True)
                with pe.Fori(1, PAIRS) as r:
                    pair(r, False)

            @block.scalar
            def _(act):
                with act.Fori(0, PAIRS) as r:
                    for s in range(2):
                        act.wait_ge(route_mm, 2 * r + s + 1)
                        act.activation(route[:, bass.ds((2 * r + s) * BATCH, BATCH), :].rearrange("p t n -> p (t n)"), ps[:, s, :], ACT.Copy).then_inc(route_out, 1)

        GROUPS = PK_KEYS
        LOOP = 6
        assert 2 * LOOP % RAW == 0 and 2 * LOOP % SPLIT == 0 and LOOP % 3 == 0
        TURNS = (GROUPS - 2) // LOOP
        LAST = 2 * GROUPS - 1
        n0 = pieces[at_experts][3]
        gelu_done, weighted, weighted_hi, weighted_lo = sem("gelu_done"), sem("weighted"), sem("weighted_hi"), sem("weighted_lo")
        with ExitStack() as own, nc.Block() as block:
            ga = own.enter_context(nc.sbuf_tensor("ga", [P, 2, T], F32))
            gh = own.enter_context(nc.sbuf_tensor("gh", [P, 2, T], F32R))
            gl = own.enter_context(nc.sbuf_tensor("gl", [P, 2, T], F32R))

            @block.sync
            def _(sp):
                first = at_experts + 2 * LOOP + RAW
                loads(sp, first)
                turns = (LAST + 1 - 2 * LOOP - RAW) // (2 * LOOP)
                with sp.Fori(0, turns) as r:
                    for e in range(2 * LOOP + RAW, 4 * LOOP + RAW):
                        g = at_experts + e
                        sp.wait_ge(lo_done, 2 * LOOP * r + (n0 + e - RAW + 1))
                        sp.dma_start(raw[:, g % RAW, :], dr["experts_t"][bass.ds(2 * LOOP * r + e, 1)].rearrange("a p n -> p (a n)")).then_inc(raw_loaded[g % RAW], 16)
                next_load[0] = first + 2 * LOOP * turns
                loads(sp, at_plep + SPLIT - 1 + RAW)

            def hi(act, r, e):
                g, n = at_experts + e, n0 + e
                act.wait_ge(raw_loaded[g % RAW], 16 * (g // RAW + 1) + 16 * (2 * LOOP // RAW) * r)
                act.wait_ge(piece_used, 2 * LOOP * r + (n - SPLIT + 1))
                act.activation(whi[:, n % SPLIT, :], raw[:, g % RAW, :], ACT.Copy).then_inc(hi_done, 1)

            def lo(dve, r, e):
                g, n = at_experts + e, n0 + e
                dve.wait_ge(hi_done, 2 * LOOP * r + (n + 1))
                dve.tensor_tensor(wlo[:, n % SPLIT, :], raw[:, g % RAW, :], whi[:, n % SPLIT, :].bitcast(F32), ALU.subtract).then_inc(lo_done, 1)

            @block.tensor
            def _(pe):
                def keys(r, e, i, early):
                    n = n0 + e
                    pe.wait_ge(lo_done, 2 * LOOP * r + (n + 1))
                    if not early:
                        pe.wait_ge(gelu_done, LOOP * r + (i - 2))
                    for c in range(C):
                        mm = products(pe, ps[:, 4 + i % 3, 0:T], [w[:, n % SPLIT, c * P:c * P + P] for w in (whi, wlo)],
                                      [y[:, c, :] for y in xH], c == 0, c == C - 1)
                    mm.then_inc(piece_used, 1)

                def values(r, e, i, start=False, stop=False):
                    n = n0 + e
                    pe.wait_ge(lo_done, 2 * LOOP * r + (n + 1))
                    pe.wait_ge(weighted_lo, LOOP * r + (i + 1))
                    for c in range(C):
                        place = ps[:, c // 2, c % 2 * T:c % 2 * T + T]
                        w = [w[:, n % SPLIT, c * P:c * P + P] for w in (whi, wlo)]
                        pe.matmul(place, w[0], gh[:, i % 2, :], start=(start and c % 2 == 0), stop=False, skip_group_check=True)
                        pe.matmul(place, w[0], gl[:, i % 2, :], start=False, stop=False, skip_group_check=True)
                        mm = pe.matmul(place, w[1], gh[:, i % 2, :], start=False, stop=stop, skip_group_check=True)
                    mm.then_inc(piece_used, 1)

                def turn(r, first):
                    for i in range(LOOP):
                        keys(r, 2 * i + 1, i + 1, first and i < 2)
                        values(r, 2 * i + 2, i, start=(first and i == 0))
                keys(0, 0, 0, True)
                turn(0, True)
                with pe.Fori(1, TURNS) as r:
                    turn(r, False)
                for i in range(GROUPS - TURNS * LOOP):
                    last = i == GROUPS - TURNS * LOOP - 1
                    if not last:
                        keys(TURNS, 2 * i + 1, i + 1, False)
                    values(TURNS, 2 * i + 2 - last, i, stop=last)

            @block.scalar
            def _(act):
                def group(r, i, early=False, tail=2):
                    act.wait_ge(piece_used, 2 * LOOP * r + (n0 + max(2 * i - 1, 0) + 1))
                    if not early:
                        act.wait_ge(weighted_lo, LOOP * r + (i - 1))
                    act.activation(ga[:, i % 2, :], ps[:, 4 + i % 3, 0:T], ACT.Gelu_apprx_tanh).then_inc(gelu_done, 1)
                    if tail >= 1:
                        hi(act, r, 2 * i + 2)
                    act.wait_ge(weighted, LOOP * r + (i + 1))
                    act.activation(gh[:, i % 2, :], ga[:, i % 2, :], ACT.Copy).then_inc(weighted_hi, 1)
                    if tail >= 2:
                        hi(act, r, 2 * i + 3)
                for e in range(2):
                    if at_experts + e >= split_upto[0]:
                        split_hi(act, at_experts + e)
                for i in range(LOOP):
                    group(0, i, early=i < 2)
                with act.Fori(1, TURNS) as r:
                    for i in range(LOOP):
                        group(r, i)
                rest = GROUPS - TURNS * LOOP
                for i in range(rest):
                    group(TURNS, i, tail=min(2, 2 * (rest - 1 - i)))
                for g in ahead(at_plep):
                    split_hi(act, g)

            @block.vector
            def _(dve):
                def group(r, i, tail=2):
                    dve.wait_ge(gelu_done, LOOP * r + (i + 1))
                    dve.tensor_tensor(ga[:, i % 2, :], ga[:, i % 2, :],
                                      route[:, :, bass.ds(LOOP * r + i, 1)].rearrange("p t a -> p (t a)"), ALU.mult).then_inc(weighted, 1)
                    if tail >= 1:
                        lo(dve, r, 2 * i + 2)
                    dve.wait_ge(weighted_hi, LOOP * r + (i + 1))
                    dve.tensor_tensor(gl[:, i % 2, :], ga[:, i % 2, :], gh[:, i % 2, :].bitcast(F32), ALU.subtract).then_inc(weighted_lo, 1)
                    if tail >= 2:
                        lo(dve, r, 2 * i + 3)
                for e in range(2):
                    if at_experts + e >= split_upto[0]:
                        split_lo(dve, at_experts + e)
                for i in range(LOOP):
                    group(0, i)
                with dve.Fori(1, TURNS) as r:
                    for i in range(LOOP):
                        group(r, i)
                rest = GROUPS - TURNS * LOOP
                for i in range(rest):
                    group(TURNS, i, tail=min(2, 2 * (rest - 1 - i)))
                for g in ahead(at_plep):
                    split_lo(dve, g)
                dve.wait_ge(piece_used, n0 + LAST + 1)
                dve.tensor_tensor(hT[:, :, :].rearrange("p c t -> p (c t)"), hT[:, :, :].rearrange("p c t -> p (c t)"),
                                  ps[:, 0:4, :].rearrange("p b n -> p (b n)"), ALU.add)
        split_upto[0] = at_plep + len(ahead(at_plep))
        peer.close()

        with ExitStack() as own:
            def ob(name, shape, dt=F32):
                return own.enter_context(nc.sbuf_tensor(name, shape, dt))

            xg, xgH = ob("xg", [P, C, T]), [ob(n, [P, C, T], F32R) for n in ("xg_hi", "xg_lo")]
            pT_in, pH = ob("pT_in", [P, 2, T]), [ob(n, [P, 2, T], F32R) for n in ("pT_hi", "pT_lo")]
            emb, sg = ob("emb", [P, C, T]), ob("sg", [P, C, T])
            p_loaded, ple_step = sem("p_loaded"), sem("ple_step")
            with nc.Block() as block:
                @block.sync
                def _(sp):
                    sp.dma_start(pT_in[:, :, :], dr["p_t"]).then_inc(p_loaded, 16)
                    sp.wait_ge(p_loaded, 16)
            split_stage(pT_in, pH, 2)
            norm_stage(hT, xg, T, lambda c, s: v("ple_norm", c), parts=xgH)
            product_stage(at_plep, pH, [(1, 2, 512, [("wide", j * P, slice(0, T), *copied(j, emb[:, 4 * t + j, :])) for j in range(4)])
                                        for t in range(2)])

            def gate_of(n):
                return (lambda act, place: act.activation(sg[:, n, :], place, ACT.Sigmoid)), None
            product_stage(at_plew, xgH, wide_tiles(C, T, gate_of))
            with nc.Block() as block:
                @block.vector
                def _(dve):
                    dve.tensor_tensor(sg[:, :, :], sg[:, :, :], emb[:, :, :], ALU.mult).then_inc(ple_step, 1)
                    dve.wait_ge(ple_step, 1)
                    dve.tensor_tensor(hT[:, :, :], hT[:, :, :], sg[:, :, :], ALU.add)

        h2 = ctx.enter_context(nc.sbuf_tensor("h2", [P, C, TT], F32))
        x2H = [ctx.enter_context(nc.sbuf_tensor(n, [P, C, TT], F32R)) for n in ("x2_hi", "x2_lo")]
        ctx_loaded, mod_step = sem("ctx_loaded"), sem("mod_step")
        with nc.Block() as block:
            @block.sync
            def _(sp):
                sp.dma_start(h2[:, :, T:TT], dr["ctx_t"]).then_inc(ctx_loaded, 16)
                sp.wait_ge(ctx_loaded, 16)

            @block.vector
            def _(dve):
                dve.tensor_copy(h2[:, :, 0:T], hT[:, :, :])
                every = mod[:, :, :, :].rearrange("p l j s -> p (l j) s")
                dve.tensor_tensor(every, every, v("ada_b", 0, LAYERS * N_MOD * C).unsqueeze(2).broadcast_to([P, LAYERS * N_MOD * C, 2]), ALU.add).then_inc(mod_step, 1)
                dve.wait_ge(mod_step, 1)
                for i in range(LAYERS):
                    for g, name, at in ((gs1, "mix2", C), (gs2, "ffn2", 4 * C)):
                        dve.scalar_tensor_tensor(out=g[:, i, :, :], in0=mod[:, i, at:at + C, :], scalar=1.0,
                                                 in1=v(name, i * C, C).unsqueeze(2).broadcast_to([P, C, 2]), op0=ALU.add, op1=ALU.mult)

        def attention(units, nk, name):
            N, KB = len(units), nk // P
            DEEP, BANKS = 5, (0, 1, 6, 7)
            with ExitStack() as own, nc.Block() as block:
                pr = own.enter_context(nc.sbuf_tensor(name + "_pr", [P, DEEP, nk], F32))
                nm = own.enter_context(nc.sbuf_tensor(name + "_nm", [P, DEEP], F32))
                sums = own.enter_context(nc.sbuf_tensor(name + "_sums", [P, DEEP], F32))
                inv = own.enter_context(nc.sbuf_tensor(name + "_inv", [P, DEEP], F32))
                pT = own.enter_context(nc.sbuf_tensor(name + "_pT", [P, 2, nk], F32))

                def scores(i):
                    return ps[:, BANKS[i % len(BANKS)], 0:nk]

                @block.tensor
                def _(pe):
                    for i in range(N + 5):
                        if i < N:
                            q, keys, _, _, _, _ = units[i]
                            if i >= len(BANKS):
                                pe.wait_ge(exp_done.h, exp_done.at(i - len(BANKS) + 1))
                            pe.matmul(scores(i), q, keys, start=True, stop=True).then_inc(scores_done.h, 1)
                        if 0 <= i - 3 < N:
                            u = i - 3
                            pe.wait_ge(probs_done.h, probs_done.at(u + 1))
                            if u >= 2:
                                pe.wait_ge(turned_out.h, turned_out.at(u - 1))
                            for j in range(KB):
                                mm = pe.transpose(ps[:, 2 + u % 2, j * P:j * P + P], pr[:, u % DEEP, j * P:j * P + P], k("ident"))
                            mm.then_inc(turned.h, 1)
                        if 0 <= i - 5 < N:
                            u = i - 5
                            _, _, _, values, half, _ = units[u]
                            pe.wait_ge(turned_out.h, turned_out.at(u + 1))
                            if u >= 2:
                                pe.wait_ge(attended_out.h, attended_out.at(u - 1))
                            for j in range(KB):
                                mm = pe.matmul(ps[64 * half:64 * half + 64, 4 + u % 2, 0:P], values[j], pT[:, u % 2, j * P:j * P + P],
                                               start=(j == 0), stop=(j == KB - 1))
                            mm.then_inc(attended.h, 1)

                @block.vector
                def _(dve):
                    for i in range(N + 6):
                        if i < N:
                            _, _, bias, _, _, _ = units[i]
                            dve.wait_ge(scores_done.h, scores_done.at(i + 1))
                            if i >= DEEP:
                                dve.wait_ge(exp_done.h, exp_done.at(i - DEEP + 1))
                            if bias is not None:
                                dve.tensor_tensor(scores(i)[:, 0:T], scores(i)[:, 0:T], bias, ALU.add).then_inc(biased.h, 1)
                                dve.wait_ge(biased.h, biased.at(i + 1))
                            dve.tensor_reduce(nm[:, i % DEEP:i % DEEP + 1], scores(i), AX.X, ALU.max, negate=True).then_inc(max_done.h, 1)
                        if 0 <= i - 2 < N:
                            u, at = i - 2, (i - 2) % DEEP
                            dve.wait_ge(exp_done.h, exp_done.at(u + 1))
                            dve.reciprocal(inv[:, at:at + 1], sums[:, at:at + 1]).then_inc(probs_link.h, 1)
                            dve.wait_ge(probs_link.h, probs_link.at(u + 1))
                            dve.tensor_scalar(pr[:, at, :], pr[:, at, :], inv[:, at:at + 1], None, ALU.mult).then_inc(probs_done.h, 1)
                        if 0 <= i - 6 < N:
                            u = i - 6
                            _, _, _, _, half, place = units[u]
                            dve.wait_ge(output_hi.h, output_hi.at(u + 1))
                            dve.tensor_tensor(place[1], ps[64 * half:64 * half + 64, 4 + u % 2, 0:P], place[0].bitcast(F32), ALU.subtract).then_inc(attended_out.h, 1)

                @block.scalar
                def _(act):
                    for i in range(N + 6):
                        if 0 <= i - 6 < N:
                            u = i - 6
                            _, _, _, _, half, place = units[u]
                            act.wait_ge(attended.h, attended.at(u + 1))
                            act.activation(place[0], ps[64 * half:64 * half + 64, 4 + u % 2, 0:P], ACT.Copy).then_inc(output_hi.h, 1)
                        if i < N:
                            act.wait_ge(max_done.h, max_done.at(i + 1))
                            if i >= DEEP:
                                act.wait_ge(turned.h, turned.at(i - DEEP + 1))
                            act.activation(pr[:, i % DEEP, :], scores(i), ACT.Exp, bias=nm[:, i % DEEP:i % DEEP + 1],
                                           accum_out=sums[:, i % DEEP:i % DEEP + 1]).then_inc(exp_done.h, 1)
                        if 0 <= i - 4 < N:
                            u = i - 4
                            act.wait_ge(turned.h, turned.at(u + 1))
                            if u >= 2:
                                act.wait_ge(attended.h, attended.at(u - 1))
                            act.activation(pT[:, u % 2, :], ps[:, 2 + u % 2, 0:nk], ACT.Copy).then_inc(turned_out.h, 1)
            for s in (scores_done, max_done, exp_done, probs_link, probs_done, turned, turned_out, attended, output_hi, attended_out):
                s.advance(N)
            if units[0][2] is not None:
                biased.advance(N)

        def add_gated(i, n, at, w):
            def go(dve, place):
                for s in range(w // T):
                    o = h2[:, n, s * T:s * T + T]
                    ins = dve.scalar_tensor_tensor(out=o, in0=place[:, s * T:s * T + T], scalar=mod[:, i, at + n, s:s + 1], in1=o, op0=ALU.mult, op1=ALU.add)
                return ins
            return None, go

        def feed_forward(i, w):
            parts = [y[:, :, 0:w] for y in x2H]
            with nc.sbuf_tensor(f"x_ffn{i}", [P, C, w], F32) as x:
                norm_stage(h2[:, :, 0:w], x, w, lambda c, s: gs2[:, i, c, s:s + 1],
                           lambda c, s: mod[:, i, 3 * C + c, s:s + 1], segs=w // T, parts=parts)
            with ExitStack() as own:
                hid = [own.enter_context(nc.sbuf_tensor(f"ffn_{n}{i}", [P, FC, w], F32R)) for n in ("hi", "lo")]
                tmp = own.enter_context(nc.sbuf_tensor(f"ffn_tmp{i}", [P, 4, w], F32))

                def activated(t, j):
                    f = 2 * t + j
                    factor = ps[:, 4 * (t % 2) + 2 + j, 0:w]
                    return (lambda act, place: act.activation(tmp[:, f % 4, :], place, ACT.Silu),
                            lambda dve, place: dve.tensor_tensor(tmp[:, f % 4, :], factor, tmp[:, f % 4, :], ALU.mult))

                def parted(t, j):
                    f = 2 * t + j

                    def high(act, place):
                        act.wait_ge(dve_evacuated.h, dve_evacuated.at(4 * t + j + 1))
                        return act.activation(hid[0][:, f, :], tmp[:, f % 4, :], ACT.Copy)
                    return high, lambda dve, place: dve.tensor_tensor(hid[1][:, f, :], tmp[:, f % 4, :], hid[0][:, f, :].bitcast(F32), ALU.subtract)

                product_stage(at_f1[i], parts, [(4, 2, 512, [("wide", j * P, slice(0, w), *(activated(t, j) if j < 2 else parted(t, j - 2)))
                                                             for j in range(4)]) for t in range(FC // 2)])

                with nc.Block() as block:
                    g0 = at_f2[i]
                    after = ahead(g0 + FC)

                    @block.sync
                    def _(sp):
                        loads(sp, g0 + FC + RAW)

                    @block.tensor
                    def _(pe):
                        for f in range(FC):
                            n_ = pieces[g0 + f][3]
                            pe.wait_ge(lo_done, n_ + 1)
                            for n in range(C):
                                mm = products(pe, ps[:, n, 0:w], [y[:, n_ % SPLIT, n * P:n * P + P] for y in (whi, wlo)],
                                              [y[:, f, :] for y in hid], f == 0, f == FC - 1)
                            mm.then_inc(piece_used, 1)

                    @block.scalar
                    def _(act):
                        for g in range(max(g0, split_upto[0]), g0 + FC + len(after)):
                            split_hi(act, g)

                    @block.vector
                    def _(dve):
                        for g in range(max(g0, split_upto[0]), g0 + FC + len(after)):
                            split_lo(dve, g)
                        dve.wait_ge(piece_used, pieces[g0 + FC - 1][3] + 1)
                        for n in range(C):
                            add_gated(i, n, 5 * C, w)[1](dve, ps[:, n, 0:w])
                split_upto[0] = g0 + FC + len(after)

        def mix_norm(i):
            with nc.sbuf_tensor(f"x_mix{i}", [P, C, TT], F32) as x:
                norm_stage(h2, x, TT, lambda c, s: gs1[:, i, c, s:s + 1], lambda c, s: mod[:, i, c, s:s + 1], segs=2, parts=x2H)

        mix_norm(0)
        with ExitStack() as own:
            def ob(name, shape):
                return own.enter_context(nc.sbuf_tensor(name, shape, F32))

            qT, kT, vt = ob("na_q", [P, C, TT]), ob("na_k", [P, C, TT]), ob("na_v", [P, TT // P, D])
            bias = ob("na_bias", [P, HEADS, TB, T])
            oT = x2H
            bias_loaded = sem("bias_loaded")
            with nc.Block() as block:
                @block.sync
                def _(sp):
                    sp.dma_start(bias[:, :, :, :], dr["na_bias_t"]).then_inc(bias_loaded, 16)
            product_stage(at_qkv[0], x2H,
                          wide_tiles(C, TT, lambda n: copied(n, qT[:, n, :], DH ** -0.5)) + wide_tiles(C, TT, lambda n: copied(n, kT[:, n, :]))
                          + [(4, 2, 512, [("tall", slice(0, 512), b * P, *copied(b, vt[:, b, n * 512:n * 512 + 512])) for b in range(TT // P)])
                             for n in range(2)])
            with nc.Block() as block:
                @block.vector
                def _(dve):
                    dve.wait_ge(bias_loaded, 16)
            units, ctx_units = [], []
            for h in range(HEADS):
                half, c = h % 2, h // 2
                r = slice(64 * half, 64 * half + 64)
                for qb in range(TB):
                    q0 = qb * P
                    units.append((qT[r, c, q0:q0 + P], kT[r, c, :], bias[:, h, qb, :], [vt[:, j, h * DH:h * DH + DH] for j in range(4)],
                                  half, [y[r, c, q0:q0 + P] for y in oT]))
                    q0 += T
                    ctx_units.append((qT[r, c, q0:q0 + P], kT[r, c, T:TT], None, [vt[:, j, h * DH:h * DH + DH] for j in (2, 3)],
                                      half, [y[r, c, q0:q0 + P] for y in oT]))
            attention(units, TT, "na")
            attention(ctx_units, TC, "nactx")
            product_stage(at_o[0], oT, wide_tiles(C, TT, lambda n: add_gated(0, n, 2 * C, TT)))
        feed_forward(0, TT)

        mix_norm(1)
        with ExitStack() as own:
            def ob(name, shape):
                return own.enter_context(nc.sbuf_tensor(name, shape, F32))

            qT, kT, vt = ob("gqa_q", [P, C, T]), ob("gqa_k", [P, 2, TT]), ob("gqa_v", [P, TT // P, GQA_KV * DH])
            rope = ob("rope", [P, 2, T])
            rot = ob("rot", [P, C + 2, T])
            rope_loaded, swap_done, rope_step, rope_pool = sem("rope_loaded"), sem("swap_done"), sem("rope_step"), sem("rope_pool")
            with nc.Block() as block:
                @block.sync
                def _(sp):
                    sp.dma_start(rope[:, :, :].rearrange("p a t -> p (a t)"), dr["rope_consts"]).then_inc(rope_loaded, 16)
            product_stage(at_qkv[1], x2H, wide_tiles(C, T, lambda n: copied(n, qT[:, n, :])) + [
                (2, 4, 256, [("wide", n * P, slice(0, TT), *copied(n, kT[:, n, :])) for n in range(2)]),
                (2, 4, 256, [("tall", slice(0, 256), b * P, *copied(b, vt[:, b, :])) for b in range(TT // P)])])
            head_norm_stage(qT, C, lambda c: v("gqa_q"))
            head_norm_stage(kT[:, :, :].rearrange("p c (s t) -> p (c s) t", t=T), 4, lambda c: v("gqa_k"))
            with nc.Block() as block:
                parts = [qT[:, c, :] for c in range(C)] + [kT[:, c, 0:T] for c in range(2)]

                @block.tensor
                def _(pe):
                    for n, x in enumerate(parts):
                        if n >= 8:
                            pe.wait_ge(rope_step, 2 * (n - 8) + 1)
                        pe.matmul(ps[:, n % 8, 0:T], k("swap"), x, start=True, stop=True).then_inc(swap_done, 1)

                @block.vector
                def _(dve):
                    dve.wait_ge(rope_loaded, 16)
                    for n, x in enumerate(parts):
                        dve.wait_ge(swap_done, n + 1)
                        dve.tensor_tensor(rot[:, n, :], ps[:, n % 8, 0:T], rope[:, 1, :], ALU.mult).then_inc(rope_step, 1)
                        dve.tensor_tensor(x, x, rope[:, 0, :], ALU.mult).then_inc(rope_step, 1)
                    for n, x in enumerate(parts):
                        dve.wait_ge(rope_step, 2 * n + 2)
                        dve.tensor_tensor(x, x, rot[:, n, :], ALU.add)
            units = []
            oT = x2H
            for c in range(C):
                for half in range(2):
                    r, kv = slice(64 * half, 64 * half + 64), 2 * (c // 4) + half
                    for qb in range(TB):
                        q0 = qb * P
                        units.append((qT[r, c, q0:q0 + P], kT[r, c // 4, :], None, [vt[:, j, kv * DH:kv * DH + DH] for j in range(4)],
                                      half, [y[r, c, q0:q0 + P] for y in oT]))
            attention(units, TT, "gqa")
            product_stage(at_o[1], oT, wide_tiles(C, T, lambda n: add_gated(1, n, 2 * C, T)))
        feed_forward(1, T)

        result = ctx.enter_context(nc.sbuf_tensor("result", [P, C, T], F32))
        norm_stage(h2[:, :, 0:T], result, T, lambda c, s: v("final", c))
        with nc.Block() as block:
            @block.sync
            def _(sp):
                sp.dma_start(dr["out_t"], result[:, :, :]).then_inc(out_stored, 16)
                sp.wait_ge(out_stored, 16)



def _feature_major(a):
    return np.ascontiguousarray(a.T.reshape(-1, P, a.shape[0]).transpose(1, 0, 2))


def _column(a):
    return a.reshape(-1, P).T


def _tiles(w, width=512, per=2):
    kk, n = w.shape
    return np.ascontiguousarray(w.reshape(kk // (per * P), per, P, n // width, width).transpose(3, 0, 2, 1, 4).reshape(-1, P, per * width))


def _heads(order, width=64):
    return np.concatenate([np.arange(h * width, h * width + width) for h in order])


def _layouts(a):
    f = {n: np.asarray(x) for n, x in a.items()}
    o = {}
    consts, mix_consts, rope = const_tables()
    o["consts"], o["mix_consts"], o["rope_consts"] = consts, mix_consts, rope
    o["x_t"] = _feature_major(f["x"][0])
    o["p_t"] = _feature_major(f["p"][0, 0])
    o["ctx_t"] = _feature_major(f["ctx_2"][0])
    nsa, gqa = _heads(NSA_ORDER), _heads(GQA_ORDER)

    w = f["w_in"][0]
    hq, hf, hi, hg, nq, nkc, nvc, nks, nvs, nkw, nvw, ng = np.split(w, np.cumsum([512] * 5 + [128] * 6), axis=1)
    o["w_in_t"] = [_tiles(hf), _tiles(hq), _tiles(nq[:, nsa]), _tiles(np.concatenate([nkc, nvc, nks, nkw], axis=1)),
                   _tiles(hg), _tiles(hi), _tiles(np.concatenate([nvs, nvw, ng], axis=1), 280)]
    w1 = f["cmp_w1"][0].reshape(2, CMP_LEN, 64, 64)
    both = np.zeros((2, P, CMP_LEN, P), w1.dtype)
    both[:, 0:64, :, 0:64] = w1.transpose(0, 2, 1, 3)
    both[:, 64:, :, 64:] = w1.transpose(0, 2, 1, 3)
    o["cmp_w1_t"] = np.ascontiguousarray(both.reshape(2, P, -1, PIECE).transpose(0, 2, 1, 3).reshape(-1, P, PIECE))
    w2 = np.zeros((P, 2, P), w1.dtype)
    w2[0:64, :, 0:64] = f["cmp_w2"][0].transpose(1, 0, 2)
    w2[64:, :, 64:] = f["cmp_w2"][0].transpose(1, 0, 2)
    o["cmp_w2_t"] = w2
    o["cmp_pe_t"] = np.ascontiguousarray(np.tile(f["cmp_pe"][0].transpose(2, 0, 1), (2, 1, 1)))
    wo = f["w_out"][0]
    o["w_out_t"] = _tiles(np.concatenate([wo[:512], wo[512:][nsa]]))
    o["peer_wq_t"] = _tiles(f["peer_wq"][0])
    o["peer_keys_t"] = np.ascontiguousarray(f["peer_keys"][0].reshape(PK_SETS * PK_KEYS // PIECE, -1, P).transpose(0, 2, 1))
    u = f["peer_u"][0].reshape(PK_KEYS, PK_KEYS, C, P).transpose(1, 3, 2, 0).reshape(PK_KEYS, P, D)
    vals = f["peer_v"][0].reshape(PK_KEYS, PK_KEYS, D).transpose(1, 0, 2)
    e = np.empty((2 * PK_KEYS, P, PIECE), u.dtype)
    e[0], e[1:-1:2] = u[0], u[1:]
    e[2:-1:2], e[-1] = vals[:-1], vals[-1]
    o["experts_t"] = e
    o["ple_gate_t"] = _tiles(f["ple_gate_w"][0])
    o["ple_proj_t"] = _tiles(f["ple_proj"][0])
    o["ada_t"] = np.concatenate([_tiles(f["ada_w_2"][i]) for i in range(LAYERS)])
    o["qkv0_t"] = _tiles(f["na_w_qkv_2"][0])
    o["o0_t"] = _tiles(f["na_w_o_2"][0])
    g = f["gqa_w_qkv_2"][0]
    kv = GQA_KV * DH
    o["qkv1_t"] = [_tiles(g[:, :D][:, gqa]), _tiles(g[:, D:D + kv], kv, 4), _tiles(g[:, D + kv:], kv, 4)]
    o["o1_t"] = _tiles(f["gqa_w_o_2"][0][gqa])
    for i in range(LAYERS):
        wi = f["ffn_w_in_2"][i].reshape(D, 2, FC // 2, 2 * P).transpose(0, 2, 1, 3).reshape(D, -1)
        o[f"ffn_in{i}_t"] = _tiles(wi)
        o[f"ffn_out{i}_t"] = np.ascontiguousarray(f["ffn_w_out_2"][i].reshape(FC, P, D))

    t = np.arange(T)
    rows = T // GRID_W
    assert rows <= NA_WIN_H
    drow = (t // GRID_W)[None, :] - (t // GRID_W)[:, None] + NA_WIN_H - 1
    start = np.clip(t % GRID_W - NA_WIN_W // 2, 0, GRID_W - NA_WIN_W)[:, None]
    inside = ((t % GRID_W)[None, :] >= start) & ((t % GRID_W)[None, :] < start + NA_WIN_W)
    dcol = np.clip((t % GRID_W)[None, :] - (t % GRID_W)[:, None] + NA_WIN_W - 1, 0, 2 * NA_WIN_W - 2)
    b = np.where(inside[None], f["na_rpb_2"][0][:, drow, dcol], np.float32(NEG))
    o["na_bias_t"] = np.ascontiguousarray(b.reshape(HEADS, TB, P, T).transpose(2, 0, 1, 3))

    vecs = {"mix_norm": _column(f["mix_norm"][0]), "lb0": _column(f["hg_lb_logits"][0]), "lb1": _column(f["hg_lb_logits"][1]),
            "hg_out": _column(f["hg_out_norm"][0]), "nsa_q": np.tile(f["nsa_q_norm"][0], 2)[:, None],
            "nsa_k": np.tile(f["nsa_k_norm"][0], (1, 2)).T, "nsa_out": _column(f["nsa_out_norm"][0][nsa]),
            "ffn_norm": _column(f["ffn_norm"][0]), "ple_norm": _column(f["ple_gate_norm"][0]),
            "mix2": _column(f["norm_mix_2"].reshape(-1)), "ffn2": _column(f["norm_ffn_2"].reshape(-1)), "final": _column(f["norm_final_2"]),
            "ada_b": _column(f["ada_b_2"].reshape(-1)), "gqa_q": np.tile(f["gqa_q_gain_2"][0], 2)[:, None],
            "gqa_k": np.tile(f["gqa_k_gain_2"][0], 2)[:, None],
            "cond": np.stack([_column(f["c_2"][0]), _column(f["c_ctx_2"])], axis=-1).reshape(P, -1)}
    o["vecs"] = np.ascontiguousarray(np.concatenate([vecs[n] for n, _ in VECS], axis=1))
    return o


def kernel(**inputs):
    import concourse.bacc as bacc
    from concourse.bass_utils import run_bass_kernel_spmd as run

    nc = bacc.Bacc("TRN2", target_bir_lowering=False, num_devices=1)
    arrays, dr = {}, {}

    def given(name, a):
        arrays[name] = np.ascontiguousarray(a)
        return nc.dram_tensor(name, arrays[name].shape, mybir.dt.from_np(arrays[name].dtype), kind="ExternalInput").ap()

    for name, a in _layouts(inputs).items():
        dr[name] = [given(f"{name}_{i}", x) for i, x in enumerate(a)] if isinstance(a, list) else given(name, a)
    dr["out_t"] = nc.dram_tensor("out_t", (P, C, T), F32, kind="ExternalOutput").ap()
    build(nc, dr)
    got = run(nc, [arrays], core_ids=[0]).results[0]["out_t"]
    return np.ascontiguousarray(got.transpose(2, 1, 0).reshape(1, T, D))
```

```python
from contextlib import ExitStack

import numpy as np

import concourse.bass as bass
from concourse import mybir

F32 = mybir.dt.float32
F32R = mybir.dt.float32r
I32 = mybir.dt.int32
U32 = mybir.dt.uint32
ACT = mybir.ActivationFunctionType
ALU = mybir.AluOpType
AX = mybir.AxisListType

P = 128
D = 1024
C = D // P
T = 256
TB = T // P
TC = 256
EPS = 1e-6
NEG = -1e30
LOWEST = -3e38

HG_HEADS, HG_CHUNK = 4, 64
HG_N = T // HG_CHUNK
NSA_HEADS, NSA_KV, NSA_DH = 8, 2, 64
NSA_G = NSA_HEADS // NSA_KV
CMP_LEN, CMP_STRIDE = 32, 16
N_CMP = (T - CMP_LEN) // CMP_STRIDE + 1
SLC_LEN, SLC_TOPK, WIN = 64, 16, 512
assert T // SLC_LEN <= SLC_TOPK and T <= WIN
PK_HEADS, PK_KEYS, PK_TOP = 8, 128, 16
PK_SETS = 2 * PK_HEADS
PK_HK = PK_HEADS * PK_TOP
HEADS, DH = 16, 64
GQA_KV = 4
GRID_W, NA_WIN_W, NA_WIN_H = 64, 16, 8
FFN = 2816
FC = FFN // P
N_MOD = 6
LAYERS = 2
ROPE_THETA = 10000.0
TT = T + TC

ADA_TILES = LAYERS * N_MOD * D // 512
ADA = (3, 5, 7, 9, 10, 22, ADA_TILES)
HG_LOT, HG_END_LOT, QK_LOT, CMP_LOT, OUT_LOT, TOP_LOT, PLE_LOT = range(len(ADA))
PIECE = 1024
RAW = 4
SPLIT = 3

NSA_ORDER = [h for c in range(NSA_G) for h in (c, NSA_G + c)]
GQA_ORDER = [h for k in (0, 2) for c in range(4) for h in (4 * k + c, 4 * k + 4 + c)]

VECS = [("mix_norm", C), ("lb0", 4), ("lb1", 4), ("hg_out", 4), ("nsa_q", 1), ("nsa_k", 3), ("nsa_out", 4),
        ("ffn_norm", C), ("ple_norm", C), ("mix2", LAYERS * C), ("ffn2", LAYERS * C), ("final", C),
        ("ada_b", LAYERS * N_MOD * C), ("gqa_q", 1), ("gqa_k", 1), ("cond", 2 * C)]
VEC_AT, NV = {}, 0
for _n, _w in VECS:
    VEC_AT[_n] = NV
    NV += _w

CONSTS = [("ident", P), ("ones", P), ("ones64", P), ("iota", P), ("swap", P)]
MIX_CONSTS = [("hg_mask", P), ("dist", TB * T), ("cdist", TB * N_CMP), ("cmask", TB * N_CMP)]
CONST_AT, NCONST = {}, 0
for _n, _w in CONSTS:
    CONST_AT[_n] = NCONST
    NCONST += _w
MIX_AT, NMIX = {}, 0
for _n, _w in MIX_CONSTS:
    MIX_AT[_n] = NMIX
    NMIX += _w


def const_tables():
    t = {}
    i = np.arange(P)
    t["ident"] = np.eye(P)
    t["ones"] = np.ones((P, P))
    t["ones64"] = (i[:, None] // 64 == i[None, :] // 64) * 1.0
    t["iota"] = np.broadcast_to(i, (P, P))
    s = np.zeros((P, P))
    for m in range(P):
        k = m + 16 if m % 32 < 16 else m - 16
        s[k, m] = -1.0 if m % 32 < 16 else 1.0
    t["swap"] = s
    t["hg_mask"] = ((i[:, None] <= i[None, :]) & (i[:, None] // HG_CHUNK == i[None, :] // HG_CHUNK)) * 1.0
    pos = np.arange(T)
    dist = (pos[:, None] - pos[None, :]).astype(np.float64)
    t["dist"] = np.where(dist >= 0, -dist, NEG).reshape(TB, P, T).transpose(1, 0, 2).reshape(P, -1)
    end = np.arange(N_CMP) * CMP_STRIDE + CMP_LEN - 1
    cd = (pos[:, None] - end[None, :]).astype(np.float64)
    t["cdist"] = np.where(cd >= 0, -cd, NEG).reshape(TB, P, N_CMP).transpose(1, 0, 2).reshape(P, -1)
    t["cmask"] = ((cd >= 0) * 1.0).reshape(TB, P, N_CMP).transpose(1, 0, 2).reshape(P, -1)
    half = DH // 2
    inv = (1.0 / (np.float32(ROPE_THETA) ** (np.arange(0, half, 2, dtype=np.float32) / np.float32(half)))).astype(np.float32)
    row = (pos // GRID_W).astype(np.float32)
    col = (pos % GRID_W).astype(np.float32)
    ang = np.concatenate([np.tile((row[:, None] * inv).T, (2, 1)), np.tile((col[:, None] * inv).T, (2, 1))])
    t["cos"] = np.tile(np.cos(ang), (2, 1))
    t["sin"] = np.tile(np.sin(ang), (2, 1))
    t["rope"] = np.concatenate([t["cos"], t["sin"]], axis=1)

    def table(names):
        return np.ascontiguousarray(np.concatenate([t[n] for n in names], axis=1).astype(np.float32))
    return table([n for n, _ in CONSTS]), table([n for n, _ in MIX_CONSTS]), table(["rope"])


class Signal:

    def __init__(self, handle):
        self.h, self.base = handle, 0

    def at(self, n):
        return self.base + n

    def advance(self, n):
        self.base += n


def build(nc, dr):
    ctx = ExitStack()
    with ctx:
        def sem(name):
            return ctx.enter_context(nc.semaphore(name))

        def signal(name):
            return Signal(sem(name))

        used = []

        def numbered(name):
            used.append(name)
            return f"{name}{used.count(name)}"

        raw = ctx.enter_context(nc.sbuf_tensor("raw", [P, RAW, PIECE], F32))
        whi = ctx.enter_context(nc.sbuf_tensor("whi", [P, SPLIT, PIECE], F32R))
        wlo = ctx.enter_context(nc.sbuf_tensor("wlo", [P, SPLIT, PIECE], F32R))
        vec = ctx.enter_context(nc.sbuf_tensor("vec", [P, NV], F32))
        kon = ctx.enter_context(nc.sbuf_tensor("kon", [P, NCONST], F32))
        eps = ctx.enter_context(nc.sbuf_tensor("eps", [P, 1], F32))
        mod = ctx.enter_context(nc.sbuf_tensor("mod", [P, LAYERS, N_MOD * C, 2], F32))
        gs1 = ctx.enter_context(nc.sbuf_tensor("gs1", [P, LAYERS, C, 2], F32))
        gs2 = ctx.enter_context(nc.sbuf_tensor("gs2", [P, LAYERS, C, 2], F32))
        tokens = ctx.enter_context(ExitStack())
        hT = tokens.enter_context(nc.sbuf_tensor("hT", [P, C, T], F32, side="right"))
        ps = ctx.enter_context(nc.psum_tensor("ps", [P, 8, 512], F32))

        def v(name, i=0, n=1):
            return vec[:, VEC_AT[name] + i:VEC_AT[name] + i + n]

        def k(name, a=0, b=None):
            w = dict(CONSTS)[name]
            return kon[:, CONST_AT[name] + a:CONST_AT[name] + (w if b is None else b)]

        raw_loaded = [sem(f"raw_loaded{i}") for i in range(RAW)]
        hi_done, lo_done = sem("hi_done"), sem("lo_done")
        piece_used, raw_used = sem("piece_used"), sem("raw_used")
        start_loaded, mix_loaded = sem("start_loaded"), sem("mix_loaded")
        act_evacuated = signal("act_evacuated")
        dve_evacuated = signal("dve_evacuated")
        squares_done = signal("squares_done")
        sums_done = signal("sums_done")
        root_done = signal("root_done")
        rstd_done = signal("rstd_done")
        scaled_done = signal("scaled_done")
        rounded_done = signal("rounded_done")
        parted_done = signal("parted_done")
        dve_squares = signal("dve_squares")
        pairs_done = signal("pairs_done")
        early_squares = signal("early_squares")
        early_sums = signal("early_sums")
        ada_out = signal("ada_out")
        out_stored = sem("out_stored")

        pieces = []
        count = {True: 0, False: 0}

        own_end = {}

        def add_pieces(name, split=True, a=0, b=None, end=None):
            first = len(pieces)
            for x in dr[name] if isinstance(dr[name], list) else [dr[name]]:
                for i in range(a, x.shape[0] if b is None else b):
                    if end:
                        own_end[len(pieces)] = end(i)
                    pieces.append((x[i], x.shape[2], split, count[split]))
                    count[split] += not end
            return first

        at_ada = []

        def add_lot():
            lot = len(at_ada)
            at_ada.append(add_pieces("ada_t", False, 4 * ADA[lot - 1] if lot else 0, 4 * ADA[lot]))
        top_pe = sem("top_pe_step")
        at_in = add_pieces("w_in_t")
        add_lot()
        add_lot()
        add_lot()
        at_cmp = add_pieces("cmp_w1_t", split=False)
        add_lot()
        add_lot()
        at_wout = add_pieces("w_out_t")
        at_wq = add_pieces("peer_wq_t")
        at_keys = add_pieces("peer_keys_t", split=False, end=lambda i: (top_pe, 4 * i + 4))
        add_lot()
        at_experts = add_pieces("experts_t")
        add_lot()
        at_plep = add_pieces("ple_proj_t")
        at_plew = add_pieces("ple_gate_t")
        at_qkv = [None] * LAYERS
        at_o = [None] * LAYERS
        at_f1 = [None] * LAYERS
        at_f2 = [None] * LAYERS
        for i in range(LAYERS):
            at_qkv[i] = add_pieces(f"qkv{i}_t")
            at_o[i] = add_pieces(f"o{i}_t")
            at_f1[i] = add_pieces(f"ffn_in{i}_t")
            at_f2[i] = add_pieces(f"ffn_out{i}_t")
        n_pieces = len(pieces)
        next_load = [0]

        def loads(sp, upto):
            for g in range(next_load[0], min(upto, n_pieces)):
                if g >= RAW:
                    _, _, split, n = pieces[g - RAW]
                    if g - RAW in own_end:
                        sp.wait_ge(*own_end[g - RAW])
                    else:
                        sp.wait_ge(lo_done if split else raw_used, n + 1)
                src, w, _, _ = pieces[g]
                sp.dma_start(raw[:, g % RAW, 0:w], src).then_inc(raw_loaded[g % RAW], 16)
            next_load[0] = max(next_load[0], min(upto, n_pieces))

        def piece_loaded(eng, g):
            eng.wait_ge(raw_loaded[g % RAW], 16 * (g // RAW + 1))

        def split_hi(act, g):
            _, w, _, n = pieces[g]
            piece_loaded(act, g)
            if n >= SPLIT:
                act.wait_ge(piece_used, n - SPLIT + 1)
            act.activation(whi[:, n % SPLIT, 0:w], raw[:, g % RAW, 0:w], ACT.Copy).then_inc(hi_done, 1)

        def split_lo(dve, g):
            _, w, _, n = pieces[g]
            dve.wait_ge(hi_done, n + 1)
            dve.tensor_tensor(wlo[:, n % SPLIT, 0:w], raw[:, g % RAW, 0:w], whi[:, n % SPLIT, 0:w].bitcast(F32),
                              ALU.subtract).then_inc(lo_done, 1)

        split_upto = [0]

        def ahead(g):
            n = 0
            while n < SPLIT - 1 and g + n < n_pieces and pieces[g + n][2]:
                n += 1
            return list(range(g, g + n))

        class Parted:

            def __init__(self, src, parts, chunks):
                self.src, self.parts, self.chunks = src, parts, chunks

            def buffers(self, own):
                pass

            def act(self, act, before):
                for c in range(self.chunks):
                    before(c)
                    act.activation(self.parts[0][:, c, :], self.src[:, c, :], ACT.Copy).then_inc(rounded_done.h, 1)

            def pe(self, pe):
                pass

            def dve(self, dve, before):
                for c in range(self.chunks):
                    before(c)
                    dve.wait_ge(rounded_done.h, rounded_done.at(c + 1))
                    dve.tensor_tensor(self.parts[1][:, c, :], self.src[:, c, :], self.parts[0][:, c, :].bitcast(F32),
                                      ALU.subtract).then_inc(parted_done.h, 1)

            def end(self):
                rounded_done.advance(self.chunks)
                parted_done.advance(self.chunks)

        class Norm:

            def __init__(self, src, n, gain, shift=None, segs=1, parts=None, dst=None, logs=False, early=False):
                self.src, self.n, self.gain, self.shift, self.segs = src, n, gain, shift, segs
                self.parts, self.x, self.logs, self.early = parts, dst, logs, early

            def buffers(self, own):
                def ob(name, shape):
                    return own.enter_context(nc.sbuf_tensor(numbered(name), shape, F32))
                self.rstd = ob("rstd", [P, self.n])
                self.root = self.rstd if self.logs else ob("root", [P, self.n])
                self.idle = ob("table_load", [P, 1])
                if self.x is None:
                    self.x = ob("normed", [P, C, self.n])

            def segment(self, s):
                w = self.n // self.segs
                return slice(s * w, s * w + w)

            def squares(self, act, a, b):
                for c in range(a, b):
                    act.wait_ge(dve_evacuated.h, dve_evacuated.at(c + 1))
                    act.activation(self.x[:, c, :], self.src[:, c, :], ACT.Square).then_inc(early_squares.h, 1)

            def sums(self, pe):
                for c in range(C):
                    pe.wait_ge(early_squares.h, early_squares.at(c + 1))
                    mm = pe.matmul(ps[:, 0, 0:self.n], k("ones"), self.x[:, c, :], start=(c == 0), stop=(c == C - 1))
                mm.then_inc(early_sums.h, 1)

            def end_early(self):
                early_squares.advance(C)
                early_sums.advance(1)

            def act(self, act, before):
                x, half = self.x, C // 2
                if not self.early:
                    for c in range(half):
                        act.activation(x[:, c, :], self.src[:, c, :], ACT.Square).then_inc(squares_done.h, 1)
                    act.activation(self.idle[:, :], eps[:, :], ACT.Ln if self.logs else ACT.Sqrt)
                    act.wait_ge(sums_done.h, sums_done.at(1))
                act.activation(self.root[:, :], ps[:, 0, 0:self.n], ACT.Ln if self.logs else ACT.Sqrt,
                               bias=eps[:, :], scale=1.0 / D).then_inc(root_done.h, 1)
                if self.logs:
                    act.wait_ge(root_done.h, root_done.at(1))
                    act.activation(self.rstd[:, :], self.root[:, :], ACT.Exp, scale=-0.5).then_inc(rstd_done.h, 1)
                if self.parts:
                    for c in range(C):
                        before(c)
                        act.wait_ge(scaled_done.h, scaled_done.at(c + 1))
                        for s in range(self.segs):
                            t = self.segment(s)
                            kind, add = (ACT.Copy, {}) if self.shift is None else (ACT.Identity, {"bias": self.shift(c, s)})
                            ins = act.activation(self.parts[0][:, c, t], x[:, c, t], kind, **add)
                        ins.then_inc(rounded_done.h, 1)

            def pe(self, pe):
                if self.early:
                    return
                half = C // 2
                for c in range(half):
                    pe.wait_ge(pairs_done.h, pairs_done.at(c + 1))
                    mm = pe.matmul(ps[:, 0, 0:self.n], k("ones"), self.x[:, half + c, :], start=(c == 0), stop=(c == half - 1))
                mm.then_inc(sums_done.h, 1)

            def dve(self, dve, before):
                x, half = self.x, C // 2
                for c in range(0 if self.early else half + 1):
                    if c < half:
                        dve.tensor_tensor(x[:, half + c, :], self.src[:, half + c, :], self.src[:, half + c, :], ALU.mult).then_inc(dve_squares.h, 1)
                    if c >= 1:
                        dve.wait_ge(squares_done.h, squares_done.at(c))
                        dve.wait_ge(dve_squares.h, dve_squares.at(c))
                        dve.tensor_tensor(x[:, half + c - 1, :], x[:, half + c - 1, :], x[:, c - 1, :], ALU.add).then_inc(pairs_done.h, 1)
                if not self.logs:
                    dve.wait_ge(root_done.h, root_done.at(1))
                    dve.reciprocal(self.rstd[:, :], self.root[:, :]).then_inc(rstd_done.h, 1)
                dve.wait_ge(rstd_done.h, rstd_done.at(1))
                for c in range(C + 1):
                    if c < C:
                        for s in range(self.segs):
                            t = self.segment(s)
                            ins = dve.scalar_tensor_tensor(out=x[:, c, t], in0=self.src[:, c, t], scalar=self.gain(c, s), in1=self.rstd[:, t],
                                                           op0=ALU.mult, op1=ALU.mult)
                        ins.then_inc(scaled_done.h, 1)
                    if self.parts and c >= 1:
                        before(c - 1)
                        dve.wait_ge(rounded_done.h, rounded_done.at(c))
                        for s in range(self.segs):
                            t = self.segment(s)
                            low, high = self.parts[1][:, c - 1, t], self.parts[0][:, c - 1, t].bitcast(F32)
                            if self.shift is None:
                                ins = dve.tensor_tensor(low, x[:, c - 1, t], high, ALU.subtract)
                            else:
                                ins = dve.scalar_tensor_tensor(out=low, in0=x[:, c - 1, t], scalar=self.shift(c - 1, s), in1=high,
                                                               op0=ALU.add, op1=ALU.subtract)
                        ins.then_inc(parted_done.h, 1)

            def end(self):
                for s, n in ((root_done, 1), (rstd_done, 1), (scaled_done, C)):
                    s.advance(n)
                if not self.early:
                    for s, n in ((squares_done, C // 2), (dve_squares, C // 2), (pairs_done, C // 2), (sums_done, 1)):
                        s.advance(n)
                if self.parts:
                    rounded_done.advance(C)
                    parted_done.advance(C)

        def products(pe, place, stationary, moving, start, stop):
            (wh, wl), (xh, xl) = stationary, moving
            pe.matmul(place, wh, xh, start=start, stop=False)
            pe.matmul(place, wh, xl, start=False, stop=False)
            return pe.matmul(place, wl, xh, start=False, stop=stop)

        def product_stage(first, x, tiles, before=None, lot=None, sync=None, then=None, last=None):
            at, a_n, d_n, spans = first, 0, 0, []
            for n_pc, per, width, jobs in tiles:
                outs = []
                for j in jobs:
                    a_n += j[3] is not None
                    d_n += j[4] is not None
                    outs.append((a_n, d_n))
                spans.append((at, outs))
                at += n_pc
            after = ahead(at)

            def place(t, j):
                kind, a, b, _, _ = tiles[t][3][j]
                n = (b.stop - b.start) if kind == "wide" else a.stop - a.start
                return ps[:, 4 * (t % 2) + j, 0:n]

            def of_first(c):
                per = tiles[0][1]
                return [first + c // per] if c % per == 0 and first + c // per >= split_upto[0] else []

            with ExitStack() as own, nc.Block() as block:
                if before:
                    before.buffers(own)

                @block.sync
                def _(sp):
                    if sync:
                        sync(sp)
                    loads(sp, at + RAW)

                @block.tensor
                def _(pe):
                    if lot is not None:
                        ada_lot_pe(pe, lot, 4)
                    if before:
                        before.pe(pe)
                    for t, (n_pc, per, width, jobs) in enumerate(tiles):
                        g0, _ = spans[t]
                        if t == 1 and lot is not None:
                            pe.wait_ge(ada_out.h, ada_out.at(1))
                        if t >= 2:
                            a_out, d_out = spans[t - 2][1][-1]
                            if a_out:
                                pe.wait_ge(act_evacuated.h, act_evacuated.at(a_out))
                            if d_out:
                                pe.wait_ge(dve_evacuated.h, dve_evacuated.at(d_out))
                        for g in range(g0, g0 + n_pc):
                            _, _, _, n = pieces[g]
                            pe.wait_ge(lo_done, n + 1)
                            wp = [w[:, n % SPLIT, 0:per * width].rearrange("p (c n) -> p c n", n=width) for w in (whi, wlo)]
                            for i in range(per):
                                c = (g - g0) * per + i
                                first_c, last_c = c == 0, c == n_pc * per - 1
                                if before and t == 0:
                                    pe.wait_ge(parted_done.h, parted_done.at(c + 1))
                                for j, (kind, a, b, _, _) in enumerate(jobs):
                                    if kind == "wide":
                                        w, y = [v_[:, i, a:a + P] for v_ in wp], [v_[:, c, b] for v_ in x]
                                    else:
                                        w, y = [v_[:, c, b:b + P] for v_ in x], [v_[:, i, a] for v_ in wp]
                                    mm = products(pe, place(t, j), w, y, first_c, last_c)
                            mm.then_inc(piece_used, 1)
                    if then:
                        then.sums(pe)

                @block.scalar
                def _(act):
                    def take_out(t):
                        g0, _ = spans[t]
                        act.wait_ge(piece_used, pieces[g0 + tiles[t][0] - 1][3] + 1)
                        for j, job in enumerate(tiles[t][3]):
                            if job[3] is not None:
                                job[3](act, place(t, j)).then_inc(act_evacuated.h, 1)
                        if then:
                            then.squares(act, 4 * t, 4 * t + 4)
                    if lot is not None:
                        ada_lot_act(act, lot, 4)
                    if before:
                        before.act(act, lambda c: [split_hi(act, g) for g in of_first(c)])
                    for t, (n_pc, _, _, _) in enumerate(tiles):
                        for i in range(n_pc):
                            if spans[t][0] + i >= split_upto[0] and not (before and t == 0):
                                split_hi(act, spans[t][0] + i)
                            if t >= 1 and i == min(1, n_pc - 1):
                                take_out(t - 1)
                    for g in after:
                        split_hi(act, g)
                    take_out(len(tiles) - 1)

                @block.vector
                def _(dve):
                    def take_out(t):
                        g0, outs = spans[t]
                        dve.wait_ge(piece_used, pieces[g0 + tiles[t][0] - 1][3] + 1)
                        for j, job in enumerate(tiles[t][3]):
                            if job[4] is not None:
                                if job[3] is not None:
                                    dve.wait_ge(act_evacuated.h, act_evacuated.at(outs[j][0]))
                                job[4](dve, place(t, j)).then_inc(dve_evacuated.h, 1)
                    if before:
                        before.dve(dve, lambda c: [split_lo(dve, g) for g in of_first(c)])
                    for t, (n_pc, _, _, _) in enumerate(tiles):
                        for i in range(n_pc):
                            if spans[t][0] + i >= split_upto[0] and not (before and t == 0):
                                split_lo(dve, spans[t][0] + i)
                            if t >= 1 and i == min(1, n_pc - 1):
                                take_out(t - 1)
                    for g in after:
                        split_lo(dve, g)
                    if last:
                        last(dve)
                    take_out(len(tiles) - 1)
            split_upto[0] = at + len(after)
            act_evacuated.advance(a_n)
            dve_evacuated.advance(d_n)
            if before:
                before.end()
            if then:
                then.end_early()
            if lot is not None:
                ada_out.advance(1)

        def wide_tiles(n, w, out, x0=0):
            return [(4, 2, 512, [("wide", j * P, slice(x0, x0 + w), *out(4 * t + j)) for j in range(4)]) for t in range(n // 4)]

        def copied(n, dst, scale=None):
            if n % 2 == 0:
                return (lambda act, place: act.activation(dst, place, ACT.Copy, scale=1.0 if scale is None else scale)), None
            if scale is None:
                return None, lambda dve, place: dve.tensor_copy(dst, place)
            return None, lambda dve, place: dve.tensor_scalar(dst, place, scale, None, ALU.mult)

        def head_norm_stage(x, n, gain, lot=None, logs=False):
            flat = x.rearrange("p n t -> p (n t)")
            groups = n * T // 512
            with ExitStack() as own, nc.Block() as block:
                sq = own.enter_context(nc.sbuf_tensor(numbered("head_squares"), [P, n * T], F32))
                rstd = own.enter_context(nc.sbuf_tensor(numbered("head_rstd"), [P, n, T], F32))

                flat_rstd = rstd[:, :, :].rearrange("p n t -> p (n t)")

                @block.sync
                def _(sp):
                    if lot is not None:
                        loads(sp, lot_end(lot) + RAW)

                @block.scalar
                def _(act):
                    act.activation(sq[:, :], flat, ACT.Square).then_inc(squares_done.h, 1)
                    act.wait_ge(sums_done.h, sums_done.at(1))
                    act.activation(sq[:, :], ps[:, 0:groups, :].rearrange("p g t -> p (g t)"), ACT.Ln if logs else ACT.Sqrt,
                                   bias=eps[:, :], scale=1.0 / 64).then_inc(root_done.h, 1)
                    if logs:
                        act.wait_ge(root_done.h, root_done.at(1))
                        act.activation(flat_rstd, sq[:, :], ACT.Exp, scale=-0.5).then_inc(rstd_done.h, 1)
                    if lot is not None:
                        ada_lot_act(act, lot, 4)

                @block.tensor
                def _(pe):
                    pe.wait_ge(squares_done.h, squares_done.at(1))
                    for g in range(groups):
                        mm = pe.matmul(ps[:, g, :], k("ones64"), sq[:, g * 512:g * 512 + 512], start=True, stop=True)
                    mm.then_inc(sums_done.h, 1)
                    if lot is not None:
                        ada_lot_pe(pe, lot, 4)

                @block.vector
                def _(dve):
                    if not logs:
                        dve.wait_ge(root_done.h, root_done.at(1))
                        dve.reciprocal(flat_rstd, sq[:, :]).then_inc(rstd_done.h, 1)
                    dve.wait_ge(rstd_done.h, rstd_done.at(1))
                    for c in range(n):
                        dve.scalar_tensor_tensor(out=x[:, c, :], in0=x[:, c, :], scalar=gain(c), in1=rstd[:, c, :],
                                                 op0=ALU.mult, op1=ALU.mult)
            for s in (squares_done, sums_done, root_done, rstd_done):
                s.advance(1)
            if lot is not None:
                ada_out.advance(1)

        ada_rows_out, ada_turned = sem("ada_rows_out"), sem("ada_turned")
        cond = ctx.enter_context(nc.sbuf_tensor("cond", [P, C, 2], F32))
        ada_row = []

        def lot_tiles(lot):
            return ADA[lot - 1] if lot else 0, ADA[lot]

        def lot_end(lot):
            a, b = lot_tiles(lot)
            return at_ada[lot] + 4 * (b - a)

        def ada_first(t, lot):
            return at_ada[lot] + 4 * (t - lot_tiles(lot)[0])

        def ada_turn(pe, t, lot, bank0):
            pe.wait_ge(ada_rows_out, t + 1)
            for j in range(4):
                n = 4 * (t - lot_tiles(lot)[0]) + j
                mm = pe.transpose(ps[:, bank0 + 2, 2 * n:2 * n + 2], ada_row[-1][:, t % 2, j * P:j * P + P], k("ident")[0:2, 0:2])
            mm.then_inc(ada_turned, 1)

        def ada_tile_pe(pe, t, lot, bank0):
            a, b = lot_tiles(lot)
            if t >= a + 2:
                pe.wait_ge(ada_rows_out, t - 1)
            for i in range(4):
                g = ada_first(t, lot) + i
                piece_loaded(pe, g)
                for j in range(2):
                    c = 2 * i + j
                    mm = pe.matmul(ps[0:2, bank0 + t % 2, :], cond[:, c, :], raw[:, g % RAW, j * 512:j * 512 + 512], start=(c == 0), stop=(c == C - 1))
                mm.then_inc(raw_used, 1)
            if t > a:
                ada_turn(pe, t - 1, lot, bank0)
            if t == b - 1:
                ada_turn(pe, t, lot, bank0)

        def ada_tile_act(act, t, lot, bank0):
            a, b = lot_tiles(lot)
            act.wait_ge(raw_used, pieces[ada_first(t, lot) + 3][3] + 1)
            if t >= 2:
                act.wait_ge(ada_turned, t - 1)
            act.activation(ada_row[-1][:, t % 2, :], ps[0:2, bank0 + t % 2, :], ACT.Copy).then_inc(ada_rows_out, 1)
            if t == b - 1:
                act.wait_ge(ada_turned, b)
                act.activation(mod[:, :, :, :].rearrange("p l j s -> p (l j s)")[:, 8 * a:8 * b], ps[:, bank0 + 2, 0:8 * (b - a)],
                               ACT.Copy).then_inc(ada_out.h, 1)

        def ada_lot_pe(pe, lot, bank0):
            for t in range(*lot_tiles(lot)):
                ada_tile_pe(pe, t, lot, bank0)

        def ada_lot_act(act, lot, bank0):
            for t in range(*lot_tiles(lot)):
                ada_tile_act(act, t, lot, bank0)

        mixer = ctx.enter_context(ExitStack())

        def mb(name, shape):
            return mixer.enter_context(nc.sbuf_tensor(name, shape, F32))

        row_space = ctx.enter_context(ExitStack())
        ada_row.append(row_space.enter_context(nc.sbuf_tensor("ada_row", [2, 2, 512], F32, side="right")))
        aH = [mixer.enter_context(nc.sbuf_tensor(n, [P, C, T], F32R)) for n in ("aT_hi", "aT_lo")]
        hgT = mb("hgT", [P, 3, 4, T])
        nqk = mb("nqk", [P, 6, T])
        cin = mb("cin", [P, 2, T])
        hg_v = mb("hg_v", [P, TB, 512])
        nv = mb("nv", [P, TB, 280])
        mixT = mb("mixT", [P, C, T])
        mkon = mb("mkon", [P, NMIX])
        cmp_pe = mb("cmp_pe", [P, 2, CMP_LEN])
        cmp_w2 = mb("cmp_w2", [P, 2, P])

        def mk(name):
            return mkon[:, MIX_AT[name]:MIX_AT[name] + dict(MIX_CONSTS)[name]]

        with nc.Block() as block:
            @block.sync
            def _(sp):
                sp.dma_start(hT[:, :, :], dr["x_t"]).then_inc(start_loaded, 16)
                sp.dma_start(vec[:, :], dr["vecs"]).then_inc(start_loaded, 16)
                sp.dma_start(kon[:, :], dr["consts"]).then_inc(start_loaded, 16)
                loads(sp, RAW)
                sp.dma_start(mkon[:, :], dr["mix_consts"]).then_inc(mix_loaded, 16)
                sp.dma_start(cmp_pe[:, :, :], dr["cmp_pe_t"]).then_inc(mix_loaded, 16)
                sp.dma_start(cmp_w2[:, :, :], dr["cmp_w2_t"]).then_inc(mix_loaded, 16)

            @block.vector
            def _(dve):
                dve.memset(eps[:, :], EPS)
                dve.wait_ge(start_loaded, 48)

        chunks = ([hgT[:, 0, j, :] for j in range(4)] + [hgT[:, 1, j, :] for j in range(4)] + [nqk[:, j, :] for j in range(4)]
                  + [cin[:, 0, :], cin[:, 1, :], nqk[:, 4, :], nqk[:, 5, :]] + [hgT[:, 2, j, :] for j in range(4)])
        product_stage(at_in, aH, wide_tiles(len(chunks), T, lambda n: copied(n, chunks[n]))
                      + [(4, 2, 512, [("tall", slice(0, 512), b * P, *copied(b, hg_v[:, b, :])) for b in range(TB)]),
                         (4, 2, 280, [("tall", slice(0, 280), b * P, *copied(b, nv[:, b, :])) for b in range(TB)])],
                      before=Norm(hT, T, lambda c, s: v("mix_norm", c), parts=aH))

        hg_act, hg_dve, hg_pe = sem("hg_act_step"), sem("hg_dve_step"), sem("hg_pe_step")
        hg_cond = sem("hg_cond")
        with ExitStack() as own, nc.Block() as block:
            def ob(name, shape):
                return own.enter_context(nc.sbuf_tensor(name, shape, F32))

            H4 = [P, HG_HEADS, T]
            lb, lbd, oml = ob("lb", [P, 4]), ob("lbd", [P, 4]), ob("oml", [P, 4])
            keep, sig, forget, key, logf, G = (ob(n, H4) for n in ("keep", "sig", "forget", "key", "logf", "G"))
            d1, d4, e1, e2, e3, e4 = (ob(n, H4) for n in ("d1", "d4", "e1", "e2", "e3", "e4"))
            qs, gate, qa, ka, qi, ki = (ob(n, H4) for n in ("qs", "gate", "qa", "ka", "qi", "ki"))
            am = ob("am", [P, TB, 512])
            kiT = ob("kiT", [P, TB, 512])
            S = ob("S", [P, 3, 512])
            osq, on, rstd = am, sig, kiT

            def fl(x):
                return x[:, :, :].rearrange("p h t -> p (h t)")

            def ch(x):
                return fl(x).rearrange("p (n s) -> p n s", s=HG_CHUNK)

            def at_end(x, i):
                return ch(x)[:, :, i:i + 1].broadcast_to([P, HG_HEADS * HG_N, HG_CHUNK])

            @block.scalar
            def _(act):
                act.activation(cond[:, :, :].rearrange("p c s -> p (c s)"), v("cond", 0, 2 * C), ACT.Silu).then_inc(hg_cond, 1)
                act.activation(fl(sig), hgT[:, 0, :, :].rearrange("p h t -> p (h t)"), ACT.Sigmoid).then_inc(hg_act, 1)
                act.wait_ge(hg_dve, 1)
                act.activation(lb[:, :], lbd[:, :], ACT.Sigmoid).then_inc(hg_act, 1)
                act.activation(fl(qs), hgT[:, 1, :, :].rearrange("p h t -> p (h t)"), ACT.Silu).then_inc(hg_act, 1)
                act.activation(fl(gate), hgT[:, 2, :, :].rearrange("p h t -> p (h t)"), ACT.Silu).then_inc(hg_act, 1)
                act.wait_ge(hg_dve, 9)
                act.activation(fl(logf), fl(forget), ACT.Ln).then_inc(hg_act, 1)
                ada_tile_act(act, 0, HG_LOT, 4)
                act.wait_ge(hg_dve, 13)
                act.activation(fl(e1), fl(d1), ACT.Exp).then_inc(hg_act, 1)
                act.activation(fl(e2), fl(d1), ACT.Exp, scale=-1.0).then_inc(hg_act, 1)
                act.activation(fl(e3), fl(G), ACT.Exp).then_inc(hg_act, 1)
                act.activation(fl(e4), fl(d4), ACT.Exp).then_inc(hg_act, 1)
                for t in range(1, ADA[HG_LOT]):
                    ada_tile_act(act, t, HG_LOT, 4)
                for b in range(TB):
                    act.wait_ge(hg_pe, 3 + b)
                    act.activation(kiT[:, b, :], ps[:, 2 + b, :], ACT.Copy).then_inc(hg_act, 1)
                for b in range(TB):
                    act.wait_ge(hg_pe, 8 + b)
                    act.activation(osq[:, b, :], ps[:, b, :], ACT.Square).then_inc(hg_act, 1)
                act.wait_ge(hg_pe, 10)
                act.activation(osq[:, :, :].rearrange("p b n -> p (b n)"), ps[:, 2:4, :].rearrange("p b n -> p (b n)"),
                               ACT.Sqrt, bias=eps[:, :], scale=1.0 / P).then_inc(hg_act, 1)
                ada_lot_act(act, HG_END_LOT, 4)

            @block.vector
            def _(dve):
                dve.tensor_scalar(v("nsa_q"), v("nsa_q"), NSA_DH ** -0.5, None, ALU.mult)
                dve.tensor_scalar(v("gqa_q"), v("gqa_q"), DH ** -0.5, None, ALU.mult)
                dve.tensor_tensor(lbd[:, :], v("lb0", 0, 4), v("lb1", 0, 4), ALU.subtract).then_inc(hg_dve, 1)
                dve.memset(keep[:, :, :], 1.0).then_inc(hg_dve, 1)
                dve.wait_ge(hg_dve, 2)
                dve.memset(ch(keep)[:, :, 0:1], 0.0).then_inc(hg_dve, 1)
                dve.memset(am[:, :, :], 0.0).then_inc(hg_dve, 1)
                dve.wait_ge(hg_act, 2)
                dve.tensor_scalar(oml[:, :], lb[:, :], -1.0, 1.0, ALU.mult, ALU.add).then_inc(hg_dve, 1)
                dve.wait_ge(hg_dve, 5)
                for h in range(4):
                    dve.tensor_scalar(forget[:, h, :], sig[:, h, :], oml[:, h:h + 1], lb[:, h:h + 1], ALU.mult, ALU.add).then_inc(hg_dve, 1)
                dve.wait_ge(hg_dve, 9)
                dve.tensor_scalar(fl(key), fl(forget), -1.0, 1.0, ALU.mult, ALU.add).then_inc(hg_dve, 1)
                dve.wait_ge(hg_act, 5)
                dve.tensor_tensor_scan(fl(G), fl(keep), fl(logf), 0.0, ALU.mult, ALU.add).then_inc(hg_dve, 1)
                dve.wait_ge(hg_dve, 11)
                dve.tensor_tensor(ch(d1), ch(G), at_end(G, HG_CHUNK // 2 - 1), ALU.subtract).then_inc(hg_dve, 1)
                dve.tensor_tensor(ch(d4), at_end(G, HG_CHUNK - 1), ch(G), ALU.subtract).then_inc(hg_dve, 1)
                dve.wait_ge(hg_act, 6)
                dve.scalar_tensor_tensor(out=fl(qa), in0=fl(qs), scalar=P ** -0.5, in1=fl(e1), op0=ALU.mult, op1=ALU.mult).then_inc(hg_dve, 1)
                dve.wait_ge(hg_act, 7)
                dve.tensor_tensor(fl(ka), fl(key), fl(e2), ALU.mult).then_inc(hg_dve, 1)
                dve.wait_ge(hg_act, 8)
                dve.scalar_tensor_tensor(out=fl(qi), in0=fl(qs), scalar=P ** -0.5, in1=fl(e3), op0=ALU.mult, op1=ALU.mult).then_inc(hg_dve, 1)
                dve.wait_ge(hg_act, 9)
                dve.tensor_tensor(fl(ki), fl(key), fl(e4), ALU.mult).then_inc(hg_dve, 1)
                dve.wait_ge(mix_loaded, 48)
                mask = mk("hg_mask").bitcast(I32).unsqueeze(1).broadcast_to([P, HG_HEADS, P])
                for b in range(TB):
                    dve.wait_ge(hg_pe, 1 + b)
                    dve.copy_predicated(am[:, b, :].rearrange("p (h t) -> p h t", t=P), mask,
                                        ps[:, b, :].rearrange("p (h t) -> p h t", t=P)).then_inc(hg_dve, 1)
                dve.wait_ge(hg_pe, 5)
                dve.tensor_copy(S[:, 0, :], ps[:, 4, :]).then_inc(hg_dve, 1)
                for n in range(1, 3):
                    dve.wait_ge(hg_dve, 16 + 4 * n)
                    dve.wait_ge(hg_pe, 5 + n)
                    for h in range(4):
                        end = n * HG_CHUNK + HG_CHUNK - 1
                        o = slice(h * P, h * P + P)
                        dve.scalar_tensor_tensor(out=S[:, n, o], in0=S[:, n - 1, o], scalar=e3[:, h, end:end + 1], in1=ps[:, 4 + n, o],
                                                 op0=ALU.mult, op1=ALU.add).then_inc(hg_dve, 1)
                dve.wait_ge(hg_act, 14)
                dve.reciprocal(rstd[:, :, :].rearrange("p b n -> p (b n)"), osq[:, :, :].rearrange("p b n -> p (b n)")).then_inc(hg_dve, 1)
                dve.wait_ge(hg_dve, 29)
                for b in range(TB):
                    for h in range(4):
                        o = slice(h * P, h * P + P)
                        dve.scalar_tensor_tensor(out=on[:, h, b * P:b * P + P], in0=ps[:, b, o], scalar=v("hg_out", h), in1=rstd[:, b, o],
                                                 op0=ALU.mult, op1=ALU.mult).then_inc(hg_dve, 1)
                dve.wait_ge(hg_dve, 37)
                dve.tensor_tensor(mixT[:, 0:4, :].rearrange("p h t -> p (h t)"), fl(on), fl(gate), ALU.mult)

            @block.sync
            def _(sp):
                loads(sp, lot_end(HG_END_LOT) + RAW)

            @block.tensor
            def _(pe):
                pe.wait_ge(hg_cond, 1)
                ada_lot_pe(pe, HG_LOT, 4)
                pe.wait_ge(hg_dve, 15)
                for b in range(TB):
                    for h in range(4):
                        o, t = slice(h * P, h * P + P), slice(b * P, b * P + P)
                        mm = pe.matmul(ps[:, b, o], ka[:, h, t], qa[:, h, t], start=True, stop=True)
                    mm.then_inc(hg_pe, 1)
                pe.wait_ge(hg_dve, 17)
                for b in range(TB):
                    for h in range(4):
                        o, t = slice(h * P, h * P + P), slice(b * P, b * P + P)
                        mm = pe.transpose(ps[:, 2 + b, o], ki[:, h, t], k("ident"))
                    mm.then_inc(hg_pe, 1)
                pe.wait_ge(ada_out.h, ada_out.at(1))
                for n in range(3):
                    b, r = n // 2, slice((n % 2) * HG_CHUNK, (n % 2) * HG_CHUNK + HG_CHUNK)
                    pe.wait_ge(hg_act, 10 + b)
                    for h in range(4):
                        o = slice(h * P, h * P + P)
                        mm = pe.matmul(ps[:, 4 + n, o], kiT[r, b, o], hg_v[r, b, o], start=True, stop=True)
                    mm.then_inc(hg_pe, 1)
                for b in range(TB):
                    pe.wait_ge(hg_dve, 19)
                    for h in range(4):
                        o = slice(h * P, h * P + P)
                        pe.matmul(ps[:, b, o], hg_v[:, b, o], am[:, b, o], start=(h == 0), stop=False, skip_group_check=True)
                    for n in range(max(1, 2 * b), 2 * b + 2):
                        pe.wait_ge(hg_dve, 16 + 4 * n)
                        for h in range(4):
                            at = h * P + (n % 2) * HG_CHUNK
                            mm = pe.matmul(ps[:, b, at:at + HG_CHUNK], S[:, n - 1, h * P:h * P + P], qi[:, h, n * HG_CHUNK:n * HG_CHUNK + HG_CHUNK],
                                           start=False, stop=True, skip_group_check=True)
                    mm.then_inc(hg_pe, 1)
                pe.wait_ge(hg_act, 13)
                for b in range(TB):
                    mm = pe.matmul(ps[:, 2 + b, :], k("ones"), osq[:, b, :], start=True, stop=True)
                mm.then_inc(hg_pe, 1)
                ada_lot_pe(pe, HG_END_LOT, 4)

        ada_out.advance(2)

        head_norm_stage(nqk, 6, lambda c: v("nsa_q") if c < 4 else v("nsa_k", c - 3), lot=QK_LOT)

        kcn = mb("kcn", [P, N_CMP])
        vcs = mb("vcs", [N_CMP, P])
        gates = mb("gates", [P, TB, 3 * NSA_HEADS])
        cmp_act, cmp_dve, cmp_pe_step = sem("cmp_act_step"), sem("cmp_dve_step"), sem("cmp_pe_step")
        with ExitStack() as own, nc.Block() as block:
            win = own.enter_context(nc.sbuf_tensor("win", [P, 2, CMP_LEN, N_CMP], F32))
            rows = own.enter_context(nc.sbuf_tensor("cmp_rows", [N_CMP, 2, P], F32))
            hid = own.enter_context(nc.sbuf_tensor("cmp_hid", [P, 2, N_CMP], F32))
            csq = own.enter_context(nc.sbuf_tensor("cmp_sq", [P, N_CMP], F32))
            crs = own.enter_context(nc.sbuf_tensor("cmp_rstd", [P, N_CMP], F32))
            c3 = cin[:, :, :].rearrange("p i (n l) -> p i l n", l=CMP_STRIDE)

            @block.sync
            def _(sp):
                loads(sp, lot_end(CMP_LOT) + RAW)

            @block.vector
            def _(dve):
                for i in range(2):
                    for j in range(2):
                        l = slice(j * CMP_STRIDE, j * CMP_STRIDE + CMP_STRIDE)
                        dve.tensor_tensor(win[:, i, l, :], c3[:, i, :, j:j + N_CMP],
                                          cmp_pe[:, i, l].unsqueeze(2).broadcast_to([P, CMP_STRIDE, N_CMP]), ALU.add).then_inc(cmp_dve, 1)
                dve.wait_ge(cmp_act, 7)
                dve.reciprocal(crs[:, :], csq[:, :]).then_inc(cmp_dve, 1)
                dve.wait_ge(cmp_dve, 5)
                dve.scalar_tensor_tensor(out=kcn[:, :], in0=ps[:, 2, 0:N_CMP], scalar=v("nsa_k", 0), in1=crs[:, :], op0=ALU.mult, op1=ALU.mult)
                dve.tensor_copy(vcs[:, :], ps[0:N_CMP, 3, 0:P])

            @block.tensor
            def _(pe):
                for i in range(2):
                    pe.wait_ge(cmp_dve, 2 * i + 2)
                    per = PIECE // P
                    for l in range(CMP_LEN):
                        g = at_cmp + (i * CMP_LEN + l) // per
                        if l % per == 0:
                            piece_loaded(pe, g)
                        o = l % per * P
                        mm = pe.matmul(ps[0:N_CMP, i, 0:P], win[:, i, l, :], raw[:, g % RAW, o:o + P], start=(l == 0), stop=(l == CMP_LEN - 1))
                        if l % per == per - 1:
                            mm.then_inc(raw_used, 1)
                for i in range(2):
                    pe.wait_ge(cmp_act, 1 + i)
                    pe.transpose(ps[:, 5 + i, 0:N_CMP], rows[:, i, :], k("ident")[0:N_CMP, 0:N_CMP]).then_inc(cmp_pe_step, 1)
                pe.wait_ge(cmp_act, 4)
                pe.matmul(ps[:, 2, 0:N_CMP], cmp_w2[:, 0, :], hid[:, 0, :], start=True, stop=True).then_inc(cmp_pe_step, 1)
                pe.matmul(ps[0:N_CMP, 3, 0:P], hid[:, 1, :], cmp_w2[:, 1, :], start=True, stop=True).then_inc(cmp_pe_step, 1)
                a, b = lot_tiles(CMP_LOT)
                ada_tile_pe(pe, a, CMP_LOT, 5)
                pe.wait_ge(cmp_act, 6)
                pe.matmul(ps[:, 4, 0:N_CMP], k("ones64"), csq[:, :], start=True, stop=True).then_inc(cmp_pe_step, 1)
                for t in range(a + 1, b):
                    ada_tile_pe(pe, t, CMP_LOT, 5)

            @block.scalar
            def _(act):
                for i in range(2):
                    act.wait_ge(raw_used, pieces[at_cmp][3] + (i + 1) * CMP_LEN * P // PIECE)
                    act.activation(rows[:, i, :], ps[0:N_CMP, i, 0:P], ACT.Gelu_apprx_tanh).then_inc(cmp_act, 1)
                for i in range(2):
                    act.wait_ge(cmp_pe_step, 1 + i)
                    act.activation(hid[:, i, :], ps[:, 5 + i, 0:N_CMP], ACT.Copy).then_inc(cmp_act, 1)
                act.activation(gates[:, :, :], nv[:, :, 256:280], ACT.Sigmoid).then_inc(cmp_act, 1)
                act.wait_ge(cmp_pe_step, 4)
                act.activation(csq[:, :], ps[:, 2, 0:N_CMP], ACT.Square).then_inc(cmp_act, 1)
                a, b = lot_tiles(CMP_LOT)
                ada_tile_act(act, a, CMP_LOT, 5)
                act.wait_ge(cmp_pe_step, 5)
                act.activation(csq[:, :], ps[:, 4, 0:N_CMP], ACT.Sqrt, bias=eps[:, :], scale=1.0 / 64).then_inc(cmp_act, 1)
                for t in range(a + 1, b):
                    ada_tile_act(act, t, CMP_LOT, 5)
        ada_out.advance(1)

        scores_done, biased, max_done = signal("scores_done"), signal("biased"), signal("max_done")
        exp_done, probs_done, turned = signal("exp_done"), signal("probs_done"), signal("turned")
        turned_out, attended, attended_out = signal("turned_out"), signal("attended"), signal("attended_out")
        probs_link, output_hi = signal("probs_link"), signal("output_hi")
        with ExitStack() as own, nc.Block() as block:
            def ob(name, shape):
                return own.enter_context(nc.sbuf_tensor(name, shape, F32))

            W3 = 512 + N_CMP
            sc = ob("nsa_sc", [P, 2, W3])
            pr = ob("nsa_pr", [P, 3, W3])
            nm = ob("nsa_nm", [P, 3, 3])
            sums, coef = ob("nsa_sums", [P, 3, 3]), ob("nsa_coef", [P, 3, 3])
            pT = ob("nsa_pT", [P, 2, 512])
            cT = ob("nsa_cT", [N_CMP, 2, P])
            units = [(c, half, qb) for c in range(NSA_G) for half in range(2) for qb in range(TB)]
            N = len(units)
            dist = mk("dist").rearrange("p (b t) -> p b t", b=TB)
            cdist = mk("cdist").rearrange("p (b t) -> p b t", b=TB)
            cmask = mk("cmask").rearrange("p (b t) -> p b t", b=TB)

            def head_of(u):
                return units[u][0] + NSA_G * units[u][1]

            @block.tensor
            def _(pe):
                for i in range(N + 3):
                    if i < N:
                        c, half, qb = units[i]
                        r = slice(64 * half, 64 * half + 64)
                        q = nqk[r, c, qb * P:qb * P + P]
                        if i >= 2:
                            pe.wait_ge(max_done.h, max_done.at(i - 1))
                        pe.matmul(ps[:, i % 2, 0:256], q, nqk[r, 4, :], start=True, stop=True)
                        pe.matmul(ps[:, i % 2, 256:512], q, nqk[r, 5, :], start=True, stop=True)
                        if i >= 1:
                            pe.wait_ge(biased.h, biased.at(2 * i))
                        pe.matmul(ps[:, 2, 0:N_CMP], q, kcn[r, :], start=True, stop=True).then_inc(scores_done.h, 1)
                    if 0 <= i - 2 < N:
                        u = i - 2
                        pe.wait_ge(probs_done.h, probs_done.at(u + 1))
                        if u >= 2:
                            pe.wait_ge(turned_out.h, turned_out.at(u - 1))
                        for j in range(4):
                            pe.transpose(ps[:, 3 + u % 2, j * P:j * P + P], pr[:, u % 3, j * P:j * P + P], k("ident"))
                        if u >= 1:
                            pe.wait_ge(turned_out.h, turned_out.at(u))
                        pe.transpose(ps[0:N_CMP, 5, 0:P], pr[:, u % 3, 512:W3], k("ident")).then_inc(turned.h, 1)
                    if 0 <= i - 3 < N:
                        u = i - 3
                        _, half, _ = units[u]
                        vcol = slice(64 * half, 64 * half + 64)
                        wcol = slice(P + 64 * half, P + 64 * half + 64)
                        pe.wait_ge(turned_out.h, turned_out.at(u + 1))
                        if u >= 2:
                            pe.wait_ge(attended_out.h, attended_out.at(u - 1))
                        o = ps[64 * half:64 * half + 64, 6 + u % 2, 0:P]
                        pe.matmul(o, nv[:, 0, vcol], pT[:, u % 2, 0:P], start=True, stop=False)
                        pe.matmul(o, nv[:, 1, vcol], pT[:, u % 2, P:2 * P], start=False, stop=False)
                        pe.matmul(o, nv[:, 0, wcol], pT[:, u % 2, 2 * P:3 * P], start=False, stop=False)
                        pe.matmul(o, nv[:, 1, wcol], pT[:, u % 2, 3 * P:4 * P], start=False, stop=False)
                        pe.matmul(o, vcs[:, vcol], cT[:, u % 2, :], start=False, stop=True).then_inc(attended.h, 1)

            @block.vector
            def _(dve):
                for i in range(N + 4):
                    if i < N:
                        _, _, qb = units[i]
                        slope = float(2.0 ** (-8.0 * (head_of(i) + 1) / NSA_HEADS))
                        dve.wait_ge(scores_done.h, scores_done.at(i + 1))
                        if i >= 2:
                            dve.wait_ge(exp_done.h, exp_done.at(3 * (i - 1)))
                        dve.scalar_tensor_tensor(out=sc[:, i % 2, 0:512].rearrange("p (a t) -> p a t", a=2),
                                                 in0=dist[:, qb:qb + 1, :].broadcast_to([P, 2, T]), scalar=slope,
                                                 in1=ps[:, i % 2, :].rearrange("p (a t) -> p a t", a=2),
                                                 op0=ALU.mult, op1=ALU.add).then_inc(biased.h, 1)
                        dve.scalar_tensor_tensor(out=sc[:, i % 2, 512:W3], in0=cdist[:, qb, :], scalar=slope,
                                                 in1=ps[:, 2, 0:N_CMP], op0=ALU.mult, op1=ALU.add).then_inc(biased.h, 1)
                        dve.wait_ge(biased.h, biased.at(2 * i + 2))
                        dve.tensor_reduce(nm[:, i % 3, 0:2], sc[:, i % 2, 0:512].rearrange("p (a t) -> p a t", a=2), AX.X, ALU.max, negate=True)
                        dve.tensor_reduce(nm[:, i % 3, 2:3], sc[:, i % 2, 512:W3], AX.X, ALU.max, negate=True).then_inc(max_done.h, 1)
                    if 0 <= i - 1 < N:
                        u = i - 1
                        _, _, qb = units[u]
                        s3, h3 = u % 3, 3 * head_of(u)
                        dve.wait_ge(exp_done.h, exp_done.at(3 * u + 3))
                        dve.scalar_tensor_tensor(out=pr[:, s3, 512:W3], in0=pr[:, s3, 512:W3], scalar=1.0, in1=cmask[:, qb, :],
                                                 op0=ALU.mult, op1=ALU.mult, accum_out=sums[:, s3, 2:3]).then_inc(probs_link.h, 1)
                        dve.wait_ge(probs_link.h, probs_link.at(4 * u + 1))
                        dve.tensor_scalar(sums[:, s3, :], sums[:, s3, :], 1e-30, None, ALU.max).then_inc(probs_link.h, 1)
                        dve.wait_ge(probs_link.h, probs_link.at(4 * u + 2))
                        dve.reciprocal(coef[:, s3, :], sums[:, s3, :]).then_inc(probs_link.h, 1)
                        dve.wait_ge(probs_link.h, probs_link.at(4 * u + 3))
                        dve.tensor_tensor(coef[:, s3, 0:2], coef[:, s3, 0:2], gates[:, qb, h3 + 1:h3 + 3], ALU.mult)
                        dve.tensor_tensor(coef[:, s3, 2:3], coef[:, s3, 2:3], gates[:, qb, h3:h3 + 1], ALU.mult).then_inc(probs_link.h, 1)
                        dve.wait_ge(probs_link.h, probs_link.at(4 * u + 4))
                        dve.tensor_scalar(pr[:, s3, 0:256], pr[:, s3, 0:256], coef[:, s3, 0:1], None, ALU.mult)
                        dve.tensor_scalar(pr[:, s3, 256:512], pr[:, s3, 256:512], coef[:, s3, 1:2], None, ALU.mult)
                        dve.tensor_scalar(pr[:, s3, 512:W3], pr[:, s3, 512:W3], coef[:, s3, 2:3], None, ALU.mult).then_inc(probs_done.h, 1)
                    if 0 <= i - 4 < N:
                        u = i - 4
                        c, half, qb = units[u]
                        dve.wait_ge(attended.h, attended.at(u + 1))
                        r = slice(64 * half, 64 * half + 64)
                        dve.tensor_copy(mixT[r, 4 + c, qb * P:qb * P + P], ps[r, 6 + u % 2, 0:P]).then_inc(attended_out.h, 1)

            @block.scalar
            def _(act):
                for i in range(N + 2):
                    if i < N:
                        act.wait_ge(max_done.h, max_done.at(i + 1))
                        if i >= 3:
                            act.wait_ge(turned.h, turned.at(i - 2))
                        for j, (a, b) in enumerate(((0, 256), (256, 512), (512, W3))):
                            acc = {"accum_out": sums[:, i % 3, j:j + 1]} if j < 2 else {}
                            act.activation(pr[:, i % 3, a:b], sc[:, i % 2, a:b], ACT.Exp, bias=nm[:, i % 3, j:j + 1], **acc).then_inc(exp_done.h, 1)
                    if 0 <= i - 2 < N:
                        u = i - 2
                        act.wait_ge(turned.h, turned.at(u + 1))
                        if u >= 2:
                            act.wait_ge(attended.h, attended.at(u - 1))
                        act.activation(pT[:, u % 2, :], ps[:, 3 + u % 2, :], ACT.Copy)
                        act.activation(cT[:, u % 2, :], ps[0:N_CMP, 5, 0:P], ACT.Copy).then_inc(turned_out.h, 1)
        for s, n in ((scores_done, 1), (biased, 2), (max_done, 1), (exp_done, 3), (probs_link, 4), (probs_done, 1),
                     (turned, 1), (turned_out, 1), (attended, 1), (attended_out, 1)):
            s.advance(n * N)

        head_norm_stage(mixT[:, 4:8, :], 4, lambda c: v("nsa_out", c), lot=OUT_LOT)

        def add_to_tokens(n):
            return None, lambda dve, place: dve.tensor_tensor(hT[:, n, :], hT[:, n, :], place, ALU.add)

        x_space = ctx.enter_context(ExitStack())
        ffn_norm = Norm(hT, T, lambda c, s: v("ffn_norm", c), dst=x_space.enter_context(nc.sbuf_tensor("x_ffn", [P, C, T], F32, side="right")), early=True)
        product_stage(at_wout, aH, wide_tiles(C, T, add_to_tokens), before=Parted(mixT, aH, C), then=ffn_norm)
        mixer.close()

        peer = ctx.enter_context(ExitStack())

        def pb(name, shape, dt=F32):
            return peer.enter_context(nc.sbuf_tensor(name, shape, dt))

        ffn_norm.parts = xH = [pb(n, [P, C, T], F32R) for n in ("xT_hi", "xT_lo")]
        keyT, wT = pb("keyT", [P, 2, T]), pb("wT", [P, T])

        top_act, top_dve, sel_step = sem("top_act_step"), sem("top_dve_step"), sem("sel_step")
        with ExitStack() as own:
            def ob(name, shape, dt=F32):
                return own.enter_context(nc.sbuf_tensor(name, shape, dt))

            qT = ob("qT", [P, PK_SETS, T])
            product_stage(at_wq, xH, wide_tiles(PK_SETS, T, lambda j: copied(j, qT[:, j, :])),
                          before=ffn_norm)
            x_space.close()
            ks = ob("key_scores", [P, TB, PK_SETS, PK_KEYS])
            top_s = ob("top_s", [P, TB, PK_HEADS, 2, PK_TOP])
            top_i = ob("top_i", [P, TB, PK_HEADS, 2, PK_TOP], U32)
            top_f = ob("top_f", [P, PK_HEADS, 2, PK_TOP])
            cand = ob("cand", [P, PK_HEADS, PK_TOP, PK_TOP])
            best_s = ob("best_s", [P, PK_HEADS, PK_TOP])
            best_c = ob("best_c", [P, PK_HEADS, PK_TOP], U32)
            half_u = ob("half_u", [P, 2, PK_HK], U32)
            half_f = ob("half_f", [P, 2, PK_HK])
            pick = ob("pick", [P, PK_HK, PK_TOP])
            expert = ob("expert", [P, TB, 3, PK_HK])
            shifted = ob("shifted", [P, PK_HEADS, PK_TOP])
            total = ob("total", [P, PK_HEADS])
            with nc.Block() as block:
                @block.sync
                def _(sp):
                    loads(sp, at_experts + RAW)

                tile0, tile_end = lot_tiles(TOP_LOT)

                @block.tensor
                def _(pe):
                    per = PIECE // PK_KEYS
                    for g in range(4):
                        w = at_keys + 4 * g // per
                        piece_loaded(pe, w)
                        for b in range(TB):
                            for j in range(4 * g, 4 * g + 4):
                                mm = pe.matmul(ps[:, 4 * b + g, j % 4 * P:j % 4 * P + P], qT[:, j, b * P:b * P + P],
                                               raw[:, w % RAW, j % per * PK_KEYS:j % per * PK_KEYS + PK_KEYS], start=True, stop=True)
                            mm.then_inc(top_pe, 1)
                    pe.wait_ge(top_act, 8)
                    ada_lot_pe(pe, TOP_LOT, 4)
                    for b in range(TB):
                        pe.wait_ge(sel_step, 13 * b + 13)
                        for i in range(3):
                            mm = pe.transpose(ps[:, i, b * P:b * P + P], expert[:, b, i, :], k("ident"))
                    mm.then_inc(top_pe, 1)

                @block.scalar
                def _(act):
                    for n in range(8):
                        g, b = n // 2, n % 2
                        act.wait_ge(top_pe, n + 1)
                        act.activation(ks[:, b, 4 * g:4 * g + 4, :].rearrange("p j n -> p (j n)"), ps[:, 4 * b + g, :], ACT.Copy).then_inc(top_act, 1)
                    ends = (tile0 + 5, tile0 + 11, tile_end)
                    for b in range(TB):
                        for t in range(ends[b - 1] if b else tile0, ends[b]):
                            ada_tile_act(act, t, TOP_LOT, 4)
                        act.wait_ge(sel_step, 13 * b + 1)
                        act.activation(shifted[:, :, :], shifted[:, :, :], ACT.Exp).then_inc(top_act, 1)
                    for t in range(ends[TB - 1], tile_end):
                        ada_tile_act(act, t, TOP_LOT, 4)
                    act.wait_ge(top_pe, 9)
                    for i, dst in enumerate((keyT[:, 0, :], keyT[:, 1, :], wT[:, :])):
                        act.activation(dst, ps[:, i, 0:T], ACT.Copy)

                @block.vector
                def _(dve):
                    done = 0
                    for b in range(TB):
                        def best(n, values, s8, i8, load):
                            nonlocal done
                            for turn in range(2):
                                for j in range(n):
                                    if turn == 0:
                                        load(j)
                                    else:
                                        dve.wait_ge(top_dve, done - n + j + 1)
                                    dve.max(s8(j, turn), values(j)).then_inc(top_dve, 1)
                                done += n
                                for j in range(n):
                                    dve.wait_ge(top_dve, done - n + j + 1)
                                    dve.max_index(i8(j, turn), s8(j, turn), values(j)).then_inc(top_dve, 1)
                                done += n
                                if turn == 0:
                                    for j in range(n):
                                        dve.wait_ge(top_dve, done - n + j + 1)
                                        dve.match_replace(values(j), s8(j, 0), values(j), LOWEST).then_inc(top_dve, 1)
                                    done += n

                        def scored(j):
                            dve.wait_ge(top_act, 2 * (j // 4) + b + 1)

                        best(PK_SETS, lambda j: ks[:, b, j, :], lambda j, t: top_s[:, b, j // 2, j % 2, 8 * t:8 * t + 8],
                             lambda j, t: top_i[:, b, j // 2, j % 2, 8 * t:8 * t + 8], scored)
                        dve.wait_ge(top_dve, done)
                        dve.tensor_tensor(cand[:, :, :, :], top_s[:, b, :, 0, :].unsqueeze(3).broadcast_to([P, PK_HEADS, PK_TOP, PK_TOP]),
                                          top_s[:, b, :, 1, :].unsqueeze(2).broadcast_to([P, PK_HEADS, PK_TOP, PK_TOP]), ALU.add).then_inc(top_dve, 1)
                        done += 1
                        dve.wait_ge(top_dve, done)
                        best(PK_HEADS, lambda h: cand[:, h, :, :].rearrange("p a b -> p (a b)"), lambda h, t: best_s[:, h, 8 * t:8 * t + 8],
                             lambda h, t: best_c[:, h, 8 * t:8 * t + 8], lambda h: None)
                        dve.wait_ge(top_dve, done)
                        s0 = 13 * b
                        dve.tensor_tensor(shifted[:, :, :], best_s[:, :, :], best_s[:, :, 0:1].broadcast_to([P, PK_HEADS, PK_TOP]), ALU.subtract).then_inc(sel_step, 1)
                        flat_c = best_c[:, :, :].rearrange("p h k -> p (h k)")
                        dve.tensor_scalar(half_u[:, 0, :], flat_c, 4, None, ALU.logical_shift_right).then_inc(sel_step, 1)
                        dve.tensor_scalar(half_u[:, 1, :], flat_c, PK_TOP - 1, None, ALU.bitwise_and).then_inc(sel_step, 1)
                        dve.tensor_copy(top_f[:, :, :, :].rearrange("p h c k -> p (h c k)"), top_i[:, b, :, :, :].rearrange("p h c k -> p (h c k)")).then_inc(sel_step, 1)
                        dve.wait_ge(sel_step, s0 + 3)
                        dve.tensor_copy(half_f[:, :, :], half_u[:, :, :]).then_inc(sel_step, 1)
                        for i in range(2):
                            dve.wait_ge(sel_step, s0 + 5 + 3 * i)
                            dve.tensor_tensor(pick[:, :, :], half_f[:, i, :].unsqueeze(2).broadcast_to([P, PK_HK, PK_TOP]),
                                              k("iota", 0, PK_TOP).unsqueeze(1).broadcast_to([P, PK_HK, PK_TOP]), ALU.is_equal).then_inc(sel_step, 1)
                            dve.wait_ge(sel_step, s0 + 6 + 3 * i)
                            p4 = pick[:, :, :].rearrange("p (h k) j -> p h k j", h=PK_HEADS)
                            dve.tensor_tensor(p4, p4, top_f[:, :, i, :].unsqueeze(2).broadcast_to([P, PK_HEADS, PK_TOP, PK_TOP]), ALU.mult).then_inc(sel_step, 1)
                            dve.wait_ge(sel_step, s0 + 7 + 3 * i)
                            dve.tensor_reduce(expert[:, b, i, :], pick[:, :, :], AX.X, ALU.add).then_inc(sel_step, 1)
                        dve.wait_ge(top_act, 9 + b)
                        dve.tensor_reduce(total[:, :], shifted[:, :, :], AX.X, ALU.add).then_inc(sel_step, 1)
                        dve.wait_ge(sel_step, s0 + 12)
                        dve.reciprocal(total[:, :], total[:, :]).then_inc(top_dve, 1)
                        done += 1
                        dve.wait_ge(top_dve, done)
                        dve.tensor_tensor(expert[:, b, 2, :].rearrange("p (h k) -> p h k", h=PK_HEADS), shifted[:, :, :],
                                          total[:, :].unsqueeze(2).broadcast_to([P, PK_HEADS, PK_TOP]), ALU.mult).then_inc(sel_step, 1)
                        if b == 0:
                            dve.wait_ge(sel_step, 13)

        ada_out.advance(1)
        row_space.close()
        route = pb("route", [P, T, PK_KEYS])
        BATCH, SLOTS = 2, 4
        hot, weighted_hot, route_mm, route_out = sem("hot"), sem("weighted_hot"), sem("route_mm"), sem("route_out")
        with ExitStack() as own, nc.Block() as block:
            ohs = own.enter_context(nc.sbuf_tensor("one_hots", [P, SLOTS, 2, BATCH, PK_KEYS], F32))
            BATCHES = T // BATCH
            ROUNDS = BATCHES // SLOTS

            @block.vector
            def _(dve):
                def turn(r, steps, first=False):
                    for s in range(steps):
                        if not first:
                            dve.wait_ge(route_mm, SLOTS * r + (s - SLOTS + 1))
                        dve.tensor_tensor(ohs[:, s, :, :, :], k("iota").unsqueeze(1).unsqueeze(1).broadcast_to([P, 2, BATCH, PK_KEYS]),
                                          keyT[:, :, bass.ds((SLOTS * r + s) * BATCH, BATCH)].unsqueeze(3).broadcast_to([P, 2, BATCH, PK_KEYS]),
                                          ALU.is_equal).then_inc(hot, 1)
                turn(0, SLOTS, True)
                with dve.Fori(1, ROUNDS) as r:
                    turn(r, SLOTS)
                turn(ROUNDS, BATCHES - ROUNDS * SLOTS)

            @block.gpsimd
            def _(pool):
                def turn(r, steps):
                    for s in range(steps):
                        pool.wait_ge(hot, SLOTS * r + (s + 1))
                        pool.tensor_tensor(ohs[:, s, 1, :, :], ohs[:, s, 1, :, :],
                                           wT[:, bass.ds((SLOTS * r + s) * BATCH, BATCH)].unsqueeze(2).broadcast_to([P, BATCH, PK_KEYS]),
                                           ALU.mult).then_inc(weighted_hot, 1)
                with pool.Fori(0, ROUNDS) as r:
                    turn(r, SLOTS)
                turn(ROUNDS, BATCHES - ROUNDS * SLOTS)

            @block.tensor
            def _(pe):
                def turn(r, steps, first=False):
                    for s in range(steps):
                        pe.wait_ge(weighted_hot, SLOTS * r + (s + 1))
                        if not first:
                            pe.wait_ge(route_out, SLOTS * r + (s - SLOTS + 1))
                        for q in range(BATCH):
                            mm = pe.matmul(ps[:, s, q * P:q * P + P], ohs[:, s, 0, q, :], ohs[:, s, 1, q, :], start=True, stop=True)
                        mm.then_inc(route_mm, 1)
                turn(0, SLOTS, True)
                with pe.Fori(1, ROUNDS) as r:
                    turn(r, SLOTS)
                turn(ROUNDS, BATCHES - ROUNDS * SLOTS)

            @block.scalar
            def _(act):
                def turn(r, steps):
                    for s in range(steps):
                        act.wait_ge(route_mm, SLOTS * r + (s + 1))
                        act.activation(route[:, bass.ds((SLOTS * r + s) * BATCH, BATCH), :].rearrange("p t n -> p (t n)"), ps[:, s, 0:BATCH * P],
                                       ACT.Copy).then_inc(route_out, 1)
                with act.Fori(0, ROUNDS) as r:
                    turn(r, SLOTS)
                turn(ROUNDS, BATCHES - ROUNDS * SLOTS)

        GROUPS = PK_KEYS
        LOOP = 18
        assert 2 * LOOP % RAW == 0 and 2 * LOOP % SPLIT == 0 and LOOP % 3 == 0
        TURNS = (GROUPS - 2) // LOOP
        LAST = 2 * GROUPS - 1
        after_experts = at_experts + LAST + 1
        n0 = pieces[at_experts][3]
        gelu_done, weighted, weighted_hi, weighted_lo = sem("gelu_done"), sem("weighted"), sem("weighted_hi"), sem("weighted_lo")
        with ExitStack() as own, nc.Block() as block:
            ga = own.enter_context(nc.sbuf_tensor("ga", [P, 2, T], F32))
            gh = own.enter_context(nc.sbuf_tensor("gh", [P, 2, T], F32R))
            gl = own.enter_context(nc.sbuf_tensor("gl", [P, 2, T], F32R))

            @block.sync
            def _(sp):
                first = at_experts + 2 * LOOP + RAW
                loads(sp, first)
                turns = (LAST + 1 - 2 * LOOP - RAW) // (2 * LOOP)
                with sp.Fori(0, turns) as r:
                    for e in range(2 * LOOP + RAW, 4 * LOOP + RAW):
                        g = at_experts + e
                        sp.wait_ge(lo_done, 2 * LOOP * r + (n0 + e - RAW + 1))
                        sp.dma_start(raw[:, g % RAW, :], dr["experts_t"][bass.ds(2 * LOOP * r + e, 1)].rearrange("a p n -> p (a n)")).then_inc(raw_loaded[g % RAW], 16)
                next_load[0] = first + 2 * LOOP * turns
                loads(sp, after_experts + len(ahead(after_experts)) + RAW)

            def hi(act, r, e):
                g, n = at_experts + e, n0 + e
                act.wait_ge(raw_loaded[g % RAW], 16 * (g // RAW + 1) + 16 * (2 * LOOP // RAW) * r)
                act.wait_ge(piece_used, 2 * LOOP * r + (n - SPLIT + 1))
                act.activation(whi[:, n % SPLIT, :], raw[:, g % RAW, :], ACT.Copy).then_inc(hi_done, 1)

            def lo(dve, r, e):
                g, n = at_experts + e, n0 + e
                dve.wait_ge(hi_done, 2 * LOOP * r + (n + 1))
                dve.tensor_tensor(wlo[:, n % SPLIT, :], raw[:, g % RAW, :], whi[:, n % SPLIT, :].bitcast(F32), ALU.subtract).then_inc(lo_done, 1)

            @block.tensor
            def _(pe):
                def keys(r, e, i, early):
                    n = n0 + e
                    pe.wait_ge(lo_done, 2 * LOOP * r + (n + 1))
                    if not early:
                        pe.wait_ge(gelu_done, LOOP * r + (i - 2))
                    for c in range(C):
                        mm = products(pe, ps[:, 4 + i % 3, 0:T], [w[:, n % SPLIT, c * P:c * P + P] for w in (whi, wlo)],
                                      [y[:, c, :] for y in xH], c == 0, c == C - 1)
                    mm.then_inc(piece_used, 1)

                def values(r, e, i, start=False, stop=False):
                    n = n0 + e
                    pe.wait_ge(lo_done, 2 * LOOP * r + (n + 1))
                    pe.wait_ge(weighted_lo, LOOP * r + (i + 1))
                    for c in range(C):
                        place = ps[:, c // 2, c % 2 * T:c % 2 * T + T]
                        w = [w[:, n % SPLIT, c * P:c * P + P] for w in (whi, wlo)]
                        pe.matmul(place, w[0], gh[:, i % 2, :], start=(start and c % 2 == 0), stop=False, skip_group_check=True)
                        pe.matmul(place, w[0], gl[:, i % 2, :], start=False, stop=False, skip_group_check=True)
                        mm = pe.matmul(place, w[1], gh[:, i % 2, :], start=False, stop=stop, skip_group_check=True)
                    mm.then_inc(piece_used, 1)

                def turn(r, first):
                    for i in range(LOOP):
                        keys(r, 2 * i + 1, i + 1, first and i < 2)
                        values(r, 2 * i + 2, i, start=(first and i == 0))
                keys(0, 0, 0, True)
                turn(0, True)
                with pe.Fori(1, TURNS) as r:
                    turn(r, False)
                for i in range(GROUPS - TURNS * LOOP):
                    last = i == GROUPS - TURNS * LOOP - 1
                    if not last:
                        keys(TURNS, 2 * i + 1, i + 1, False)
                    values(TURNS, 2 * i + 2 - last, i, stop=last)

            @block.scalar
            def _(act):
                def group(r, i, early=False, tail=2):
                    act.wait_ge(piece_used, 2 * LOOP * r + (n0 + max(2 * i - 1, 0) + 1))
                    if not early:
                        act.wait_ge(weighted_lo, LOOP * r + (i - 1))
                    act.activation(ga[:, i % 2, :], ps[:, 4 + i % 3, 0:T], ACT.Gelu_apprx_tanh).then_inc(gelu_done, 1)
                    if tail >= 1:
                        hi(act, r, 2 * i + 2)
                    act.wait_ge(weighted, LOOP * r + (i + 1))
                    act.activation(gh[:, i % 2, :], ga[:, i % 2, :], ACT.Copy).then_inc(weighted_hi, 1)
                    if tail >= 2:
                        hi(act, r, 2 * i + 3)
                for e in range(2):
                    if at_experts + e >= split_upto[0]:
                        split_hi(act, at_experts + e)
                for i in range(LOOP):
                    group(0, i, early=i < 2)
                with act.Fori(1, TURNS) as r:
                    for i in range(LOOP):
                        group(r, i)
                rest = GROUPS - TURNS * LOOP
                for i in range(rest):
                    group(TURNS, i, tail=min(2, 2 * (rest - 1 - i)))
                for g in ahead(after_experts):
                    split_hi(act, g)

            @block.vector
            def _(dve):
                def group(r, i, tail=2):
                    dve.wait_ge(gelu_done, LOOP * r + (i + 1))
                    dve.tensor_tensor(ga[:, i % 2, :], ga[:, i % 2, :],
                                      route[:, :, bass.ds(LOOP * r + i, 1)].rearrange("p t a -> p (t a)"), ALU.mult).then_inc(weighted, 1)
                    if tail >= 1:
                        lo(dve, r, 2 * i + 2)
                    dve.wait_ge(weighted_hi, LOOP * r + (i + 1))
                    dve.tensor_tensor(gl[:, i % 2, :], ga[:, i % 2, :], gh[:, i % 2, :].bitcast(F32), ALU.subtract).then_inc(weighted_lo, 1)
                    if tail >= 2:
                        lo(dve, r, 2 * i + 3)
                for e in range(2):
                    if at_experts + e >= split_upto[0]:
                        split_lo(dve, at_experts + e)
                for i in range(LOOP):
                    group(0, i)
                with dve.Fori(1, TURNS) as r:
                    for i in range(LOOP):
                        group(r, i)
                rest = GROUPS - TURNS * LOOP
                for i in range(rest):
                    group(TURNS, i, tail=min(2, 2 * (rest - 1 - i)))
                for g in ahead(after_experts):
                    split_lo(dve, g)
                dve.wait_ge(piece_used, n0 + LAST + 1)
                dve.tensor_tensor(hT[:, :, :].rearrange("p c t -> p (c t)"), hT[:, :, :].rearrange("p c t -> p (c t)"),
                                  ps[:, 0:4, :].rearrange("p b n -> p (b n)"), ALU.add)
        split_upto[0] = after_experts + len(ahead(after_experts))
        peer.close()

        h2 = ctx.enter_context(nc.sbuf_tensor("h2", [P, C, TT], F32))
        x2H = [ctx.enter_context(nc.sbuf_tensor(n, [P, C, TT], F32R)) for n in ("x2_hi", "x2_lo")]
        x2 = ctx.enter_context(nc.sbuf_tensor("x2", [P, C, TT], F32))
        ctx_loaded, mod_step = sem("ctx_loaded"), sem("mod_step")

        def mix_norm(i):
            return Norm(h2, TT, lambda c, s: gs1[:, i, c, s:s + 1], lambda c, s: mod[:, i, c, s:s + 1], segs=2, parts=x2H, dst=x2,
                        logs=True, early=True)

        def ffn_norm_of(i, w):
            return Norm(h2[:, :, 0:w], w, lambda c, s: gs2[:, i, c, s:s + 1], lambda c, s: mod[:, i, 3 * C + c, s:s + 1],
                        segs=w // T, parts=[y[:, :, 0:w] for y in x2H], dst=x2[:, :, 0:w], logs=True, early=True)

        def finish_modulations(dve):
            every = mod[:, :, :, :].rearrange("p l j s -> p (l j) s")
            dve.tensor_tensor(every, every, v("ada_b", 0, LAYERS * N_MOD * C).unsqueeze(2).broadcast_to([P, LAYERS * N_MOD * C, 2]), ALU.add).then_inc(mod_step, 1)
            dve.wait_ge(mod_step, 1)
            for i in range(LAYERS):
                for g, name, at in ((gs1, "mix2", C), (gs2, "ffn2", 4 * C)):
                    dve.scalar_tensor_tensor(out=g[:, i, :, :], in0=mod[:, i, at:at + C, :], scalar=1.0,
                                             in1=v(name, i * C, C).unsqueeze(2).broadcast_to([P, C, 2]), op0=ALU.add, op1=ALU.mult)

        with ExitStack() as own:
            def ob(name, shape, dt=F32):
                return own.enter_context(nc.sbuf_tensor(name, shape, dt))

            ada_row.append(own.enter_context(nc.sbuf_tensor("ada_row2", [2, 2, 512], F32, side="right")))
            xgH = [ob(n, [P, C, T], F32R) for n in ("xg_hi", "xg_lo")]
            pT_in, pH = ob("pT_in", [P, 2, T]), [ob(n, [P, 2, T], F32R) for n in ("pT_hi", "pT_lo")]
            emb, sg = ob("emb", [P, C, T]), ob("sg", [P, C, T])
            p_loaded, ple_step = sem("p_loaded"), sem("ple_step")

            def load_streams(sp):
                sp.dma_start(pT_in[:, :, :], dr["p_t"]).then_inc(p_loaded, 16)
                sp.dma_start(h2[:, :, T:TT], dr["ctx_t"]).then_inc(ctx_loaded, 16)
                sp.wait_ge(ctx_loaded, 16)

            class Embedded(Parted):
                def act(self, act, before):
                    act.wait_ge(p_loaded, 16)
                    Parted.act(self, act, before)
            product_stage(at_plep, pH, [(1, 2, 512, [("wide", j * P, slice(0, T), *copied(j, emb[:, 4 * t + j, :])) for j in range(4)])
                                        for t in range(2)], before=Embedded(pT_in, pH, 2), lot=PLE_LOT, sync=load_streams)

            def gated(n):
                def add(dve, place):
                    dve.tensor_tensor(sg[:, n, :], sg[:, n, :], emb[:, n, :], ALU.mult).then_inc(ple_step, 1)
                    dve.wait_ge(ple_step, n + 1)
                    return dve.tensor_tensor(h2[:, n, 0:T], hT[:, n, :], sg[:, n, :], ALU.add)
                return (lambda act, place: act.activation(sg[:, n, :], place, ACT.Sigmoid)), add
            mix0_norm = mix_norm(0)
            product_stage(at_plew, xgH, wide_tiles(C, T, gated), before=Norm(hT, T, lambda c, s: v("ple_norm", c), parts=xgH, logs=True),
                          then=mix0_norm, last=finish_modulations)
        tokens.close()

        def attention(units, name, bias_loaded=None):
            N, N_BIAS = len(units), sum(u[2] is not None for u in units)
            WIDE = max(u[1].shape[-1] for u in units)
            DEEP, BANKS = 5, (0, 1, 6, 7)
            with ExitStack() as own, nc.Block() as block:
                pr = own.enter_context(nc.sbuf_tensor(name + "_pr", [P, DEEP, WIDE], F32))
                nm = own.enter_context(nc.sbuf_tensor(name + "_nm", [P, DEEP], F32))
                sums = own.enter_context(nc.sbuf_tensor(name + "_sums", [P, DEEP], F32))
                inv = own.enter_context(nc.sbuf_tensor(name + "_inv", [P, DEEP], F32))
                pT = own.enter_context(nc.sbuf_tensor(name + "_pT", [P, 2, WIDE], F32))

                def nk(u):
                    return units[u][1].shape[-1]

                def scores(i):
                    return ps[:, BANKS[i % len(BANKS)], 0:nk(i)]

                @block.tensor
                def _(pe):
                    for i in range(N + 5):
                        if i < N:
                            q, keys, _, _, _, _ = units[i]
                            if i >= len(BANKS):
                                pe.wait_ge(exp_done.h, exp_done.at(i - len(BANKS) + 1))
                            pe.matmul(scores(i), q, keys, start=True, stop=True).then_inc(scores_done.h, 1)
                        if 0 <= i - 3 < N:
                            u = i - 3
                            pe.wait_ge(probs_done.h, probs_done.at(u + 1))
                            if u >= 2:
                                pe.wait_ge(turned_out.h, turned_out.at(u - 1))
                            for j in range(nk(u) // P):
                                mm = pe.transpose(ps[:, 2 + u % 2, j * P:j * P + P], pr[:, u % DEEP, j * P:j * P + P], k("ident"))
                            mm.then_inc(turned.h, 1)
                        if 0 <= i - 5 < N:
                            u = i - 5
                            _, _, _, values, half, _ = units[u]
                            pe.wait_ge(turned_out.h, turned_out.at(u + 1))
                            if u >= 2:
                                pe.wait_ge(attended_out.h, attended_out.at(u - 1))
                            for j in range(nk(u) // P):
                                mm = pe.matmul(ps[64 * half:64 * half + 64, 4 + u % 2, 0:P], values[j], pT[:, u % 2, j * P:j * P + P],
                                               start=(j == 0), stop=(j == nk(u) // P - 1))
                            mm.then_inc(attended.h, 1)

                @block.vector
                def _(dve):
                    if bias_loaded:
                        dve.wait_ge(bias_loaded, 16)
                    for i in range(N + 6):
                        if i < N:
                            _, _, bias, _, _, _ = units[i]
                            dve.wait_ge(scores_done.h, scores_done.at(i + 1))
                            if i >= DEEP:
                                dve.wait_ge(exp_done.h, exp_done.at(i - DEEP + 1))
                            if bias is not None:
                                dve.tensor_tensor(scores(i)[:, 0:T], scores(i)[:, 0:T], bias, ALU.add).then_inc(biased.h, 1)
                                dve.wait_ge(biased.h, biased.at(i + 1))
                            dve.tensor_reduce(nm[:, i % DEEP:i % DEEP + 1], scores(i), AX.X, ALU.max, negate=True).then_inc(max_done.h, 1)
                        if 0 <= i - 2 < N:
                            u, at = i - 2, (i - 2) % DEEP
                            dve.wait_ge(exp_done.h, exp_done.at(u + 1))
                            dve.reciprocal(inv[:, at:at + 1], sums[:, at:at + 1]).then_inc(probs_link.h, 1)
                            dve.wait_ge(probs_link.h, probs_link.at(u + 1))
                            dve.tensor_scalar(pr[:, at, 0:nk(u)], pr[:, at, 0:nk(u)], inv[:, at:at + 1], None, ALU.mult).then_inc(probs_done.h, 1)
                        if 0 <= i - 6 < N:
                            u = i - 6
                            _, _, _, _, half, place = units[u]
                            dve.wait_ge(output_hi.h, output_hi.at(u + 1))
                            dve.tensor_tensor(place[1], ps[64 * half:64 * half + 64, 4 + u % 2, 0:P], place[0].bitcast(F32), ALU.subtract).then_inc(attended_out.h, 1)

                @block.scalar
                def _(act):
                    for i in range(N + 6):
                        if 0 <= i - 6 < N:
                            u = i - 6
                            _, _, _, _, half, place = units[u]
                            act.wait_ge(attended.h, attended.at(u + 1))
                            act.activation(place[0], ps[64 * half:64 * half + 64, 4 + u % 2, 0:P], ACT.Copy).then_inc(output_hi.h, 1)
                        if i < N:
                            act.wait_ge(max_done.h, max_done.at(i + 1))
                            if i >= DEEP:
                                act.wait_ge(turned.h, turned.at(i - DEEP + 1))
                            act.activation(pr[:, i % DEEP, 0:nk(i)], scores(i), ACT.Exp, bias=nm[:, i % DEEP:i % DEEP + 1],
                                           accum_out=sums[:, i % DEEP:i % DEEP + 1]).then_inc(exp_done.h, 1)
                        if 0 <= i - 4 < N:
                            u = i - 4
                            act.wait_ge(turned.h, turned.at(u + 1))
                            if u >= 2:
                                act.wait_ge(attended.h, attended.at(u - 1))
                            act.activation(pT[:, u % 2, 0:nk(u)], ps[:, 2 + u % 2, 0:nk(u)], ACT.Copy).then_inc(turned_out.h, 1)
            for s in (scores_done, max_done, exp_done, probs_link, probs_done, turned, turned_out, attended, output_hi, attended_out):
                s.advance(N)
            biased.advance(N_BIAS)

        def add_gated(i, n, at, w):
            def go(dve, place):
                for s in range(w // T):
                    o = h2[:, n, s * T:s * T + T]
                    ins = dve.scalar_tensor_tensor(out=o, in0=place[:, s * T:s * T + T], scalar=mod[:, i, at + n, s:s + 1], in1=o, op0=ALU.mult, op1=ALU.add)
                return ins
            return None, go

        def feed_forward(i, w, norm, then):
            parts = [y[:, :, 0:w] for y in x2H]
            with ExitStack() as own:
                hid = [own.enter_context(nc.sbuf_tensor(f"ffn_{n}{i}", [P, FC, w], F32R)) for n in ("hi", "lo")]
                tmp = own.enter_context(nc.sbuf_tensor(f"ffn_tmp{i}", [P, 4, w], F32))

                def activated(t, j):
                    f = 2 * t + j
                    factor = ps[:, 4 * (t % 2) + 2 + j, 0:w]
                    return (lambda act, place: act.activation(tmp[:, f % 4, :], place, ACT.Silu),
                            lambda dve, place: dve.tensor_tensor(tmp[:, f % 4, :], factor, tmp[:, f % 4, :], ALU.mult))

                def parted(t, j):
                    f = 2 * t + j

                    def high(act, place):
                        act.wait_ge(dve_evacuated.h, dve_evacuated.at(4 * t + j + 1))
                        return act.activation(hid[0][:, f, :], tmp[:, f % 4, :], ACT.Copy)
                    return high, lambda dve, place: dve.tensor_tensor(hid[1][:, f, :], tmp[:, f % 4, :], hid[0][:, f, :].bitcast(F32), ALU.subtract)

                product_stage(at_f1[i], parts, [(4, 2, 512, [("wide", j * P, slice(0, w), *(activated(t, j) if j < 2 else parted(t, j - 2)))
                                                             for j in range(4)]) for t in range(FC // 2)], before=norm)

                with nc.Block() as block:
                    g0 = at_f2[i]
                    after = ahead(g0 + FC)

                    @block.sync
                    def _(sp):
                        loads(sp, g0 + FC + RAW)

                    @block.tensor
                    def _(pe):
                        for f in range(FC):
                            n_ = pieces[g0 + f][3]
                            pe.wait_ge(lo_done, n_ + 1)
                            for n in range(C):
                                mm = products(pe, ps[:, n, 0:w], [y[:, n_ % SPLIT, n * P:n * P + P] for y in (whi, wlo)],
                                              [y[:, f, :] for y in hid], f == 0, f == FC - 1)
                            mm.then_inc(piece_used, 1)
                        then.sums(pe)

                    @block.scalar
                    def _(act):
                        for g in range(max(g0, split_upto[0]), g0 + FC + len(after)):
                            split_hi(act, g)
                        then.squares(act, 0, C)

                    @block.vector
                    def _(dve):
                        for g in range(max(g0, split_upto[0]), g0 + FC + len(after)):
                            split_lo(dve, g)
                        dve.wait_ge(piece_used, pieces[g0 + FC - 1][3] + 1)
                        for n in range(C):
                            add_gated(i, n, 5 * C, w)[1](dve, ps[:, n, 0:w]).then_inc(dve_evacuated.h, 1)
                dve_evacuated.advance(C)
                then.end_early()
                split_upto[0] = g0 + FC + len(after)

        with ExitStack() as own:
            def ob(name, shape):
                return own.enter_context(nc.sbuf_tensor(name, shape, F32))

            qT, kT, vt = ob("na_q", [P, C, TT]), ob("na_k", [P, C, TT]), ob("na_v", [P, TT // P, D])
            bias = ob("na_bias", [P, HEADS, TB, T])
            oT = x2H
            bias_loaded = sem("bias_loaded")
            product_stage(at_qkv[0], x2H,
                          wide_tiles(C, TT, lambda n: copied(n, qT[:, n, :], DH ** -0.5)) + wide_tiles(C, TT, lambda n: copied(n, kT[:, n, :]))
                          + [(4, 2, 512, [("tall", slice(0, 512), b * P, *copied(b, vt[:, b, n * 512:n * 512 + 512])) for b in range(TT // P)])
                             for n in range(2)], before=mix0_norm,
                          sync=lambda sp: sp.dma_start(bias[:, :, :, :], dr["na_bias_t"]).then_inc(bias_loaded, 16))
            units, ctx_units = [], []
            for h in range(HEADS):
                half, c = h % 2, h // 2
                r = slice(64 * half, 64 * half + 64)
                for qb in range(TB):
                    q0 = qb * P
                    units.append((qT[r, c, q0:q0 + P], kT[r, c, :], bias[:, h, qb, :], [vt[:, j, h * DH:h * DH + DH] for j in range(4)],
                                  half, [y[r, c, q0:q0 + P] for y in oT]))
                    q0 += T
                    ctx_units.append((qT[r, c, q0:q0 + P], kT[r, c, T:TT], None, [vt[:, j, h * DH:h * DH + DH] for j in (2, 3)],
                                      half, [y[r, c, q0:q0 + P] for y in oT]))
            attention(units + ctx_units, "na", bias_loaded)
            ffn0_norm = ffn_norm_of(0, TT)
            product_stage(at_o[0], oT, wide_tiles(C, TT, lambda n: add_gated(0, n, 2 * C, TT)), then=ffn0_norm)
        mix1_norm = mix_norm(1)
        feed_forward(0, TT, ffn0_norm, mix1_norm)

        with ExitStack() as own:
            def ob(name, shape):
                return own.enter_context(nc.sbuf_tensor(name, shape, F32))

            qT, kT, vt = ob("gqa_q", [P, C, T]), ob("gqa_k", [P, 2, TT]), ob("gqa_v", [P, TT // P, GQA_KV * DH])
            rope = ob("rope", [P, 2, T])
            rope_loaded, swap_done, rope_step = sem("rope_loaded"), sem("swap_done"), sem("rope_step")
            product_stage(at_qkv[1], x2H, wide_tiles(C, T, lambda n: copied(n, qT[:, n, :])) + [
                (2, 4, 256, [("wide", n * P, slice(0, TT), *copied(n, kT[:, n, :])) for n in range(2)]),
                (2, 4, 256, [("tall", slice(0, 256), b * P, *copied(b, vt[:, b, :])) for b in range(TT // P)])], before=mix1_norm,
                          sync=lambda sp: sp.dma_start(rope[:, :, :].rearrange("p a t -> p (a t)"), dr["rope_consts"]).then_inc(rope_loaded, 16))
            groups = [(kT[:, c, :], kT[:, c:c + 1, 0:T], "gqa_k") for c in range(2)]
            groups += [(qT[:, c:c + 2, :].rearrange("p c t -> p (c t)"), qT[:, c:c + 2, :], "gqa_q") for c in range(0, C, 2)]
            NG = len(groups)
            with ExitStack() as inner, nc.Block() as block:
                def ib(name, n):
                    return inner.enter_context(nc.sbuf_tensor(name, [P, n, 512], F32))

                sq, logs, rstd, rot = ib("gqa_squares", 3), ib("gqa_logs", 2), ib("gqa_rstd", 2), ib("rot", 2)
                gq_square, gq_sum, gq_log, gq_rstd, gq_normed = (sem(n) for n in ("gq_square", "gq_sum", "gq_log", "gq_rstd", "gq_normed"))

                def tokens_of(n):
                    return groups[n][1].shape[1] * T

                @block.scalar
                def _(act):
                    for i in range(NG + 1):
                        if i < NG:
                            if i >= 3:
                                act.wait_ge(gq_sum, i - 2)
                            act.activation(sq[:, i % 3, :], groups[i][0], ACT.Square).then_inc(gq_square, 1)
                        if i >= 1:
                            n = i - 1
                            act.wait_ge(gq_sum, n + 1)
                            act.activation(logs[:, n % 2, :], ps[:, n % 2, :], ACT.Ln, bias=eps[:, :], scale=1.0 / DH).then_inc(gq_log, 1)
                            if n >= 2:
                                act.wait_ge(gq_normed, n - 1)
                            act.wait_ge(gq_log, n + 1)
                            act.activation(rstd[:, n % 2, :], logs[:, n % 2, :], ACT.Exp, scale=-0.5).then_inc(gq_rstd, 1)

                @block.tensor
                def _(pe):
                    for i in range(NG + 2):
                        if i < NG:
                            pe.wait_ge(gq_square, i + 1)
                            if i >= 2:
                                pe.wait_ge(gq_log, i - 1)
                            pe.matmul(ps[:, i % 2, :], k("ones64"), sq[:, i % 3, :], start=True, stop=True).then_inc(gq_sum, 1)
                        if i >= 2:
                            n = i - 2
                            pe.wait_ge(gq_normed, n + 1)
                            if n >= 2:
                                pe.wait_ge(rope_step, 2 * (n - 2) + 1)
                            pe.matmul(ps[:, 2 + n % 2, 0:tokens_of(n)], k("swap"), groups[n][1], start=True, stop=True).then_inc(swap_done, 1)

                @block.vector
                def _(dve):
                    dve.wait_ge(rope_loaded, 16)
                    for i in range(NG + 1):
                        if i < NG:
                            x, _, gain = groups[i]
                            dve.wait_ge(gq_rstd, i + 1)
                            dve.scalar_tensor_tensor(out=x, in0=x, scalar=v(gain), in1=rstd[:, i % 2, :], op0=ALU.mult, op1=ALU.mult).then_inc(gq_normed, 1)
                        if i >= 1:
                            n = i - 1
                            x, w = groups[n][1], groups[n][1].shape[1]
                            cos, sin = (rope[:, j:j + 1, :].broadcast_to([P, w, T]) for j in range(2))
                            turned_ = rot[:, n % 2, 0:w * T].rearrange("p (c t) -> p c t", t=T)
                            dve.wait_ge(swap_done, n + 1)
                            dve.tensor_tensor(turned_, ps[:, 2 + n % 2, 0:w * T].rearrange("p (c t) -> p c t", t=T), sin, ALU.mult).then_inc(rope_step, 1)
                            dve.tensor_tensor(x, x, cos, ALU.mult).then_inc(rope_step, 1)
                            dve.wait_ge(rope_step, 2 * n + 2)
                            dve.tensor_tensor(x, x, turned_, ALU.add)
            units = []
            oT = x2H
            for c in range(C):
                for half in range(2):
                    r, kv = slice(64 * half, 64 * half + 64), 2 * (c // 4) + half
                    for qb in range(TB):
                        q0 = qb * P
                        units.append((qT[r, c, q0:q0 + P], kT[r, c // 4, :], None, [vt[:, j, kv * DH:kv * DH + DH] for j in range(4)],
                                      half, [y[r, c, q0:q0 + P] for y in oT]))
            attention(units, "gqa")
            ffn1_norm = ffn_norm_of(1, T)
            product_stage(at_o[1], oT, wide_tiles(C, T, lambda n: add_gated(1, n, 2 * C, T)), then=ffn1_norm)
        final_norm = Norm(h2[:, :, 0:T], T, lambda c, s: v("final", c), dst=x2[:, :, 0:T], logs=True, early=True)
        feed_forward(1, T, ffn1_norm, final_norm)

        with ExitStack() as own, nc.Block() as block:
            final_norm.buffers(own)

            @block.scalar
            def _(act):
                final_norm.act(act, None)

            @block.vector
            def _(dve):
                final_norm.dve(dve, None)

            @block.sync
            def _(sp):
                for part in range(2):
                    c = slice(part * C // 2, part * C // 2 + C // 2)
                    sp.wait_ge(scaled_done.h, scaled_done.at(c.stop))
                    sp.dma_start(dr["out_t"][:, c, :], x2[:, c, 0:T]).then_inc(out_stored, 16)
                sp.wait_ge(out_stored, 32)



def _feature_major(a):
    return np.ascontiguousarray(a.T.reshape(-1, P, a.shape[0]).transpose(1, 0, 2))


def _column(a):
    return a.reshape(-1, P).T


def _tiles(w, width=512, per=2):
    kk, n = w.shape
    return np.ascontiguousarray(w.reshape(kk // (per * P), per, P, n // width, width).transpose(3, 0, 2, 1, 4).reshape(-1, P, per * width))


def _heads(order, width=64):
    return np.concatenate([np.arange(h * width, h * width + width) for h in order])


def _layouts(a):
    f = {n: np.asarray(x) for n, x in a.items()}
    o = {}
    consts, mix_consts, rope = const_tables()
    o["consts"], o["mix_consts"], o["rope_consts"] = consts, mix_consts, rope
    o["x_t"] = _feature_major(f["x"][0])
    o["p_t"] = _feature_major(f["p"][0, 0])
    o["ctx_t"] = _feature_major(f["ctx_2"][0])
    nsa, gqa = _heads(NSA_ORDER), _heads(GQA_ORDER)

    w = f["w_in"][0]
    hq, hf, hi, hg, nq, nkc, nvc, nks, nvs, nkw, nvw, ng = np.split(w, np.cumsum([512] * 5 + [128] * 6), axis=1)
    o["w_in_t"] = [_tiles(hf), _tiles(hq), _tiles(nq[:, nsa]), _tiles(np.concatenate([nkc, nvc, nks, nkw], axis=1)),
                   _tiles(hg), _tiles(hi), _tiles(np.concatenate([nvs, nvw, ng], axis=1), 280)]
    w1 = f["cmp_w1"][0].reshape(2, CMP_LEN, 64, 64)
    both = np.zeros((2, P, CMP_LEN, P), w1.dtype)
    both[:, 0:64, :, 0:64] = w1.transpose(0, 2, 1, 3)
    both[:, 64:, :, 64:] = w1.transpose(0, 2, 1, 3)
    o["cmp_w1_t"] = np.ascontiguousarray(both.reshape(2, P, -1, PIECE).transpose(0, 2, 1, 3).reshape(-1, P, PIECE))
    w2 = np.zeros((P, 2, P), w1.dtype)
    w2[0:64, :, 0:64] = f["cmp_w2"][0].transpose(1, 0, 2)
    w2[64:, :, 64:] = f["cmp_w2"][0].transpose(1, 0, 2)
    o["cmp_w2_t"] = w2
    o["cmp_pe_t"] = np.ascontiguousarray(np.tile(f["cmp_pe"][0].transpose(2, 0, 1), (2, 1, 1)))
    wo = f["w_out"][0]
    o["w_out_t"] = _tiles(np.concatenate([wo[:512], wo[512:][nsa]]))
    o["peer_wq_t"] = _tiles(f["peer_wq"][0])
    o["peer_keys_t"] = np.ascontiguousarray(f["peer_keys"][0].reshape(PK_SETS * PK_KEYS // PIECE, -1, P).transpose(0, 2, 1))
    u = f["peer_u"][0].reshape(PK_KEYS, PK_KEYS, C, P).transpose(1, 3, 2, 0).reshape(PK_KEYS, P, D)
    vals = f["peer_v"][0].reshape(PK_KEYS, PK_KEYS, D).transpose(1, 0, 2)
    e = np.empty((2 * PK_KEYS, P, PIECE), u.dtype)
    e[0], e[1:-1:2] = u[0], u[1:]
    e[2:-1:2], e[-1] = vals[:-1], vals[-1]
    o["experts_t"] = e
    o["ple_gate_t"] = _tiles(f["ple_gate_w"][0])
    o["ple_proj_t"] = _tiles(f["ple_proj"][0])
    o["ada_t"] = np.concatenate([_tiles(f["ada_w_2"][i]) for i in range(LAYERS)])
    o["qkv0_t"] = _tiles(f["na_w_qkv_2"][0])
    o["o0_t"] = _tiles(f["na_w_o_2"][0])
    g = f["gqa_w_qkv_2"][0]
    kv = GQA_KV * DH
    o["qkv1_t"] = [_tiles(g[:, :D][:, gqa]), _tiles(g[:, D:D + kv], kv, 4), _tiles(g[:, D + kv:], kv, 4)]
    o["o1_t"] = _tiles(f["gqa_w_o_2"][0][gqa])
    for i in range(LAYERS):
        wi = f["ffn_w_in_2"][i].reshape(D, 2, FC // 2, 2 * P).transpose(0, 2, 1, 3).reshape(D, -1)
        o[f"ffn_in{i}_t"] = _tiles(wi)
        o[f"ffn_out{i}_t"] = np.ascontiguousarray(f["ffn_w_out_2"][i].reshape(FC, P, D))

    t = np.arange(T)
    rows = T // GRID_W
    assert rows <= NA_WIN_H
    drow = (t // GRID_W)[None, :] - (t // GRID_W)[:, None] + NA_WIN_H - 1
    start = np.clip(t % GRID_W - NA_WIN_W // 2, 0, GRID_W - NA_WIN_W)[:, None]
    inside = ((t % GRID_W)[None, :] >= start) & ((t % GRID_W)[None, :] < start + NA_WIN_W)
    dcol = np.clip((t % GRID_W)[None, :] - (t % GRID_W)[:, None] + NA_WIN_W - 1, 0, 2 * NA_WIN_W - 2)
    b = np.where(inside[None], f["na_rpb_2"][0][:, drow, dcol], np.float32(NEG))
    o["na_bias_t"] = np.ascontiguousarray(b.reshape(HEADS, TB, P, T).transpose(2, 0, 1, 3))

    vecs = {"mix_norm": _column(f["mix_norm"][0]), "lb0": _column(f["hg_lb_logits"][0]), "lb1": _column(f["hg_lb_logits"][1]),
            "hg_out": _column(f["hg_out_norm"][0]), "nsa_q": np.tile(f["nsa_q_norm"][0], 2)[:, None],
            "nsa_k": np.tile(f["nsa_k_norm"][0], (1, 2)).T, "nsa_out": _column(f["nsa_out_norm"][0][nsa]),
            "ffn_norm": _column(f["ffn_norm"][0]), "ple_norm": _column(f["ple_gate_norm"][0]),
            "mix2": _column(f["norm_mix_2"].reshape(-1)), "ffn2": _column(f["norm_ffn_2"].reshape(-1)), "final": _column(f["norm_final_2"]),
            "ada_b": _column(f["ada_b_2"].reshape(-1)), "gqa_q": np.tile(f["gqa_q_gain_2"][0], 2)[:, None],
            "gqa_k": np.tile(f["gqa_k_gain_2"][0], 2)[:, None],
            "cond": np.stack([_column(f["c_2"][0]), _column(f["c_ctx_2"])], axis=-1).reshape(P, -1)}
    o["vecs"] = np.ascontiguousarray(np.concatenate([vecs[n] for n, _ in VECS], axis=1))
    return o


def kernel(**inputs):
    import concourse.bacc as bacc
    from concourse.bass_utils import run_bass_kernel_spmd as run

    nc = bacc.Bacc("TRN2", target_bir_lowering=False, num_devices=1)
    arrays, dr = {}, {}

    def given(name, a):
        arrays[name] = np.ascontiguousarray(a)
        return nc.dram_tensor(name, arrays[name].shape, mybir.dt.from_np(arrays[name].dtype), kind="ExternalInput").ap()

    for name, a in _layouts(inputs).items():
        dr[name] = [given(f"{name}_{i}", x) for i, x in enumerate(a)] if isinstance(a, list) else given(name, a)
    dr["out_t"] = nc.dram_tensor("out_t", (P, C, T), F32, kind="ExternalOutput").ap()
    build(nc, dr)
    got = run(nc, [arrays], core_ids=[0]).results[0]["out_t"]
    return np.ascontiguousarray(got.transpose(2, 1, 0).reshape(1, T, D))
```

```python
from contextlib import ExitStack

import numpy as np

import concourse.bass as bass
from concourse import mybir

F32 = mybir.dt.float32
F32R = mybir.dt.float32r
I32 = mybir.dt.int32
BF16 = mybir.dt.bfloat16
U32 = mybir.dt.uint32
ACT = mybir.ActivationFunctionType
ALU = mybir.AluOpType
AX = mybir.AxisListType

P = 128
D = 1024
C = D // P
T = 256
TB = T // P
TC = 256
EPS = 1e-6
NEG = -1e30
LOWEST = -3e38

HG_HEADS, HG_CHUNK = 4, 64
HG_N = T // HG_CHUNK
NSA_HEADS, NSA_KV, NSA_DH = 8, 2, 64
NSA_G = NSA_HEADS // NSA_KV
CMP_LEN, CMP_STRIDE = 32, 16
N_CMP = (T - CMP_LEN) // CMP_STRIDE + 1
SLC_LEN, SLC_TOPK, WIN = 64, 16, 512
assert T // SLC_LEN <= SLC_TOPK and T <= WIN
PK_HEADS, PK_KEYS, PK_TOP = 8, 128, 16
PK_SETS = 2 * PK_HEADS
PK_HK = PK_HEADS * PK_TOP
HEADS, DH = 16, 64
GQA_KV = 4
GRID_W, NA_WIN_W, NA_WIN_H = 64, 16, 8
FFN = 2816
FC = FFN // P
N_MOD = 6
LAYERS = 2
ROPE_THETA = 10000.0
TT = T + TC

ADA_TILES = LAYERS * N_MOD * D // 512
ADA = (3, 5, 7, 9, 10, 11, ADA_TILES)
HG_LOT, HG_END_LOT, QK_LOT, CMP_LOT, NSA_LOT, OUT_LOT, TOP_LOT = range(len(ADA))
PIECE = 1024
RAW = 4
SPLIT = 3

NSA_ORDER = [h for c in range(NSA_G) for h in (c, NSA_G + c)]
GQA_ORDER = [h for k in (0, 2) for c in range(4) for h in (4 * k + c, 4 * k + 4 + c)]

VECS = [("mix_norm", C), ("lb0", 4), ("lb1", 4), ("hg_out", 4), ("nsa_q", 1), ("nsa_k", 3), ("nsa_out", 4),
        ("ffn_norm", C), ("ple_norm", C), ("mix2", LAYERS * C), ("ffn2", LAYERS * C), ("final", C),
        ("ada_b", LAYERS * N_MOD * C), ("gqa_q", 1), ("gqa_k", 1), ("cond", 2 * C)]
VEC_AT, NV = {}, 0
for _n, _w in VECS:
    VEC_AT[_n] = NV
    NV += _w

CONSTS = [("ident", P), ("ones", P), ("ones64", P), ("iota", P), ("swap", P)]
MIX_CONSTS = [("hg_mask", P), ("dist", TB * T), ("cdist", TB * N_CMP), ("cmask", TB * N_CMP)]
CONST_AT, NCONST = {}, 0
for _n, _w in CONSTS:
    CONST_AT[_n] = NCONST
    NCONST += _w
MIX_AT, NMIX = {}, 0
for _n, _w in MIX_CONSTS:
    MIX_AT[_n] = NMIX
    NMIX += _w


def const_tables():
    t = {}
    i = np.arange(P)
    t["ident"] = np.eye(P)
    t["ones"] = np.ones((P, P))
    t["ones64"] = (i[:, None] // 64 == i[None, :] // 64) * 1.0
    t["iota"] = np.broadcast_to(i, (P, P))
    s = np.zeros((P, P))
    for m in range(P):
        k = m + 16 if m % 32 < 16 else m - 16
        s[k, m] = -1.0 if m % 32 < 16 else 1.0
    t["swap"] = s
    t["hg_mask"] = ((i[:, None] <= i[None, :]) & (i[:, None] // HG_CHUNK == i[None, :] // HG_CHUNK)) * 1.0
    pos = np.arange(T)
    dist = (pos[:, None] - pos[None, :]).astype(np.float64)
    t["dist"] = np.where(dist >= 0, -dist, NEG).reshape(TB, P, T).transpose(1, 0, 2).reshape(P, -1)
    end = np.arange(N_CMP) * CMP_STRIDE + CMP_LEN - 1
    cd = (pos[:, None] - end[None, :]).astype(np.float64)
    t["cdist"] = np.where(cd >= 0, -cd, NEG).reshape(TB, P, N_CMP).transpose(1, 0, 2).reshape(P, -1)
    t["cmask"] = ((cd >= 0) * 1.0).reshape(TB, P, N_CMP).transpose(1, 0, 2).reshape(P, -1)
    half = DH // 2
    inv = (1.0 / (np.float32(ROPE_THETA) ** (np.arange(0, half, 2, dtype=np.float32) / np.float32(half)))).astype(np.float32)
    row = (pos // GRID_W).astype(np.float32)
    col = (pos % GRID_W).astype(np.float32)
    ang = np.concatenate([np.tile((row[:, None] * inv).T, (2, 1)), np.tile((col[:, None] * inv).T, (2, 1))])
    t["cos"] = np.tile(np.cos(ang), (2, 1))
    t["sin"] = np.tile(np.sin(ang), (2, 1))
    t["rope"] = np.concatenate([t["cos"], t["sin"]], axis=1)

    def table(names):
        return np.ascontiguousarray(np.concatenate([t[n] for n in names], axis=1).astype(np.float32))
    return table([n for n, _ in CONSTS]), table([n for n, _ in MIX_CONSTS]), table(["rope"])


class Signal:

    def __init__(self, handle):
        self.h, self.base = handle, 0

    def at(self, n):
        return self.base + n

    def advance(self, n):
        self.base += n


def build(nc, dr):
    ctx = ExitStack()
    with ctx:
        def sem(name):
            return ctx.enter_context(nc.semaphore(name))

        def signal(name):
            return Signal(sem(name))

        used = []

        def numbered(name):
            used.append(name)
            return f"{name}{used.count(name)}"

        raw = ctx.enter_context(nc.sbuf_tensor("raw", [P, RAW, PIECE], F32))
        whi = ctx.enter_context(nc.sbuf_tensor("whi", [P, SPLIT, PIECE], F32R))
        wlo = ctx.enter_context(nc.sbuf_tensor("wlo", [P, SPLIT, PIECE], F32R))
        vec = ctx.enter_context(nc.sbuf_tensor("vec", [P, NV], F32))
        kon = ctx.enter_context(nc.sbuf_tensor("kon", [P, NCONST], F32))
        eps = ctx.enter_context(nc.sbuf_tensor("eps", [P, 1], F32))
        idle = ctx.enter_context(nc.sbuf_tensor("idle", [P, 1], F32))
        mod = ctx.enter_context(nc.sbuf_tensor("mod", [P, LAYERS, N_MOD * C, 2], F32))
        gs1 = ctx.enter_context(nc.sbuf_tensor("gs1", [P, LAYERS, C, 2], F32))
        gs2 = ctx.enter_context(nc.sbuf_tensor("gs2", [P, LAYERS, C, 2], F32))
        tokens = ctx.enter_context(ExitStack())
        hT = tokens.enter_context(nc.sbuf_tensor("hT", [P, C, T], F32, side="right"))
        ps = ctx.enter_context(nc.psum_tensor("ps", [P, 8, 512], F32))

        def v(name, i=0, n=1):
            return vec[:, VEC_AT[name] + i:VEC_AT[name] + i + n]

        def k(name, a=0, b=None):
            w = dict(CONSTS)[name]
            return kon[:, CONST_AT[name] + a:CONST_AT[name] + (w if b is None else b)]

        raw_loaded = [sem(f"raw_loaded{i}") for i in range(RAW)]
        hi_done, lo_done = sem("hi_done"), sem("lo_done")
        piece_used, raw_used = sem("piece_used"), sem("raw_used")
        start_loaded, mix_loaded = sem("start_loaded"), sem("mix_loaded")
        act_evacuated = signal("act_evacuated")
        dve_evacuated = signal("dve_evacuated")
        squares_done = signal("squares_done")
        sums_done = signal("sums_done")
        root_done = signal("root_done")
        rstd_done = signal("rstd_done")
        scaled_done = signal("scaled_done")
        rounded_done = signal("rounded_done")
        parted_done = signal("parted_done")
        dve_squares = signal("dve_squares")
        pairs_done = signal("pairs_done")
        early_squares = signal("early_squares")
        early_sums = signal("early_sums")
        folded = signal("folded")
        ada_out = signal("ada_out")
        out_stored = sem("out_stored")

        pieces = []
        count = {True: 0, False: 0}

        own_end = {}

        def add_pieces(name, split=True, a=0, b=None, end=None):
            first = len(pieces)
            for x in dr[name] if isinstance(dr[name], list) else [dr[name]]:
                for i in range(a, x.shape[0] if b is None else b):
                    if end:
                        own_end[len(pieces)] = end(i)
                    pieces.append((x[i], x.shape[2], split, count[split]))
                    count[split] += not end
            return first

        at_ada = []

        def add_lot():
            lot = len(at_ada)
            at_ada.append(add_pieces("ada_t", False, 4 * ADA[lot - 1] if lot else 0, 4 * ADA[lot]))
        top_pe = sem("top_pe_step")
        at_in = add_pieces("w_in_t")
        add_lot()
        add_lot()
        add_lot()
        at_cmp = add_pieces("cmp_w1_t", split=False)
        add_lot()
        add_lot()
        add_lot()
        at_wout = add_pieces("w_out_t")
        at_wq = add_pieces("peer_wq_t")
        at_keys = add_pieces("peer_keys_t", split=False, end=lambda i: (top_pe, 4 * i + 4))
        add_lot()
        at_experts = add_pieces("experts_t")
        at_ple = add_pieces("ple_gate_t")
        add_pieces("ple_proj_t")
        at_qkv = [None] * LAYERS
        at_o = [None] * LAYERS
        at_f1 = [None] * LAYERS
        at_f2 = [None] * LAYERS
        for i in range(LAYERS):
            at_qkv[i] = add_pieces(f"qkv{i}_t")
            at_o[i] = add_pieces(f"o{i}_t")
            at_f1[i] = add_pieces(f"ffn_in{i}_t")
            at_f2[i] = add_pieces(f"ffn_out{i}_t")
        n_pieces = len(pieces)
        next_load = [0]

        def loads(sp, upto):
            for g in range(next_load[0], min(upto, n_pieces)):
                if g >= RAW:
                    _, _, split, n = pieces[g - RAW]
                    if g - RAW in own_end:
                        sp.wait_ge(*own_end[g - RAW])
                    else:
                        sp.wait_ge(lo_done if split else raw_used, n + 1)
                src, w, _, _ = pieces[g]
                sp.dma_start(raw[:, g % RAW, 0:w], src).then_inc(raw_loaded[g % RAW], 16)
            next_load[0] = max(next_load[0], min(upto, n_pieces))

        def piece_loaded(eng, g):
            eng.wait_ge(raw_loaded[g % RAW], 16 * (g // RAW + 1))

        def split_hi(act, g):
            _, w, _, n = pieces[g]
            piece_loaded(act, g)
            if n >= SPLIT:
                act.wait_ge(piece_used, n - SPLIT + 1)
            act.activation(whi[:, n % SPLIT, 0:w], raw[:, g % RAW, 0:w], ACT.Copy).then_inc(hi_done, 1)

        def split_lo(dve, g):
            _, w, _, n = pieces[g]
            dve.wait_ge(hi_done, n + 1)
            dve.tensor_tensor(wlo[:, n % SPLIT, 0:w], raw[:, g % RAW, 0:w], whi[:, n % SPLIT, 0:w].bitcast(F32),
                              ALU.subtract).then_inc(lo_done, 1)

        split_upto = [0]

        def ahead(g):
            n = 0
            while n < SPLIT - 1 and g + n < n_pieces and pieces[g + n][2]:
                n += 1
            return list(range(g, g + n))

        class Parted:

            def __init__(self, src, parts, chunks, after=0, loaded=None):
                self.src, self.parts, self.chunks, self.after, self.loaded = src, parts, chunks, after, loaded

            def buffers(self, own):
                pass

            def act(self, act, before):
                if self.loaded:
                    act.wait_ge(self.loaded, 16)
                for c in range(self.chunks):
                    before(c)
                    act.activation(self.parts[0][:, c, :], self.src[:, c, :], ACT.Copy).then_inc(rounded_done.h, 1)

            def pe(self, pe):
                pass

            def dve(self, dve, before):
                for c in range(self.chunks):
                    before(c)
                    dve.wait_ge(rounded_done.h, rounded_done.at(self.after + c + 1))
                    dve.tensor_tensor(self.parts[1][:, c, :], self.src[:, c, :], self.parts[0][:, c, :].bitcast(F32),
                                      ALU.subtract).then_inc(parted_done.h, 1)

            def end(self):
                rounded_done.advance(self.chunks)
                parted_done.advance(self.chunks)

        class Norm:

            def __init__(self, src, n, gain, shift=None, segs=1, parts=None, dst=None, logs=False, early=False):
                self.src, self.n, self.gain, self.shift, self.segs = src, n, gain, shift, segs
                self.parts, self.x, self.logs, self.early = parts, dst, logs, early

            def buffers(self, own):
                def ob(name, shape):
                    return own.enter_context(nc.sbuf_tensor(numbered(name), shape, F32))
                self.rstd = ob("rstd", [P, self.n])
                self.root = self.rstd if self.logs else ob("root", [P, self.n])
                if self.x is None:
                    self.x = ob("normed", [P, C, self.n])

            def segment(self, s):
                w = self.n // self.segs
                return slice(s * w, s * w + w)

            def load_table(self, act):
                act.activation(idle[:, :], eps[:, :], ACT.Ln if self.logs else ACT.Sqrt)

            def squares(self, act, a, b):
                for c in range(a, b):
                    act.wait_ge(dve_evacuated.h, dve_evacuated.at(c + 1))
                    act.activation(self.x[:, c, :], self.src[:, c, :], ACT.Square).then_inc(early_squares.h, 1)

            def fold(self, dve):
                for c in range(1, C // 2):
                    dve.wait_ge(early_squares.h, early_squares.at(c + 1))
                    if c >= 2:
                        dve.wait_ge(folded.h, folded.at(c - 1))
                    dve.tensor_tensor(self.x[:, 0, :], self.x[:, 0, :], self.x[:, c, :], ALU.add).then_inc(folded.h, 1)

            def sums(self, pe, fold):
                if fold:
                    pe.wait_ge(folded.h, folded.at(C // 2 - 1))
                for c in [0] * fold + list(range(C // 2 if fold else 0, C)):
                    pe.wait_ge(early_squares.h, early_squares.at(c + 1))
                    mm = pe.matmul(ps[:, 0, 0:self.n], k("ones"), self.x[:, c, :], start=(c == 0), stop=(c == C - 1))
                mm.then_inc(early_sums.h, 1)

            def end_early(self, fold):
                if fold:
                    folded.advance(C // 2 - 1)
                early_squares.advance(C)
                early_sums.advance(1)

            def act(self, act, before):
                x, half = self.x, C // 2
                if not self.early:
                    for c in range(half):
                        act.activation(x[:, c, :], self.src[:, c, :], ACT.Square).then_inc(squares_done.h, 1)
                    self.load_table(act)
                    act.wait_ge(sums_done.h, sums_done.at(1))
                act.activation(self.root[:, :], ps[:, 0, 0:self.n], ACT.Ln if self.logs else ACT.Sqrt,
                               bias=eps[:, :], scale=1.0 / D).then_inc(root_done.h, 1)
                if self.logs:
                    act.wait_ge(root_done.h, root_done.at(1))
                    act.activation(self.rstd[:, :], self.root[:, :], ACT.Exp, scale=-0.5).then_inc(rstd_done.h, 1)
                if self.parts:
                    for c in range(C):
                        before(c)
                        act.wait_ge(scaled_done.h, scaled_done.at(c + 1))
                        for s in range(self.segs):
                            t = self.segment(s)
                            kind, add = (ACT.Copy, {}) if self.shift is None else (ACT.Identity, {"bias": self.shift(c, s)})
                            ins = act.activation(self.parts[0][:, c, t], x[:, c, t], kind, **add)
                        ins.then_inc(rounded_done.h, 1)

            def pe(self, pe):
                if self.early:
                    return
                half = C // 2
                for c in range(half):
                    pe.wait_ge(pairs_done.h, pairs_done.at(c + 1))
                    mm = pe.matmul(ps[:, 0, 0:self.n], k("ones"), self.x[:, half + c, :], start=(c == 0), stop=(c == half - 1))
                mm.then_inc(sums_done.h, 1)

            def dve(self, dve, before):
                x, half = self.x, C // 2
                for c in range(0 if self.early else half + 1):
                    if c < half:
                        dve.tensor_tensor(x[:, half + c, :], self.src[:, half + c, :], self.src[:, half + c, :], ALU.mult).then_inc(dve_squares.h, 1)
                    if c >= 1:
                        dve.wait_ge(squares_done.h, squares_done.at(c))
                        dve.wait_ge(dve_squares.h, dve_squares.at(c))
                        dve.tensor_tensor(x[:, half + c - 1, :], x[:, half + c - 1, :], x[:, c - 1, :], ALU.add).then_inc(pairs_done.h, 1)
                if not self.logs:
                    dve.wait_ge(root_done.h, root_done.at(1))
                    dve.reciprocal(self.rstd[:, :], self.root[:, :]).then_inc(rstd_done.h, 1)
                dve.wait_ge(rstd_done.h, rstd_done.at(1))
                for c in range(C + 1):
                    if c < C:
                        for s in range(self.segs):
                            t = self.segment(s)
                            ins = dve.scalar_tensor_tensor(out=x[:, c, t], in0=self.src[:, c, t], scalar=self.gain(c, s), in1=self.rstd[:, t],
                                                           op0=ALU.mult, op1=ALU.mult)
                        ins.then_inc(scaled_done.h, 1)
                    if self.parts and c >= 1:
                        before(c - 1)
                        dve.wait_ge(rounded_done.h, rounded_done.at(c))
                        for s in range(self.segs):
                            t = self.segment(s)
                            low, high = self.parts[1][:, c - 1, t], self.parts[0][:, c - 1, t].bitcast(F32)
                            if self.shift is None:
                                ins = dve.tensor_tensor(low, x[:, c - 1, t], high, ALU.subtract)
                            else:
                                ins = dve.scalar_tensor_tensor(out=low, in0=x[:, c - 1, t], scalar=self.shift(c - 1, s), in1=high,
                                                               op0=ALU.add, op1=ALU.subtract)
                        ins.then_inc(parted_done.h, 1)

            def end(self):
                for s, n in ((root_done, 1), (rstd_done, 1), (scaled_done, C)):
                    s.advance(n)
                if not self.early:
                    for s, n in ((squares_done, C // 2), (dve_squares, C // 2), (pairs_done, C // 2), (sums_done, 1)):
                        s.advance(n)
                if self.parts:
                    rounded_done.advance(C)
                    parted_done.advance(C)

        def products(pe, place, stationary, moving, start, stop):
            (wh, wl), (xh, xl) = stationary, moving
            pe.matmul(place, wh, xh, start=start, stop=False)
            pe.matmul(place, wh, xl, start=False, stop=False)
            return pe.matmul(place, wl, xh, start=False, stop=stop)

        def product_stage(first, x, tiles, before=None, lot=None, sync=None, then=None, last=None, fold=False, also=None):
            own_x, also_at = also or (None, None)
            at, a_n, d_n, spans = first, 0, 0, []
            for n_pc, per, width, jobs in tiles:
                outs = []
                for j in jobs:
                    a_n += j[3] is not None
                    d_n += j[4] is not None
                    outs.append((a_n, d_n))
                spans.append((at, outs))
                at += n_pc
            after = ahead(at)

            def place(t, j):
                kind, a, b, _, _ = tiles[t][3][j]
                n = (b.stop - b.start) if kind == "wide" else a.stop - a.start
                return ps[:, 4 * (t % 2) + j, 0:n]

            def of_first(c):
                per = tiles[0][1]
                return [first + c // per] if c % per == 0 and first + c // per >= split_upto[0] else []

            with ExitStack() as own, nc.Block() as block:
                if before:
                    before.buffers(own)

                @block.sync
                def _(sp):
                    if sync:
                        sync(sp)
                    loads(sp, at + RAW)

                @block.tensor
                def _(pe):
                    if lot is not None:
                        ada_lot_pe(pe, lot, 4)
                    if before:
                        before.pe(pe)
                    for t, (n_pc, per, width, jobs) in enumerate(tiles):
                        g0, _ = spans[t]
                        if t == 1 and lot is not None:
                            pe.wait_ge(ada_out.h, ada_out.at(1))
                        if t >= 2:
                            a_out, d_out = spans[t - 2][1][-1]
                            if a_out:
                                pe.wait_ge(act_evacuated.h, act_evacuated.at(a_out))
                            if d_out:
                                pe.wait_ge(dve_evacuated.h, dve_evacuated.at(d_out))
                        for g in range(g0, g0 + n_pc):
                            _, _, _, n = pieces[g]
                            pe.wait_ge(lo_done, n + 1)
                            wp = [w[:, n % SPLIT, 0:per * width].rearrange("p (c n) -> p c n", n=width) for w in (whi, wlo)]
                            xs = own_x.parts if also and t >= also_at else x
                            for i in range(per):
                                c = (g - g0) * per + i
                                first_c, last_c = c == 0, c == n_pc * per - 1
                                if before and t == 0:
                                    pe.wait_ge(parted_done.h, parted_done.at(c + 1))
                                if also and t == also_at:
                                    pe.wait_ge(parted_done.h, parted_done.at(own_x.after + c + 1))
                                for j, (kind, a, b, _, _) in enumerate(jobs):
                                    if kind == "wide":
                                        w, y = [v_[:, i, a:a + P] for v_ in wp], [v_[:, c, b] for v_ in xs]
                                    else:
                                        w, y = [v_[:, c, b:b + P] for v_ in xs], [v_[:, i, a] for v_ in wp]
                                    mm = products(pe, place(t, j), w, y, first_c, last_c)
                            mm.then_inc(piece_used, 1)
                    if then:
                        a_out, d_out = spans[-2][1][-1]
                        if a_out:
                            pe.wait_ge(act_evacuated.h, act_evacuated.at(a_out))
                        if d_out:
                            pe.wait_ge(dve_evacuated.h, dve_evacuated.at(d_out))
                        then.sums(pe, fold)

                @block.scalar
                def _(act):
                    def take_out(t):
                        g0, _ = spans[t]
                        act.wait_ge(piece_used, pieces[g0 + tiles[t][0] - 1][3] + 1)
                        for j, job in enumerate(tiles[t][3]):
                            if job[3] is not None:
                                job[3](act, place(t, j)).then_inc(act_evacuated.h, 1)
                        if then:
                            then.squares(act, spans[t - 1][1][-1][1] if t else 0, spans[t][1][-1][1])
                    if lot is not None:
                        ada_lot_act(act, lot, 4)
                    if before:
                        before.act(act, lambda c: [split_hi(act, g) for g in of_first(c)])
                    if also:
                        own_x.act(act, lambda c: None)
                    for t, (n_pc, _, _, _) in enumerate(tiles):
                        for i in range(n_pc):
                            if spans[t][0] + i >= split_upto[0] and not (before and t == 0):
                                split_hi(act, spans[t][0] + i)
                            if t >= 1 and i == min(1, n_pc - 1):
                                take_out(t - 1)
                    for g in after:
                        split_hi(act, g)
                    take_out(len(tiles) - 1)
                    if then:
                        then.load_table(act)

                @block.vector
                def _(dve):
                    def take_out(t):
                        g0, outs = spans[t]
                        dve.wait_ge(piece_used, pieces[g0 + tiles[t][0] - 1][3] + 1)
                        for j, job in enumerate(tiles[t][3]):
                            if job[4] is not None:
                                if job[3] is not None:
                                    dve.wait_ge(act_evacuated.h, act_evacuated.at(outs[j][0]))
                                job[4](dve, place(t, j)).then_inc(dve_evacuated.h, 1)
                    if before:
                        before.dve(dve, lambda c: [split_lo(dve, g) for g in of_first(c)])
                    if also:
                        own_x.dve(dve, lambda c: None)
                    for t, (n_pc, _, _, _) in enumerate(tiles):
                        for i in range(n_pc):
                            if spans[t][0] + i >= split_upto[0] and not (before and t == 0):
                                split_lo(dve, spans[t][0] + i)
                            if t >= 1 and i == min(1, n_pc - 1):
                                take_out(t - 1)
                    for g in after:
                        split_lo(dve, g)
                    if last:
                        last(dve)
                    if fold:
                        then.fold(dve)
                    take_out(len(tiles) - 1)
            split_upto[0] = at + len(after)
            act_evacuated.advance(a_n)
            dve_evacuated.advance(d_n)
            if before:
                before.end()
            if also:
                own_x.end()
            if then:
                then.end_early(fold)
            if lot is not None:
                ada_out.advance(1)

        def wide_tiles(n, w, out, x0=0):
            return [(4, 2, 512, [("wide", j * P, slice(x0, x0 + w), *out(4 * t + j)) for j in range(4)]) for t in range(n // 4)]

        def copied(n, dst, scale=None):
            if n % 2 == 0:
                return (lambda act, place: act.activation(dst, place, ACT.Copy, scale=1.0 if scale is None else scale)), None
            if scale is None:
                return None, lambda dve, place: dve.tensor_copy(dst, place)
            return None, lambda dve, place: dve.tensor_scalar(dst, place, scale, None, ALU.mult)

        def head_norm_stage(x, n, gain, lot=None, logs=False):
            flat = x.rearrange("p n t -> p (n t)")
            groups = n * T // 512
            with ExitStack() as own, nc.Block() as block:
                sq = own.enter_context(nc.sbuf_tensor(numbered("head_squares"), [P, n * T], F32))
                rstd = own.enter_context(nc.sbuf_tensor(numbered("head_rstd"), [P, n, T], F32))

                flat_rstd = rstd[:, :, :].rearrange("p n t -> p (n t)")

                @block.sync
                def _(sp):
                    if lot is not None:
                        loads(sp, lot_end(lot) + RAW)

                @block.scalar
                def _(act):
                    act.activation(sq[:, :], flat, ACT.Square).then_inc(squares_done.h, 1)
                    act.wait_ge(sums_done.h, sums_done.at(1))
                    act.activation(sq[:, :], ps[:, 0:groups, :].rearrange("p g t -> p (g t)"), ACT.Ln if logs else ACT.Sqrt,
                                   bias=eps[:, :], scale=1.0 / 64).then_inc(root_done.h, 1)
                    if logs:
                        act.wait_ge(root_done.h, root_done.at(1))
                        act.activation(flat_rstd, sq[:, :], ACT.Exp, scale=-0.5).then_inc(rstd_done.h, 1)
                    if lot is not None:
                        ada_lot_act(act, lot, 4)

                @block.tensor
                def _(pe):
                    pe.wait_ge(squares_done.h, squares_done.at(1))
                    for g in range(groups):
                        mm = pe.matmul(ps[:, g, :], k("ones64"), sq[:, g * 512:g * 512 + 512], start=True, stop=True)
                    mm.then_inc(sums_done.h, 1)
                    if lot is not None:
                        ada_lot_pe(pe, lot, 4)

                @block.vector
                def _(dve):
                    if not logs:
                        dve.wait_ge(root_done.h, root_done.at(1))
                        dve.reciprocal(flat_rstd, sq[:, :]).then_inc(rstd_done.h, 1)
                    dve.wait_ge(rstd_done.h, rstd_done.at(1))
                    for c in range(n):
                        dve.scalar_tensor_tensor(out=x[:, c, :], in0=x[:, c, :], scalar=gain(c), in1=rstd[:, c, :],
                                                 op0=ALU.mult, op1=ALU.mult)
            for s in (squares_done, sums_done, root_done, rstd_done):
                s.advance(1)
            if lot is not None:
                ada_out.advance(1)

        ada_rows_out, ada_turned = sem("ada_rows_out"), sem("ada_turned")
        cond = ctx.enter_context(nc.sbuf_tensor("cond", [P, C, 2], F32))
        ada_row = []

        def lot_tiles(lot):
            return ADA[lot - 1] if lot else 0, ADA[lot]

        def lot_end(lot):
            a, b = lot_tiles(lot)
            return at_ada[lot] + 4 * (b - a)

        def ada_first(t, lot):
            return at_ada[lot] + 4 * (t - lot_tiles(lot)[0])

        def ada_turn(pe, t, lot, bank0):
            pe.wait_ge(ada_rows_out, t + 1)
            for j in range(4):
                n = 4 * (t - lot_tiles(lot)[0]) + j
                mm = pe.transpose(ps[:, bank0 + 2, 2 * n:2 * n + 2], ada_row[-1][:, t % 2, j * P:j * P + P], k("ident")[0:2, 0:2])
            mm.then_inc(ada_turned, 1)

        def ada_tile_pe(pe, t, lot, bank0):
            a, b = lot_tiles(lot)
            if t >= a + 2:
                pe.wait_ge(ada_rows_out, t - 1)
            for i in range(4):
                g = ada_first(t, lot) + i
                piece_loaded(pe, g)
                for j in range(2):
                    c = 2 * i + j
                    mm = pe.matmul(ps[0:2, bank0 + t % 2, :], cond[:, c, :], raw[:, g % RAW, j * 512:j * 512 + 512], start=(c == 0), stop=(c == C - 1))
                mm.then_inc(raw_used, 1)
            if t > a:
                ada_turn(pe, t - 1, lot, bank0)
            if t == b - 1:
                ada_turn(pe, t, lot, bank0)

        def ada_tile_act(act, t, lot, bank0):
            a, b = lot_tiles(lot)
            act.wait_ge(raw_used, pieces[ada_first(t, lot) + 3][3] + 1)
            if t >= 2:
                act.wait_ge(ada_turned, t - 1)
            act.activation(ada_row[-1][:, t % 2, :], ps[0:2, bank0 + t % 2, :], ACT.Copy).then_inc(ada_rows_out, 1)
            if t == b - 1:
                act.wait_ge(ada_turned, b)
                act.activation(mod[:, :, :, :].rearrange("p l j s -> p (l j s)")[:, 8 * a:8 * b], ps[:, bank0 + 2, 0:8 * (b - a)],
                               ACT.Copy).then_inc(ada_out.h, 1)

        def ada_lot_pe(pe, lot, bank0):
            for t in range(*lot_tiles(lot)):
                ada_tile_pe(pe, t, lot, bank0)

        def ada_lot_act(act, lot, bank0):
            for t in range(*lot_tiles(lot)):
                ada_tile_act(act, t, lot, bank0)

        mixer = ctx.enter_context(ExitStack())

        def mb(name, shape):
            return mixer.enter_context(nc.sbuf_tensor(name, shape, F32))

        row_space = ctx.enter_context(ExitStack())
        ada_row.append(row_space.enter_context(nc.sbuf_tensor("ada_row", [2, 2, 512], F32, side="right")))
        aH = [mixer.enter_context(nc.sbuf_tensor(n, [P, C, T], F32R)) for n in ("aT_hi", "aT_lo")]
        hgT = mb("hgT", [P, 3, 4, T])
        nqk = mb("nqk", [P, 6, T])
        cin = mb("cin", [P, 2, T])
        hg_v = mb("hg_v", [P, TB, 512])
        nv = mb("nv", [P, TB, 280])
        mixT = mb("mixT", [P, C, T])
        mkon = mb("mkon", [P, NMIX])
        cmp_pe = mb("cmp_pe", [P, 2, CMP_LEN])
        cmp_w2 = mb("cmp_w2", [P, 2, P])

        def mk(name):
            return mkon[:, MIX_AT[name]:MIX_AT[name] + dict(MIX_CONSTS)[name]]

        with nc.Block() as block:
            @block.sync
            def _(sp):
                sp.dma_start(hT[:, :, :], dr["x_t"]).then_inc(start_loaded, 16)
                sp.dma_start(vec[:, :], dr["vecs"]).then_inc(start_loaded, 16)
                sp.dma_start(kon[:, :], dr["consts"]).then_inc(start_loaded, 16)
                loads(sp, RAW)
                sp.dma_start(mkon[:, :], dr["mix_consts"]).then_inc(mix_loaded, 16)
                sp.dma_start(cmp_pe[:, :, :], dr["cmp_pe_t"]).then_inc(mix_loaded, 16)
                sp.dma_start(cmp_w2[:, :, :], dr["cmp_w2_t"]).then_inc(mix_loaded, 16)

            @block.vector
            def _(dve):
                dve.memset(eps[:, :], EPS)
                dve.wait_ge(start_loaded, 48)

        chunks = ([hgT[:, 0, j, :] for j in range(4)] + [hgT[:, 1, j, :] for j in range(4)] + [nqk[:, j, :] for j in range(4)]
                  + [cin[:, 0, :], cin[:, 1, :], nqk[:, 4, :], nqk[:, 5, :]] + [hgT[:, 2, j, :] for j in range(4)])
        product_stage(at_in, aH, wide_tiles(len(chunks), T, lambda n: copied(n, chunks[n]))
                      + [(4, 2, 512, [("tall", slice(0, 512), b * P, *copied(b, hg_v[:, b, :])) for b in range(TB)]),
                         (4, 2, 280, [("tall", slice(0, 280), b * P, *copied(b, nv[:, b, :])) for b in range(TB)])],
                      before=Norm(hT, T, lambda c, s: v("mix_norm", c), parts=aH))

        hg_act, hg_dve, hg_pe = sem("hg_act_step"), sem("hg_dve_step"), sem("hg_pe_step")
        hg_cond = sem("hg_cond")
        with ExitStack() as own, nc.Block() as block:
            def ob(name, shape):
                return own.enter_context(nc.sbuf_tensor(name, shape, F32))

            H4 = [P, HG_HEADS, T]
            lb, lbd, oml = ob("lb", [P, 4]), ob("lbd", [P, 4]), ob("oml", [P, 4])
            keep, sig, forget, key, logf, G = (ob(n, H4) for n in ("keep", "sig", "forget", "key", "logf", "G"))
            d1, d4, e1, e2, e3, e4 = (ob(n, H4) for n in ("d1", "d4", "e1", "e2", "e3", "e4"))
            qs, gate, qa, ka, qi, ki = (ob(n, H4) for n in ("qs", "gate", "qa", "ka", "qi", "ki"))
            am = ob("am", [P, TB, 512])
            kiT = ob("kiT", [P, TB, 512])
            S = ob("S", [P, 3, 512])
            osq, on, rstd = am, sig, kiT

            def fl(x):
                return x[:, :, :].rearrange("p h t -> p (h t)")

            def ch(x):
                return fl(x).rearrange("p (n s) -> p n s", s=HG_CHUNK)

            def at_end(x, i):
                return ch(x)[:, :, i:i + 1].broadcast_to([P, HG_HEADS * HG_N, HG_CHUNK])

            @block.scalar
            def _(act):
                act.activation(cond[:, :, :].rearrange("p c s -> p (c s)"), v("cond", 0, 2 * C), ACT.Silu).then_inc(hg_cond, 1)
                act.activation(fl(sig), hgT[:, 0, :, :].rearrange("p h t -> p (h t)"), ACT.Sigmoid).then_inc(hg_act, 1)
                act.wait_ge(hg_dve, 1)
                act.activation(lb[:, :], lbd[:, :], ACT.Sigmoid).then_inc(hg_act, 1)
                act.activation(fl(qs), hgT[:, 1, :, :].rearrange("p h t -> p (h t)"), ACT.Silu).then_inc(hg_act, 1)
                act.activation(fl(gate), hgT[:, 2, :, :].rearrange("p h t -> p (h t)"), ACT.Silu).then_inc(hg_act, 1)
                act.wait_ge(hg_dve, 9)
                act.activation(fl(logf), fl(forget), ACT.Ln).then_inc(hg_act, 1)
                ada_tile_act(act, 0, HG_LOT, 4)
                act.wait_ge(hg_dve, 13)
                act.activation(fl(e1), fl(d1), ACT.Exp).then_inc(hg_act, 1)
                act.activation(fl(e2), fl(d1), ACT.Exp, scale=-1.0).then_inc(hg_act, 1)
                act.activation(fl(e3), fl(G), ACT.Exp).then_inc(hg_act, 1)
                act.activation(fl(e4), fl(d4), ACT.Exp).then_inc(hg_act, 1)
                for t in range(1, ADA[HG_LOT]):
                    ada_tile_act(act, t, HG_LOT, 4)
                for b in range(TB):
                    act.wait_ge(hg_pe, 3 + b)
                    act.activation(kiT[:, b, :], ps[:, 2 + b, :], ACT.Copy).then_inc(hg_act, 1)
                for b in range(TB):
                    act.wait_ge(hg_pe, 8 + b)
                    act.activation(osq[:, b, :], ps[:, b, :], ACT.Square).then_inc(hg_act, 1)
                act.wait_ge(hg_pe, 10)
                act.activation(osq[:, :, :].rearrange("p b n -> p (b n)"), ps[:, 2:4, :].rearrange("p b n -> p (b n)"),
                               ACT.Sqrt, bias=eps[:, :], scale=1.0 / P).then_inc(hg_act, 1)
                ada_lot_act(act, HG_END_LOT, 4)

            @block.vector
            def _(dve):
                dve.tensor_scalar(v("nsa_q"), v("nsa_q"), NSA_DH ** -0.5, None, ALU.mult)
                dve.tensor_scalar(v("gqa_q"), v("gqa_q"), DH ** -0.5, None, ALU.mult)
                dve.tensor_tensor(lbd[:, :], v("lb0", 0, 4), v("lb1", 0, 4), ALU.subtract).then_inc(hg_dve, 1)
                dve.memset(keep[:, :, :], 1.0).then_inc(hg_dve, 1)
                dve.wait_ge(hg_dve, 2)
                dve.memset(ch(keep)[:, :, 0:1], 0.0).then_inc(hg_dve, 1)
                dve.memset(am[:, :, :], 0.0).then_inc(hg_dve, 1)
                dve.wait_ge(hg_act, 2)
                dve.tensor_scalar(oml[:, :], lb[:, :], -1.0, 1.0, ALU.mult, ALU.add).then_inc(hg_dve, 1)
                dve.wait_ge(hg_dve, 5)
                for h in range(4):
                    dve.tensor_scalar(forget[:, h, :], sig[:, h, :], oml[:, h:h + 1], lb[:, h:h + 1], ALU.mult, ALU.add).then_inc(hg_dve, 1)
                dve.wait_ge(hg_dve, 9)
                dve.tensor_scalar(fl(key), fl(forget), -1.0, 1.0, ALU.mult, ALU.add).then_inc(hg_dve, 1)
                dve.wait_ge(hg_act, 5)
                dve.tensor_tensor_scan(fl(G), fl(keep), fl(logf), 0.0, ALU.mult, ALU.add).then_inc(hg_dve, 1)
                dve.wait_ge(hg_dve, 11)
                dve.tensor_tensor(ch(d1), ch(G), at_end(G, HG_CHUNK // 2 - 1), ALU.subtract).then_inc(hg_dve, 1)
                dve.tensor_tensor(ch(d4), at_end(G, HG_CHUNK - 1), ch(G), ALU.subtract).then_inc(hg_dve, 1)
                dve.wait_ge(hg_act, 6)
                dve.scalar_tensor_tensor(out=fl(qa), in0=fl(qs), scalar=P ** -0.5, in1=fl(e1), op0=ALU.mult, op1=ALU.mult).then_inc(hg_dve, 1)
                dve.wait_ge(hg_act, 7)
                dve.tensor_tensor(fl(ka), fl(key), fl(e2), ALU.mult).then_inc(hg_dve, 1)
                dve.wait_ge(hg_act, 8)
                dve.scalar_tensor_tensor(out=fl(qi), in0=fl(qs), scalar=P ** -0.5, in1=fl(e3), op0=ALU.mult, op1=ALU.mult).then_inc(hg_dve, 1)
                dve.wait_ge(hg_act, 9)
                dve.tensor_tensor(fl(ki), fl(key), fl(e4), ALU.mult).then_inc(hg_dve, 1)
                dve.wait_ge(mix_loaded, 48)
                mask = mk("hg_mask").bitcast(I32).unsqueeze(1).broadcast_to([P, HG_HEADS, P])
                for b in range(TB):
                    dve.wait_ge(hg_pe, 1 + b)
                    dve.copy_predicated(am[:, b, :].rearrange("p (h t) -> p h t", t=P), mask,
                                        ps[:, b, :].rearrange("p (h t) -> p h t", t=P)).then_inc(hg_dve, 1)
                dve.wait_ge(hg_pe, 5)
                dve.tensor_copy(S[:, 0, :], ps[:, 4, :]).then_inc(hg_dve, 1)
                for n in range(1, 3):
                    dve.wait_ge(hg_dve, 16 + 4 * n)
                    dve.wait_ge(hg_pe, 5 + n)
                    for h in range(4):
                        end = n * HG_CHUNK + HG_CHUNK - 1
                        o = slice(h * P, h * P + P)
                        dve.scalar_tensor_tensor(out=S[:, n, o], in0=S[:, n - 1, o], scalar=e3[:, h, end:end + 1], in1=ps[:, 4 + n, o],
                                                 op0=ALU.mult, op1=ALU.add).then_inc(hg_dve, 1)
                dve.wait_ge(hg_act, 14)
                dve.reciprocal(rstd[:, :, :].rearrange("p b n -> p (b n)"), osq[:, :, :].rearrange("p b n -> p (b n)")).then_inc(hg_dve, 1)
                dve.wait_ge(hg_dve, 29)
                for b in range(TB):
                    for h in range(4):
                        o = slice(h * P, h * P + P)
                        dve.scalar_tensor_tensor(out=on[:, h, b * P:b * P + P], in0=ps[:, b, o], scalar=v("hg_out", h), in1=rstd[:, b, o],
                                                 op0=ALU.mult, op1=ALU.mult).then_inc(hg_dve, 1)
                dve.wait_ge(hg_dve, 37)
                dve.tensor_tensor(mixT[:, 0:4, :].rearrange("p h t -> p (h t)"), fl(on), fl(gate), ALU.mult)

            @block.sync
            def _(sp):
                loads(sp, lot_end(HG_END_LOT) + RAW)

            @block.tensor
            def _(pe):
                pe.wait_ge(hg_cond, 1)
                ada_lot_pe(pe, HG_LOT, 4)
                pe.wait_ge(hg_dve, 15)
                for b in range(TB):
                    for h in range(4):
                        o, t = slice(h * P, h * P + P), slice(b * P, b * P + P)
                        mm = pe.matmul(ps[:, b, o], ka[:, h, t], qa[:, h, t], start=True, stop=True)
                    mm.then_inc(hg_pe, 1)
                pe.wait_ge(hg_dve, 17)
                for b in range(TB):
                    for h in range(4):
                        o, t = slice(h * P, h * P + P), slice(b * P, b * P + P)
                        mm = pe.transpose(ps[:, 2 + b, o], ki[:, h, t], k("ident"))
                    mm.then_inc(hg_pe, 1)
                pe.wait_ge(ada_out.h, ada_out.at(1))
                for n in range(3):
                    b, r = n // 2, slice((n % 2) * HG_CHUNK, (n % 2) * HG_CHUNK + HG_CHUNK)
                    pe.wait_ge(hg_act, 10 + b)
                    for h in range(4):
                        o = slice(h * P, h * P + P)
                        mm = pe.matmul(ps[:, 4 + n, o], kiT[r, b, o], hg_v[r, b, o], start=True, stop=True)
                    mm.then_inc(hg_pe, 1)
                for b in range(TB):
                    pe.wait_ge(hg_dve, 19)
                    for h in range(4):
                        o = slice(h * P, h * P + P)
                        pe.matmul(ps[:, b, o], hg_v[:, b, o], am[:, b, o], start=(h == 0), stop=False, skip_group_check=True)
                    for n in range(max(1, 2 * b), 2 * b + 2):
                        pe.wait_ge(hg_dve, 16 + 4 * n)
                        for h in range(4):
                            at = h * P + (n % 2) * HG_CHUNK
                            mm = pe.matmul(ps[:, b, at:at + HG_CHUNK], S[:, n - 1, h * P:h * P + P], qi[:, h, n * HG_CHUNK:n * HG_CHUNK + HG_CHUNK],
                                           start=False, stop=True, skip_group_check=True)
                    mm.then_inc(hg_pe, 1)
                pe.wait_ge(hg_act, 13)
                for b in range(TB):
                    mm = pe.matmul(ps[:, 2 + b, :], k("ones"), osq[:, b, :], start=True, stop=True)
                mm.then_inc(hg_pe, 1)
                ada_lot_pe(pe, HG_END_LOT, 4)

        ada_out.advance(2)

        head_norm_stage(nqk, 6, lambda c: v("nsa_q") if c < 4 else v("nsa_k", c - 3), lot=QK_LOT)

        kcn = mb("kcn", [P, N_CMP])
        vcs = mb("vcs", [N_CMP, P])
        gates = mb("gates", [P, TB, 3 * NSA_HEADS])
        cmp_act, cmp_dve, cmp_pe_step = sem("cmp_act_step"), sem("cmp_dve_step"), sem("cmp_pe_step")
        with ExitStack() as own, nc.Block() as block:
            win = own.enter_context(nc.sbuf_tensor("win", [P, 2, CMP_LEN, N_CMP], F32))
            rows = own.enter_context(nc.sbuf_tensor("cmp_rows", [N_CMP, 2, P], F32))
            hid = own.enter_context(nc.sbuf_tensor("cmp_hid", [P, 2, N_CMP], F32))
            csq = own.enter_context(nc.sbuf_tensor("cmp_sq", [P, N_CMP], F32))
            crs = own.enter_context(nc.sbuf_tensor("cmp_rstd", [P, N_CMP], F32))
            c3 = cin[:, :, :].rearrange("p i (n l) -> p i l n", l=CMP_STRIDE)

            @block.sync
            def _(sp):
                loads(sp, lot_end(CMP_LOT) + RAW)

            @block.vector
            def _(dve):
                for i in range(2):
                    for j in range(2):
                        l = slice(j * CMP_STRIDE, j * CMP_STRIDE + CMP_STRIDE)
                        dve.tensor_tensor(win[:, i, l, :], c3[:, i, :, j:j + N_CMP],
                                          cmp_pe[:, i, l].unsqueeze(2).broadcast_to([P, CMP_STRIDE, N_CMP]), ALU.add).then_inc(cmp_dve, 1)
                dve.wait_ge(cmp_act, 7)
                dve.reciprocal(crs[:, :], csq[:, :]).then_inc(cmp_dve, 1)
                dve.wait_ge(cmp_dve, 5)
                dve.scalar_tensor_tensor(out=kcn[:, :], in0=ps[:, 2, 0:N_CMP], scalar=v("nsa_k", 0), in1=crs[:, :], op0=ALU.mult, op1=ALU.mult)
                dve.tensor_copy(vcs[:, :], ps[0:N_CMP, 3, 0:P])

            @block.tensor
            def _(pe):
                for i in range(2):
                    pe.wait_ge(cmp_dve, 2 * i + 2)
                    per = PIECE // P
                    for l in range(CMP_LEN):
                        g = at_cmp + (i * CMP_LEN + l) // per
                        if l % per == 0:
                            piece_loaded(pe, g)
                        o = l % per * P
                        mm = pe.matmul(ps[0:N_CMP, i, 0:P], win[:, i, l, :], raw[:, g % RAW, o:o + P], start=(l == 0), stop=(l == CMP_LEN - 1))
                        if l % per == per - 1:
                            mm.then_inc(raw_used, 1)
                for i in range(2):
                    pe.wait_ge(cmp_act, 1 + i)
                    pe.transpose(ps[:, 5 + i, 0:N_CMP], rows[:, i, :], k("ident")[0:N_CMP, 0:N_CMP]).then_inc(cmp_pe_step, 1)
                pe.wait_ge(cmp_act, 4)
                pe.matmul(ps[:, 2, 0:N_CMP], cmp_w2[:, 0, :], hid[:, 0, :], start=True, stop=True).then_inc(cmp_pe_step, 1)
                pe.matmul(ps[0:N_CMP, 3, 0:P], hid[:, 1, :], cmp_w2[:, 1, :], start=True, stop=True).then_inc(cmp_pe_step, 1)
                a, b = lot_tiles(CMP_LOT)
                ada_tile_pe(pe, a, CMP_LOT, 5)
                pe.wait_ge(cmp_act, 6)
                pe.matmul(ps[:, 4, 0:N_CMP], k("ones64"), csq[:, :], start=True, stop=True).then_inc(cmp_pe_step, 1)
                for t in range(a + 1, b):
                    ada_tile_pe(pe, t, CMP_LOT, 5)

            @block.scalar
            def _(act):
                for i in range(2):
                    act.wait_ge(raw_used, pieces[at_cmp][3] + (i + 1) * CMP_LEN * P // PIECE)
                    act.activation(rows[:, i, :], ps[0:N_CMP, i, 0:P], ACT.Gelu_apprx_tanh).then_inc(cmp_act, 1)
                for i in range(2):
                    act.wait_ge(cmp_pe_step, 1 + i)
                    act.activation(hid[:, i, :], ps[:, 5 + i, 0:N_CMP], ACT.Copy).then_inc(cmp_act, 1)
                act.activation(gates[:, :, :], nv[:, :, 256:280], ACT.Sigmoid).then_inc(cmp_act, 1)
                act.wait_ge(cmp_pe_step, 4)
                act.activation(csq[:, :], ps[:, 2, 0:N_CMP], ACT.Square).then_inc(cmp_act, 1)
                a, b = lot_tiles(CMP_LOT)
                ada_tile_act(act, a, CMP_LOT, 5)
                act.wait_ge(cmp_pe_step, 5)
                act.activation(csq[:, :], ps[:, 4, 0:N_CMP], ACT.Sqrt, bias=eps[:, :], scale=1.0 / 64).then_inc(cmp_act, 1)
                for t in range(a + 1, b):
                    ada_tile_act(act, t, CMP_LOT, 5)
        ada_out.advance(1)

        scores_done, biased, max_done = signal("scores_done"), signal("biased"), signal("max_done")
        exp_done, probs_done, turned = signal("exp_done"), signal("probs_done"), signal("turned")
        turned_out, attended, attended_out = signal("turned_out"), signal("attended"), signal("attended_out")
        probs_link, output_hi = signal("probs_link"), signal("output_hi")
        with ExitStack() as own, nc.Block() as block:
            def ob(name, shape):
                return own.enter_context(nc.sbuf_tensor(name, shape, F32))

            W3 = 512 + N_CMP
            DEEP = 5
            sc = ob("nsa_sc", [P, 2, W3])
            pr = ob("nsa_pr", [P, DEEP, W3])
            nm = ob("nsa_nm", [P, DEEP, 3])
            sums, coef = ob("nsa_sums", [P, DEEP, 3]), ob("nsa_coef", [P, DEEP, 3])
            pT = ob("nsa_pT", [P, 2, 512])
            cT = ob("nsa_cT", [N_CMP, 2, P])
            units = [(c, half, qb) for c in range(NSA_G) for half in range(2) for qb in range(TB)]
            N = len(units)
            dist = mk("dist").rearrange("p (b t) -> p b t", b=TB)
            cdist = mk("cdist").rearrange("p (b t) -> p b t", b=TB)
            cmask = mk("cmask").rearrange("p (b t) -> p b t", b=TB)

            def head_of(u):
                return units[u][0] + NSA_G * units[u][1]

            @block.sync
            def _(sp):
                loads(sp, lot_end(NSA_LOT) + RAW)

            @block.tensor
            def _(pe):
                for i in range(N + 5):
                    if i == 2:
                        ada_lot_pe(pe, NSA_LOT, 5)
                    if i == 3:
                        pe.wait_ge(ada_out.h, ada_out.at(1))
                    if i < N:
                        c, half, qb = units[i]
                        r = slice(64 * half, 64 * half + 64)
                        q = nqk[r, c, qb * P:qb * P + P]
                        if i >= 2:
                            pe.wait_ge(max_done.h, max_done.at(i - 1))
                        pe.matmul(ps[:, i % 2, 0:256], q, nqk[r, 4, :], start=True, stop=True)
                        pe.matmul(ps[:, i % 2, 256:512], q, nqk[r, 5, :], start=True, stop=True)
                        if i >= 1:
                            pe.wait_ge(biased.h, biased.at(2 * i - 1))
                        pe.matmul(ps[:, 2, 0:N_CMP], q, kcn[r, :], start=True, stop=True).then_inc(scores_done.h, 1)
                    if 0 <= i - 3 < N:
                        u = i - 3
                        pe.wait_ge(probs_done.h, probs_done.at(u + 1))
                        if u >= 2:
                            pe.wait_ge(turned_out.h, turned_out.at(u - 1))
                        for j in range(4):
                            pe.transpose(ps[:, 3 + u % 2, j * P:j * P + P], pr[:, u % DEEP, j * P:j * P + P], k("ident"))
                        if u >= 1:
                            pe.wait_ge(turned_out.h, turned_out.at(u))
                        pe.transpose(ps[0:N_CMP, 5, 0:P], pr[:, u % DEEP, 512:W3], k("ident")).then_inc(turned.h, 1)
                    if 0 <= i - 5 < N:
                        u = i - 5
                        _, half, _ = units[u]
                        vcol = slice(64 * half, 64 * half + 64)
                        wcol = slice(P + 64 * half, P + 64 * half + 64)
                        pe.wait_ge(turned_out.h, turned_out.at(u + 1))
                        if u >= 2:
                            pe.wait_ge(attended_out.h, attended_out.at(u - 1))
                        o = ps[64 * half:64 * half + 64, 6 + u % 2, 0:P]
                        pe.matmul(o, nv[:, 0, vcol], pT[:, u % 2, 0:P], start=True, stop=False)
                        pe.matmul(o, nv[:, 1, vcol], pT[:, u % 2, P:2 * P], start=False, stop=False)
                        pe.matmul(o, nv[:, 0, wcol], pT[:, u % 2, 2 * P:3 * P], start=False, stop=False)
                        pe.matmul(o, nv[:, 1, wcol], pT[:, u % 2, 3 * P:4 * P], start=False, stop=False)
                        pe.matmul(o, vcs[:, vcol], cT[:, u % 2, :], start=False, stop=True).then_inc(attended.h, 1)

            @block.vector
            def _(dve):
                for i in range(N + 6):
                    new, old = i < N, 0 <= i - 2 < N
                    if new:
                        at, qb = i % DEEP, units[i][2]
                        slope = float(2.0 ** (-8.0 * (head_of(i) + 1) / NSA_HEADS))
                    if old:
                        u, s3 = i - 2, (i - 2) % DEEP
                        qu, h3 = units[u][2], 3 * head_of(u)
                        dve.wait_ge(exp_done.h, exp_done.at(3 * u + 3))
                        dve.scalar_tensor_tensor(out=pr[:, s3, 512:W3], in0=pr[:, s3, 512:W3], scalar=1.0, in1=cmask[:, qu, :],
                                                 op0=ALU.mult, op1=ALU.mult, accum_out=sums[:, s3, 2:3]).then_inc(probs_link.h, 1)
                    if new:
                        dve.wait_ge(scores_done.h, scores_done.at(i + 1))
                        dve.scalar_tensor_tensor(out=sc[:, i % 2, 512:W3], in0=cdist[:, qb, :], scalar=slope,
                                                 in1=ps[:, 2, 0:N_CMP], op0=ALU.mult, op1=ALU.add).then_inc(biased.h, 1)
                        dve.scalar_tensor_tensor(out=sc[:, i % 2, 0:512].rearrange("p (a t) -> p a t", a=2),
                                                 in0=dist[:, qb:qb + 1, :].broadcast_to([P, 2, T]), scalar=slope,
                                                 in1=ps[:, i % 2, :].rearrange("p (a t) -> p a t", a=2),
                                                 op0=ALU.mult, op1=ALU.add).then_inc(biased.h, 1)
                    if old:
                        dve.wait_ge(probs_link.h, probs_link.at(4 * u + 1))
                        dve.tensor_scalar(sums[:, s3, :], sums[:, s3, :], 1e-30, None, ALU.max).then_inc(probs_link.h, 1)
                    if new:
                        dve.wait_ge(biased.h, biased.at(2 * i + 1))
                        dve.tensor_reduce(nm[:, at, 2:3], sc[:, i % 2, 512:W3], AX.X, ALU.max, negate=True)
                    if old:
                        dve.wait_ge(probs_link.h, probs_link.at(4 * u + 2))
                        dve.reciprocal(coef[:, s3, :], sums[:, s3, :]).then_inc(probs_link.h, 1)
                    if new:
                        dve.wait_ge(biased.h, biased.at(2 * i + 2))
                        dve.tensor_reduce(nm[:, at, 0:2], sc[:, i % 2, 0:512].rearrange("p (a t) -> p a t", a=2), AX.X, ALU.max, negate=True).then_inc(max_done.h, 1)
                    if old:
                        dve.wait_ge(probs_link.h, probs_link.at(4 * u + 3))
                        dve.tensor_tensor(coef[:, s3, 0:2], coef[:, s3, 0:2], gates[:, qu, h3 + 1:h3 + 3], ALU.mult)
                        dve.tensor_tensor(coef[:, s3, 2:3], coef[:, s3, 2:3], gates[:, qu, h3:h3 + 1], ALU.mult).then_inc(probs_link.h, 1)
                    if 0 <= i - 6 < N:
                        w = i - 6
                        c, half, qw = units[w]
                        dve.wait_ge(attended.h, attended.at(w + 1))
                        r = slice(64 * half, 64 * half + 64)
                        dve.tensor_copy(mixT[r, 4 + c, qw * P:qw * P + P], ps[r, 6 + w % 2, 0:P]).then_inc(attended_out.h, 1)
                    if old:
                        dve.wait_ge(probs_link.h, probs_link.at(4 * u + 4))
                        dve.tensor_scalar(pr[:, s3, 0:256], pr[:, s3, 0:256], coef[:, s3, 0:1], None, ALU.mult)
                        dve.tensor_scalar(pr[:, s3, 256:512], pr[:, s3, 256:512], coef[:, s3, 1:2], None, ALU.mult)
                        dve.tensor_scalar(pr[:, s3, 512:W3], pr[:, s3, 512:W3], coef[:, s3, 2:3], None, ALU.mult).then_inc(probs_done.h, 1)

            @block.scalar
            def _(act):
                for i in range(N + 4):
                    if i == 2:
                        ada_lot_act(act, NSA_LOT, 5)
                    if 0 <= i - 4 < N:
                        u = i - 4
                        act.wait_ge(turned.h, turned.at(u + 1))
                        if u >= 2:
                            act.wait_ge(attended.h, attended.at(u - 1))
                        act.activation(pT[:, u % 2, :], ps[:, 3 + u % 2, :], ACT.Copy)
                        act.activation(cT[:, u % 2, :], ps[0:N_CMP, 5, 0:P], ACT.Copy).then_inc(turned_out.h, 1)
                    if i < N:
                        act.wait_ge(max_done.h, max_done.at(i + 1))
                        if i >= DEEP:
                            act.wait_ge(turned.h, turned.at(i - DEEP + 1))
                        for j, (a, b) in enumerate(((0, 256), (256, 512), (512, W3))):
                            acc = {"accum_out": sums[:, i % DEEP, j:j + 1]} if j < 2 else {}
                            act.activation(pr[:, i % DEEP, a:b], sc[:, i % 2, a:b], ACT.Exp, bias=nm[:, i % DEEP, j:j + 1], **acc).then_inc(exp_done.h, 1)
        ada_out.advance(1)
        for s, n in ((scores_done, 1), (biased, 2), (max_done, 1), (exp_done, 3), (probs_link, 4), (probs_done, 1),
                     (turned, 1), (turned_out, 1), (attended, 1), (attended_out, 1)):
            s.advance(n * N)

        head_norm_stage(mixT[:, 4:8, :], 4, lambda c: v("nsa_out", c), lot=OUT_LOT)

        def add_to_tokens(n):
            return None, lambda dve, place: dve.tensor_tensor(hT[:, n, :], hT[:, n, :], place, ALU.add)

        x_space = ctx.enter_context(ExitStack())
        ffn_norm = Norm(hT, T, lambda c, s: v("ffn_norm", c), dst=x_space.enter_context(nc.sbuf_tensor("x_ffn", [P, C, T], F32, side="right")), early=True)
        product_stage(at_wout, aH, wide_tiles(C, T, add_to_tokens), before=Parted(mixT, aH, C), then=ffn_norm)
        mixer.close()

        peer = ctx.enter_context(ExitStack())

        def pb(name, shape, dt=F32):
            return peer.enter_context(nc.sbuf_tensor(name, shape, dt))

        ffn_norm.parts = xH = [pb(n, [P, C, T], F32R) for n in ("xT_hi", "xT_lo")]
        keyT, wT = pb("keyT", [P, 2, T]), pb("wT", [P, T])

        top_act, top_dve, sel_step = sem("top_act_step"), sem("top_dve_step"), sem("sel_step")
        with ExitStack() as own:
            def ob(name, shape, dt=F32):
                return own.enter_context(nc.sbuf_tensor(name, shape, dt))

            qT = ob("qT", [P, PK_SETS, T])
            product_stage(at_wq, xH, wide_tiles(PK_SETS, T, lambda j: copied(j, qT[:, j, :])),
                          before=ffn_norm)
            x_space.close()
            ks = ob("key_scores", [P, TB, PK_SETS, PK_KEYS])
            top_s = ob("top_s", [P, TB, PK_HEADS, 2, PK_TOP])
            top_i = ob("top_i", [P, TB, PK_HEADS, 2, PK_TOP], U32)
            top_f = ob("top_f", [P, PK_HEADS, 2, PK_TOP], BF16)
            cand = ob("cand", [P, PK_HEADS, PK_TOP, PK_TOP])
            best_s = ob("best_s", [P, PK_HEADS, PK_TOP])
            best_c = ob("best_c", [P, PK_HEADS, PK_TOP], U32)
            half_u = ob("half_u", [P, 2, PK_HK], U32)
            half_f = ob("half_f", [P, 2, PK_HK], BF16)
            pick = ob("pick", [P, PK_HK, PK_TOP], BF16)
            places = ob("places", [P, PK_TOP], BF16)
            expert = ob("expert", [P, TB, 3, PK_HK])
            shifted = ob("shifted", [P, PK_HEADS, PK_TOP])
            total = ob("total", [P, PK_HEADS])
            with nc.Block() as block:
                @block.sync
                def _(sp):
                    loads(sp, at_experts + RAW)

                tile0, tile_end = lot_tiles(TOP_LOT)

                @block.tensor
                def _(pe):
                    per = PIECE // PK_KEYS
                    for g in range(4):
                        w = at_keys + 4 * g // per
                        piece_loaded(pe, w)
                        for b in range(TB):
                            for j in range(4 * g, 4 * g + 4):
                                mm = pe.matmul(ps[:, 4 * b + g, j % 4 * P:j % 4 * P + P], qT[:, j, b * P:b * P + P],
                                               raw[:, w % RAW, j % per * PK_KEYS:j % per * PK_KEYS + PK_KEYS], start=True, stop=True)
                            mm.then_inc(top_pe, 1)
                    pe.wait_ge(top_act, 8)
                    ada_lot_pe(pe, TOP_LOT, 4)
                    for b in range(TB):
                        pe.wait_ge(sel_step, 13 * b + 13)
                        for i in range(3):
                            mm = pe.transpose(ps[:, i, b * P:b * P + P], expert[:, b, i, :], k("ident"))
                    mm.then_inc(top_pe, 1)

                @block.scalar
                def _(act):
                    for n in range(8):
                        g, b = n // 2, n % 2
                        act.wait_ge(top_pe, n + 1)
                        act.activation(ks[:, b, 4 * g:4 * g + 4, :].rearrange("p j n -> p (j n)"), ps[:, 4 * b + g, :], ACT.Copy).then_inc(top_act, 1)
                    ends = (tile0 + 5, tile0 + 11, tile_end)
                    for b in range(TB):
                        for t in range(ends[b - 1] if b else tile0, ends[b]):
                            ada_tile_act(act, t, TOP_LOT, 4)
                        act.wait_ge(sel_step, 13 * b + 1)
                        act.activation(shifted[:, :, :], shifted[:, :, :], ACT.Exp).then_inc(top_act, 1)
                    for t in range(ends[TB - 1], tile_end):
                        ada_tile_act(act, t, TOP_LOT, 4)
                    act.wait_ge(top_pe, 9)
                    for i, dst in enumerate((keyT[:, 0, :], keyT[:, 1, :], wT[:, :])):
                        act.activation(dst, ps[:, i, 0:T], ACT.Copy)

                @block.vector
                def _(dve):
                    done = 1
                    dve.tensor_copy(places[:, :], k("iota", 0, PK_TOP)).then_inc(top_dve, 1)
                    for b in range(TB):
                        def best(n, values, s8, i8, load):
                            nonlocal done
                            for turn in range(2):
                                for j in range(n):
                                    if turn == 0:
                                        load(j)
                                    else:
                                        dve.wait_ge(top_dve, done - n + j + 1)
                                    dve.max(s8(j, turn), values(j)).then_inc(top_dve, 1)
                                done += n
                                for j in range(n):
                                    dve.wait_ge(top_dve, done - n + j + 1)
                                    dve.max_index(i8(j, turn), s8(j, turn), values(j)).then_inc(top_dve, 1)
                                done += n
                                if turn == 0:
                                    for j in range(n):
                                        dve.wait_ge(top_dve, done - n + j + 1)
                                        dve.match_replace(values(j), s8(j, 0), values(j), LOWEST).then_inc(top_dve, 1)
                                    done += n

                        def scored(j):
                            dve.wait_ge(top_act, 2 * (j // 4) + b + 1)

                        best(PK_SETS, lambda j: ks[:, b, j, :], lambda j, t: top_s[:, b, j // 2, j % 2, 8 * t:8 * t + 8],
                             lambda j, t: top_i[:, b, j // 2, j % 2, 8 * t:8 * t + 8], scored)
                        dve.wait_ge(top_dve, done)
                        dve.tensor_tensor(cand[:, :, :, :], top_s[:, b, :, 0, :].unsqueeze(3).broadcast_to([P, PK_HEADS, PK_TOP, PK_TOP]),
                                          top_s[:, b, :, 1, :].unsqueeze(2).broadcast_to([P, PK_HEADS, PK_TOP, PK_TOP]), ALU.add).then_inc(top_dve, 1)
                        done += 1
                        dve.wait_ge(top_dve, done)
                        best(PK_HEADS, lambda h: cand[:, h, :, :].rearrange("p a b -> p (a b)"), lambda h, t: best_s[:, h, 8 * t:8 * t + 8],
                             lambda h, t: best_c[:, h, 8 * t:8 * t + 8], lambda h: None)
                        dve.wait_ge(top_dve, done)
                        s0 = 13 * b
                        dve.tensor_tensor(shifted[:, :, :], best_s[:, :, :], best_s[:, :, 0:1].broadcast_to([P, PK_HEADS, PK_TOP]), ALU.subtract).then_inc(sel_step, 1)
                        flat_c = best_c[:, :, :].rearrange("p h k -> p (h k)")
                        dve.tensor_scalar(half_u[:, 0, :], flat_c, 4, None, ALU.logical_shift_right).then_inc(sel_step, 1)
                        dve.tensor_scalar(half_u[:, 1, :], flat_c, PK_TOP - 1, None, ALU.bitwise_and).then_inc(sel_step, 1)
                        dve.tensor_copy(top_f[:, :, :, :].rearrange("p h c k -> p (h c k)"), top_i[:, b, :, :, :].rearrange("p h c k -> p (h c k)")).then_inc(sel_step, 1)
                        dve.wait_ge(sel_step, s0 + 3)
                        dve.tensor_copy(half_f[:, :, :], half_u[:, :, :]).then_inc(sel_step, 1)
                        for i in range(2):
                            dve.wait_ge(sel_step, s0 + 5 + 3 * i)
                            dve.tensor_tensor(pick[:, :, :], half_f[:, i, :].unsqueeze(2).broadcast_to([P, PK_HK, PK_TOP]),
                                              places[:, :].unsqueeze(1).broadcast_to([P, PK_HK, PK_TOP]), ALU.is_equal).then_inc(sel_step, 1)
                            dve.wait_ge(sel_step, s0 + 6 + 3 * i)
                            p4 = pick[:, :, :].rearrange("p (h k) j -> p h k j", h=PK_HEADS)
                            dve.tensor_tensor(p4, p4, top_f[:, :, i, :].unsqueeze(2).broadcast_to([P, PK_HEADS, PK_TOP, PK_TOP]), ALU.mult).then_inc(sel_step, 1)
                            dve.wait_ge(sel_step, s0 + 7 + 3 * i)
                            dve.tensor_reduce(expert[:, b, i, :], pick[:, :, :], AX.X, ALU.add).then_inc(sel_step, 1)
                        dve.wait_ge(top_act, 9 + b)
                        dve.tensor_reduce(total[:, :], shifted[:, :, :], AX.X, ALU.add).then_inc(sel_step, 1)
                        dve.wait_ge(sel_step, s0 + 12)
                        dve.reciprocal(total[:, :], total[:, :]).then_inc(top_dve, 1)
                        done += 1
                        dve.wait_ge(top_dve, done)
                        dve.tensor_tensor(expert[:, b, 2, :].rearrange("p (h k) -> p h k", h=PK_HEADS), shifted[:, :, :],
                                          total[:, :].unsqueeze(2).broadcast_to([P, PK_HEADS, PK_TOP]), ALU.mult).then_inc(sel_step, 1)
                        if b == 0:
                            dve.wait_ge(sel_step, 13)

        ada_out.advance(1)
        row_space.close()
        route = pb("route", [P, T, PK_KEYS])
        BATCH, SLOTS = 2, 4
        hot, weighted_hot, route_mm, route_out = sem("hot"), sem("weighted_hot"), sem("route_mm"), sem("route_out")
        with ExitStack() as own, nc.Block() as block:
            ohs = own.enter_context(nc.sbuf_tensor("one_hots", [P, SLOTS, 2, BATCH, PK_KEYS], F32))
            BATCHES = T // BATCH
            ROUNDS = BATCHES // SLOTS

            @block.vector
            def _(dve):
                def turn(r, steps, first=False):
                    for s in range(steps):
                        if not first:
                            dve.wait_ge(route_mm, SLOTS * r + (s - SLOTS + 1))
                        dve.tensor_tensor(ohs[:, s, :, :, :], k("iota").unsqueeze(1).unsqueeze(1).broadcast_to([P, 2, BATCH, PK_KEYS]),
                                          keyT[:, :, bass.ds((SLOTS * r + s) * BATCH, BATCH)].unsqueeze(3).broadcast_to([P, 2, BATCH, PK_KEYS]),
                                          ALU.is_equal).then_inc(hot, 1)
                turn(0, SLOTS, True)
                with dve.Fori(1, ROUNDS) as r:
                    turn(r, SLOTS)
                turn(ROUNDS, BATCHES - ROUNDS * SLOTS)
                for g in ahead(at_experts):
                    split_lo(dve, g)

            @block.gpsimd
            def _(pool):
                def turn(r, steps):
                    for s in range(steps):
                        pool.wait_ge(hot, SLOTS * r + (s + 1))
                        pool.tensor_tensor(ohs[:, s, 1, :, :], ohs[:, s, 1, :, :],
                                           wT[:, bass.ds((SLOTS * r + s) * BATCH, BATCH)].unsqueeze(2).broadcast_to([P, BATCH, PK_KEYS]),
                                           ALU.mult).then_inc(weighted_hot, 1)
                with pool.Fori(0, ROUNDS) as r:
                    turn(r, SLOTS)
                turn(ROUNDS, BATCHES - ROUNDS * SLOTS)

            @block.tensor
            def _(pe):
                def turn(r, steps, first=False):
                    for s in range(steps):
                        pe.wait_ge(weighted_hot, SLOTS * r + (s + 1))
                        if not first:
                            pe.wait_ge(route_out, SLOTS * r + (s - SLOTS + 1))
                        for q in range(BATCH):
                            mm = pe.matmul(ps[:, s, q * P:q * P + P], ohs[:, s, 0, q, :], ohs[:, s, 1, q, :], start=True, stop=True)
                        mm.then_inc(route_mm, 1)
                turn(0, SLOTS, True)
                with pe.Fori(1, ROUNDS) as r:
                    turn(r, SLOTS)
                turn(ROUNDS, BATCHES - ROUNDS * SLOTS)

            @block.scalar
            def _(act):
                def turn(r, steps):
                    for s in range(steps):
                        act.wait_ge(route_mm, SLOTS * r + (s + 1))
                        act.activation(route[:, bass.ds((SLOTS * r + s) * BATCH, BATCH), :].rearrange("p t n -> p (t n)"), ps[:, s, 0:BATCH * P],
                                       ACT.Copy).then_inc(route_out, 1)
                for g in ahead(at_experts):
                    split_hi(act, g)
                with act.Fori(0, ROUNDS) as r:
                    turn(r, SLOTS)
                turn(ROUNDS, BATCHES - ROUNDS * SLOTS)

        split_upto[0] = at_experts + len(ahead(at_experts))

        GROUPS = PK_KEYS
        LOOP = 18
        assert 2 * LOOP % RAW == 0 and 2 * LOOP % SPLIT == 0 and LOOP % 3 == 0 and LOOP % 2 == 0
        TURNS = (GROUPS - 2) // LOOP - 1
        REST = range(2 + TURNS * LOOP, GROUPS)
        LAST = 2 * GROUPS - 1
        after_experts = at_experts + LAST + 1
        n0 = pieces[at_experts][3]
        gelu_done, weighted, weighted_hi, weighted_lo = sem("gelu_done"), sem("weighted"), sem("weighted_hi"), sem("weighted_lo")

        def keys_at(i):
            return i if i < 2 else 2 * i - 2

        def values_at(i):
            return min(2 * i + 3, GROUPS + i)

        with ExitStack() as own, nc.Block() as block:
            ga = own.enter_context(nc.sbuf_tensor("ga", [P, 2, T], F32))
            gh = own.enter_context(nc.sbuf_tensor("gh", [P, 2, T], F32R))
            gl = own.enter_context(nc.sbuf_tensor("gl", [P, 2, T], F32R))

            @block.sync
            def _(sp):
                first = at_experts + 2 * LOOP + RAW
                loads(sp, first)
                turns = (LAST + 1 - 2 * LOOP - RAW) // (2 * LOOP)
                with sp.Fori(0, turns) as r:
                    for e in range(2 * LOOP + RAW, 4 * LOOP + RAW):
                        g = at_experts + e
                        sp.wait_ge(lo_done, 2 * LOOP * r + (n0 + e - RAW + 1))
                        sp.dma_start(raw[:, g % RAW, :], dr["experts_t"][bass.ds(2 * LOOP * r + e, 1)].rearrange("a p n -> p (a n)")).then_inc(raw_loaded[g % RAW], 16)
                next_load[0] = first + 2 * LOOP * turns
                loads(sp, after_experts + len(ahead(after_experts)) + RAW)

            def hi(act, r, e):
                g, n = at_experts + e, n0 + e
                act.wait_ge(raw_loaded[g % RAW], 16 * (g // RAW + 1) + 16 * (2 * LOOP // RAW) * r)
                act.wait_ge(piece_used, 2 * LOOP * r + (n - SPLIT + 1))
                act.activation(whi[:, n % SPLIT, :], raw[:, g % RAW, :], ACT.Copy).then_inc(hi_done, 1)

            def lo(dve, r, e):
                g, n = at_experts + e, n0 + e
                dve.wait_ge(hi_done, 2 * LOOP * r + (n + 1))
                dve.tensor_tensor(wlo[:, n % SPLIT, :], raw[:, g % RAW, :], whi[:, n % SPLIT, :].bitcast(F32), ALU.subtract).then_inc(lo_done, 1)

            @block.tensor
            def _(pe):
                def keys(r, i, early=False):
                    n = n0 + keys_at(i)
                    pe.wait_ge(lo_done, 2 * LOOP * r + (n + 1))
                    if not early:
                        pe.wait_ge(gelu_done, LOOP * r + (i - 2))
                    for c in range(C):
                        mm = products(pe, ps[:, 4 + i % 3, 0:T], [w[:, n % SPLIT, c * P:c * P + P] for w in (whi, wlo)],
                                      [y[:, c, :] for y in xH], c == 0, c == C - 1)
                    mm.then_inc(piece_used, 1)

                def values(r, i, start=False, stop=False):
                    n = n0 + values_at(i)
                    pe.wait_ge(lo_done, 2 * LOOP * r + (n + 1))
                    pe.wait_ge(weighted_lo, LOOP * r + (i + 1))
                    for c in range(C):
                        place = ps[:, c // 2, c % 2 * T:c % 2 * T + T]
                        w = [w[:, n % SPLIT, c * P:c * P + P] for w in (whi, wlo)]
                        pe.matmul(place, w[0], gh[:, i % 2, :], start=(start and c % 2 == 0), stop=False, skip_group_check=True)
                        pe.matmul(place, w[0], gl[:, i % 2, :], start=False, stop=False, skip_group_check=True)
                        mm = pe.matmul(place, w[1], gh[:, i % 2, :], start=False, stop=stop, skip_group_check=True)
                    mm.then_inc(piece_used, 1)

                for i in range(3):
                    keys(0, i, early=True)
                values(0, 0, start=True)
                keys(0, 3)
                values(0, 1)
                with pe.Fori(0, TURNS) as r:
                    for i in range(2, 2 + LOOP):
                        keys(r, i + 2)
                        values(r, i)
                for i in REST:
                    if i + 2 < GROUPS:
                        keys(0, i + 2)
                    values(0, i, stop=(i == GROUPS - 1))

            @block.scalar
            def _(act):
                def group(r, i, then):
                    act.wait_ge(piece_used, 2 * LOOP * r + (n0 + keys_at(i) + 1))
                    if i >= 2:
                        act.wait_ge(weighted_lo, LOOP * r + (i - 1))
                    act.activation(ga[:, i % 2, :], ps[:, 4 + i % 3, 0:T], ACT.Gelu_apprx_tanh).then_inc(gelu_done, 1)
                    for e in then[:1]:
                        hi(act, r, e)
                    act.wait_ge(weighted, LOOP * r + (i + 1))
                    if i >= 2:
                        act.wait_ge(piece_used, 2 * LOOP * r + (n0 + values_at(i - 2) + 1))
                    act.activation(gh[:, i % 2, :], ga[:, i % 2, :], ACT.Copy).then_inc(weighted_hi, 1)
                    for e in then[1:]:
                        hi(act, r, e)
                for e in range(3):
                    if at_experts + e >= split_upto[0]:
                        split_hi(act, at_experts + e)
                for i in range(2):
                    group(0, i, [i + 3])
                with act.Fori(0, TURNS) as r:
                    for i in range(2, 2 + LOOP):
                        group(r, i, [2 * i + 1, 2 * i + 2])
                for i in REST:
                    group(0, i, [e for e in (2 * i + 1, 2 * i + 2) if e <= LAST])
                for g in ahead(after_experts):
                    split_hi(act, g)

            @block.vector
            def _(dve):
                def group(r, i, then):
                    dve.wait_ge(gelu_done, LOOP * r + (i + 1))
                    at = bass.ds(LOOP * r + i, 1)
                    dve.tensor_tensor(ga[:, i % 2, :], ga[:, i % 2, :], route[:, :, at].rearrange("p t a -> p (t a)"), ALU.mult).then_inc(weighted, 1)
                    for e in then[:1]:
                        lo(dve, r, e)
                    dve.wait_ge(weighted_hi, LOOP * r + (i + 1))
                    dve.tensor_tensor(gl[:, i % 2, :], ga[:, i % 2, :], gh[:, i % 2, :].bitcast(F32), ALU.subtract).then_inc(weighted_lo, 1)
                    for e in then[1:]:
                        lo(dve, r, e)
                for e in range(3):
                    if at_experts + e >= split_upto[0]:
                        split_lo(dve, at_experts + e)
                for i in range(2):
                    group(0, i, [i + 3])
                with dve.Fori(0, TURNS) as r:
                    for i in range(2, 2 + LOOP):
                        group(r, i, [2 * i + 1, 2 * i + 2])
                for i in REST:
                    group(0, i, [e for e in (2 * i + 1, 2 * i + 2) if e <= LAST])
                for g in ahead(after_experts):
                    split_lo(dve, g)
                dve.wait_ge(piece_used, n0 + LAST + 1)
                dve.tensor_tensor(hT[:, :, :].rearrange("p c t -> p (c t)"), hT[:, :, :].rearrange("p c t -> p (c t)"),
                                  ps[:, 0:4, :].rearrange("p b n -> p (b n)"), ALU.add)
        split_upto[0] = after_experts + len(ahead(after_experts))
        peer.close()

        h2 = ctx.enter_context(nc.sbuf_tensor("h2", [P, C, TT], F32))
        x2H = [ctx.enter_context(nc.sbuf_tensor(n, [P, C, TT], F32R)) for n in ("x2_hi", "x2_lo")]
        x2 = ctx.enter_context(nc.sbuf_tensor("x2", [P, C, TT], F32))
        ctx_loaded, mod_step = sem("ctx_loaded"), sem("mod_step")

        def mix_norm(i):
            return Norm(h2, TT, lambda c, s: gs1[:, i, c, s:s + 1], lambda c, s: mod[:, i, c, s:s + 1], segs=2, parts=x2H, dst=x2,
                        logs=True, early=True)

        def ffn_norm_of(i, w):
            return Norm(h2[:, :, 0:w], w, lambda c, s: gs2[:, i, c, s:s + 1], lambda c, s: mod[:, i, 3 * C + c, s:s + 1],
                        segs=w // T, parts=[y[:, :, 0:w] for y in x2H], dst=x2[:, :, 0:w], logs=w > T, early=True)

        def finish_modulations(dve):
            every = mod[:, :, :, :].rearrange("p l j s -> p (l j) s")
            dve.tensor_tensor(every, every, v("ada_b", 0, LAYERS * N_MOD * C).unsqueeze(2).broadcast_to([P, LAYERS * N_MOD * C, 2]), ALU.add).then_inc(mod_step, 1)
            dve.wait_ge(mod_step, 1)
            for i in range(LAYERS):
                for g, name, at in ((gs1, "mix2", C), (gs2, "ffn2", 4 * C)):
                    dve.scalar_tensor_tensor(out=g[:, i, :, :], in0=mod[:, i, at:at + C, :], scalar=1.0,
                                             in1=v(name, i * C, C).unsqueeze(2).broadcast_to([P, C, 2]), op0=ALU.add, op1=ALU.mult)

        with ExitStack() as own:
            def ob(name, shape, dt=F32):
                return own.enter_context(nc.sbuf_tensor(name, shape, dt))

            xgH = [ob(n, [P, C, T], F32R) for n in ("xg_hi", "xg_lo")]
            pT_in, pH = ob("pT_in", [P, 2, T]), [ob(n, [P, 2, T], F32R) for n in ("pT_hi", "pT_lo")]
            sg = ob("sg", [P, C, T])
            p_loaded, ple_step = sem("p_loaded"), sem("ple_step")

            def load_streams(sp):
                sp.dma_start(pT_in[:, :, :], dr["p_t"]).then_inc(p_loaded, 16)
                sp.dma_start(h2[:, :, T:TT], dr["ctx_t"]).then_inc(ctx_loaded, 16)

            def gate(n):
                return (lambda act, place: act.activation(sg[:, n, :], place, ACT.Sigmoid)), None

            def gated(n):
                def add(dve, place):
                    if n == 0:
                        dve.wait_ge(act_evacuated.h, act_evacuated.at(C))
                        dve.wait_ge(ctx_loaded, 16)
                    dve.tensor_tensor(sg[:, n, :], sg[:, n, :], place, ALU.mult).then_inc(ple_step, 1)
                    dve.wait_ge(ple_step, n + 1)
                    return dve.tensor_tensor(h2[:, n, 0:T], hT[:, n, :], sg[:, n, :], ALU.add)
                return None, add
            mix0_norm = mix_norm(0)
            product_stage(at_ple, xgH, wide_tiles(C, T, gate) + [(1, 2, 512, [("wide", j * P, slice(0, T), *gated(4 * t + j)) for j in range(4)])
                                                                 for t in range(2)],
                          before=Norm(hT, T, lambda c, s: v("ple_norm", c), parts=xgH), also=(Parted(pT_in, pH, 2, after=C, loaded=p_loaded), 2),
                          sync=load_streams, then=mix0_norm, last=finish_modulations)
        tokens.close()

        def attention(units, name, bias_loaded=None):
            N, N_BIAS = len(units), sum(u[2] is not None for u in units)
            WIDE = max(u[1].shape[-1] for u in units)
            DEEP, BANKS = 5, (0, 1, 6, 7)
            with ExitStack() as own, nc.Block() as block:
                pr = own.enter_context(nc.sbuf_tensor(name + "_pr", [P, DEEP, WIDE], F32))
                nm = own.enter_context(nc.sbuf_tensor(name + "_nm", [P, DEEP], F32))
                sums = own.enter_context(nc.sbuf_tensor(name + "_sums", [P, DEEP], F32))
                inv = own.enter_context(nc.sbuf_tensor(name + "_inv", [P, DEEP], F32))
                pT = own.enter_context(nc.sbuf_tensor(name + "_pT", [P, 2, WIDE], F32))

                def nk(u):
                    return units[u][1].shape[-1]

                def scores(i):
                    return ps[:, BANKS[i % len(BANKS)], 0:nk(i)]

                @block.tensor
                def _(pe):
                    for i in range(N + 5):
                        if i < N:
                            q, keys, _, _, _, _ = units[i]
                            if i >= len(BANKS):
                                pe.wait_ge(exp_done.h, exp_done.at(i - len(BANKS) + 1))
                            pe.matmul(scores(i), q, keys, start=True, stop=True).then_inc(scores_done.h, 1)
                        if 0 <= i - 3 < N:
                            u = i - 3
                            pe.wait_ge(probs_done.h, probs_done.at(u + 1))
                            if u >= 2:
                                pe.wait_ge(turned_out.h, turned_out.at(u - 1))
                            for j in range(nk(u) // P):
                                mm = pe.transpose(ps[:, 2 + u % 2, j * P:j * P + P], pr[:, u % DEEP, j * P:j * P + P], k("ident"))
                            mm.then_inc(turned.h, 1)
                        if 0 <= i - 5 < N:
                            u = i - 5
                            _, _, _, values, half, _ = units[u]
                            pe.wait_ge(turned_out.h, turned_out.at(u + 1))
                            if u >= 2:
                                pe.wait_ge(attended_out.h, attended_out.at(u - 1))
                            for j in range(nk(u) // P):
                                mm = pe.matmul(ps[64 * half:64 * half + 64, 4 + u % 2, 0:P], values[j], pT[:, u % 2, j * P:j * P + P],
                                               start=(j == 0), stop=(j == nk(u) // P - 1))
                            mm.then_inc(attended.h, 1)

                @block.vector
                def _(dve):
                    if bias_loaded:
                        dve.wait_ge(bias_loaded, 16)
                    for i in range(N + 6):
                        if i < N:
                            _, _, bias, _, _, _ = units[i]
                            dve.wait_ge(scores_done.h, scores_done.at(i + 1))
                            if i >= DEEP:
                                dve.wait_ge(exp_done.h, exp_done.at(i - DEEP + 1))
                            if bias is not None:
                                dve.tensor_tensor(scores(i)[:, 0:T], scores(i)[:, 0:T], bias, ALU.add).then_inc(biased.h, 1)
                                dve.wait_ge(biased.h, biased.at(i + 1))
                            dve.tensor_reduce(nm[:, i % DEEP:i % DEEP + 1], scores(i), AX.X, ALU.max, negate=True).then_inc(max_done.h, 1)
                        if 0 <= i - 2 < N:
                            u, at = i - 2, (i - 2) % DEEP
                            dve.wait_ge(exp_done.h, exp_done.at(u + 1))
                            dve.reciprocal(inv[:, at:at + 1], sums[:, at:at + 1]).then_inc(probs_link.h, 1)
                            dve.wait_ge(probs_link.h, probs_link.at(u + 1))
                            dve.tensor_scalar(pr[:, at, 0:nk(u)], pr[:, at, 0:nk(u)], inv[:, at:at + 1], None, ALU.mult).then_inc(probs_done.h, 1)
                        if 0 <= i - 6 < N:
                            u = i - 6
                            _, _, _, _, half, place = units[u]
                            dve.wait_ge(output_hi.h, output_hi.at(u + 1))
                            dve.tensor_tensor(place[1], ps[64 * half:64 * half + 64, 4 + u % 2, 0:P], place[0].bitcast(F32), ALU.subtract).then_inc(attended_out.h, 1)

                @block.scalar
                def _(act):
                    for i in range(N + 6):
                        if 0 <= i - 6 < N:
                            u = i - 6
                            _, _, _, _, half, place = units[u]
                            act.wait_ge(attended.h, attended.at(u + 1))
                            act.activation(place[0], ps[64 * half:64 * half + 64, 4 + u % 2, 0:P], ACT.Copy).then_inc(output_hi.h, 1)
                        if 0 <= i - 4 < N:
                            u = i - 4
                            act.wait_ge(turned.h, turned.at(u + 1))
                            if u >= 2:
                                act.wait_ge(attended.h, attended.at(u - 1))
                            act.activation(pT[:, u % 2, 0:nk(u)], ps[:, 2 + u % 2, 0:nk(u)], ACT.Copy).then_inc(turned_out.h, 1)
                        if i < N:
                            act.wait_ge(max_done.h, max_done.at(i + 1))
                            if i >= DEEP:
                                act.wait_ge(turned.h, turned.at(i - DEEP + 1))
                            act.activation(pr[:, i % DEEP, 0:nk(i)], scores(i), ACT.Exp, bias=nm[:, i % DEEP:i % DEEP + 1],
                                           accum_out=sums[:, i % DEEP:i % DEEP + 1]).then_inc(exp_done.h, 1)
            for s in (scores_done, max_done, exp_done, probs_link, probs_done, turned, turned_out, attended, output_hi, attended_out):
                s.advance(N)
            biased.advance(N_BIAS)

        def add_gated(i, n, at, w):
            def go(dve, place):
                for s in range(w // T):
                    o = h2[:, n, s * T:s * T + T]
                    ins = dve.scalar_tensor_tensor(out=o, in0=place[:, s * T:s * T + T], scalar=mod[:, i, at + n, s:s + 1], in1=o, op0=ALU.mult, op1=ALU.add)
                return ins
            return None, go

        def feed_forward(i, w, norm, then):
            parts = [y[:, :, 0:w] for y in x2H]
            with ExitStack() as own:
                hid = [own.enter_context(nc.sbuf_tensor(f"ffn_{n}{i}", [P, FC, w], F32R)) for n in ("hi", "lo")]
                tmp = own.enter_context(nc.sbuf_tensor(f"ffn_tmp{i}", [P, 4, w], F32))

                def activated(t, j):
                    f = 2 * t + j
                    factor = ps[:, 4 * (t % 2) + 2 + j, 0:w]
                    return (lambda act, place: act.activation(tmp[:, f % 4, :], place, ACT.Silu),
                            lambda dve, place: dve.tensor_tensor(tmp[:, f % 4, :], factor, tmp[:, f % 4, :], ALU.mult))

                def parted(t, j):
                    f = 2 * t + j

                    def high(act, place):
                        act.wait_ge(dve_evacuated.h, dve_evacuated.at(4 * t + j + 1))
                        return act.activation(hid[0][:, f, :], tmp[:, f % 4, :], ACT.Copy)
                    return high, lambda dve, place: dve.tensor_tensor(hid[1][:, f, :], tmp[:, f % 4, :], hid[0][:, f, :].bitcast(F32), ALU.subtract)

                product_stage(at_f1[i], parts, [(4, 2, 512, [("wide", j * P, slice(0, w), *(activated(t, j) if j < 2 else parted(t, j - 2)))
                                                             for j in range(4)]) for t in range(FC // 2)], before=norm)

                with nc.Block() as block:
                    g0 = at_f2[i]
                    after = ahead(g0 + FC)

                    @block.sync
                    def _(sp):
                        loads(sp, g0 + FC + RAW)

                    @block.tensor
                    def _(pe):
                        for f in range(FC):
                            n_ = pieces[g0 + f][3]
                            pe.wait_ge(lo_done, n_ + 1)
                            for n in range(C):
                                mm = products(pe, ps[:, n, 0:w], [y[:, n_ % SPLIT, n * P:n * P + P] for y in (whi, wlo)],
                                              [y[:, f, :] for y in hid], f == 0, f == FC - 1)
                            mm.then_inc(piece_used, 1)
                        then.sums(pe, False)

                    @block.scalar
                    def _(act):
                        for g in range(max(g0, split_upto[0]), g0 + FC + len(after)):
                            split_hi(act, g)
                        then.squares(act, 0, C)
                        then.load_table(act)

                    @block.vector
                    def _(dve):
                        for g in range(max(g0, split_upto[0]), g0 + FC + len(after)):
                            split_lo(dve, g)
                        dve.wait_ge(piece_used, pieces[g0 + FC - 1][3] + 1)
                        for n in range(C):
                            add_gated(i, n, 5 * C, w)[1](dve, ps[:, n, 0:w]).then_inc(dve_evacuated.h, 1)
                dve_evacuated.advance(C)
                then.end_early(False)
                split_upto[0] = g0 + FC + len(after)

        with ExitStack() as own:
            def ob(name, shape):
                return own.enter_context(nc.sbuf_tensor(name, shape, F32))

            qT, kT, vt = ob("na_q", [P, C, TT]), ob("na_k", [P, C, TT]), ob("na_v", [P, TT // P, D])
            bias = ob("na_bias", [P, HEADS, TB, T])
            oT = x2H
            bias_loaded = sem("bias_loaded")
            product_stage(at_qkv[0], x2H,
                          wide_tiles(C, TT, lambda n: copied(n, qT[:, n, :], DH ** -0.5)) + wide_tiles(C, TT, lambda n: copied(n, kT[:, n, :]))
                          + [(4, 2, 512, [("tall", slice(0, 512), b * P, *copied(b, vt[:, b, n * 512:n * 512 + 512])) for b in range(TT // P)])
                             for n in range(2)], before=mix0_norm,
                          sync=lambda sp: sp.dma_start(bias[:, :, :, :], dr["na_bias_t"]).then_inc(bias_loaded, 16))
            units, ctx_units = [], []
            for h in range(HEADS):
                half, c = h % 2, h // 2
                r = slice(64 * half, 64 * half + 64)
                for qb in range(TB):
                    q0 = qb * P
                    units.append((qT[r, c, q0:q0 + P], kT[r, c, :], bias[:, h, qb, :], [vt[:, j, h * DH:h * DH + DH] for j in range(4)],
                                  half, [y[r, c, q0:q0 + P] for y in oT]))
                    q0 += T
                    ctx_units.append((qT[r, c, q0:q0 + P], kT[r, c, T:TT], None, [vt[:, j, h * DH:h * DH + DH] for j in (2, 3)],
                                      half, [y[r, c, q0:q0 + P] for y in oT]))
            attention(units + ctx_units, "na", bias_loaded)
            ffn0_norm = ffn_norm_of(0, TT)
            product_stage(at_o[0], oT, wide_tiles(C, TT, lambda n: add_gated(0, n, 2 * C, TT)), then=ffn0_norm, fold=True)
        mix1_norm = mix_norm(1)
        feed_forward(0, TT, ffn0_norm, mix1_norm)

        with ExitStack() as own:
            def ob(name, shape):
                return own.enter_context(nc.sbuf_tensor(name, shape, F32))

            qT, kT, vt = ob("gqa_q", [P, C, T]), ob("gqa_k", [P, 2, TT]), ob("gqa_v", [P, TT // P, GQA_KV * DH])
            rope = ob("rope", [P, 2, T])
            rope_loaded, swap_done, rope_step = sem("rope_loaded"), sem("swap_done"), sem("rope_step")
            sq = ob("gqa_squares", [P, 2 + C // 2, TT])

            def squared(dst, square):
                def go(act, place):
                    act.activation(square, place, ACT.Square)
                    return act.activation(dst, place, ACT.Copy)
                return go, None
            product_stage(at_qkv[1], x2H, wide_tiles(C, T, lambda n: squared(qT[:, n, :], sq[:, 2 + n // 2, n % 2 * T:n % 2 * T + T])) + [
                (2, 4, 256, [("wide", n * P, slice(0, TT), *squared(kT[:, n, :], sq[:, n, :])) for n in range(2)]),
                (2, 4, 256, [("tall", slice(0, 256), b * P, *copied(b, vt[:, b, :])) for b in range(TT // P)])], before=mix1_norm,
                          sync=lambda sp: sp.dma_start(rope[:, :, :].rearrange("p a t -> p (a t)"), dr["rope_consts"]).then_inc(rope_loaded, 16))
            groups = [(kT[:, c, :], kT[:, c:c + 1, 0:T], "gqa_k") for c in range(2)]
            groups += [(qT[:, c:c + 2, :].rearrange("p c t -> p (c t)"), qT[:, c:c + 2, :], "gqa_q") for c in range(0, C, 2)]
            NG = len(groups)
            with ExitStack() as inner, nc.Block() as block:
                def ib(name, n):
                    return inner.enter_context(nc.sbuf_tensor(name, [P, n, 512], F32))

                rstd, rot, cosine = ib("gqa_rstd", NG), ib("rot", 2), ib("cosine", 2)
                gq_sum, gq_log, gq_rstd, gq_normed, cos_done, rotated = (
                    sem(n) for n in ("gq_sum", "gq_log", "gq_rstd", "gq_normed", "cos_done", "rotated"))

                def tokens_of(n):
                    return groups[n][1].shape[1] * T

                HALF = NG // 2

                @block.scalar
                def _(act):
                    for batch in (range(HALF), range(HALF, NG)):
                        for n in batch:
                            act.wait_ge(gq_sum, n + 1)
                            act.activation(sq[:, n, :], ps[:, n, :], ACT.Ln, bias=eps[:, :], scale=1.0 / DH).then_inc(gq_log, 1)
                        for n in batch:
                            act.wait_ge(gq_log, n + 1)
                            act.activation(rstd[:, n, :], sq[:, n, :], ACT.Exp, scale=-0.5).then_inc(gq_rstd, 1)

                @block.tensor
                def _(pe):
                    for n in range(NG):
                        pe.matmul(ps[:, n, :], k("ones64"), sq[:, n, :], start=True, stop=True).then_inc(gq_sum, 1)
                    for n in range(NG):
                        pe.wait_ge(gq_normed, n + 1)
                        if n >= 2:
                            pe.wait_ge(rope_step, n - 1)
                        pe.matmul(ps[:, NG + n % 2, 0:tokens_of(n)], k("swap"), groups[n][1], start=True, stop=True).then_inc(swap_done, 1)

                def columns(x, n):
                    return x[:, n % 2, 0:tokens_of(n)].rearrange("p (c t) -> p c t", t=T)

                def table(j, n):
                    return rope[:, j:j + 1, :].broadcast_to([P, groups[n][1].shape[1], T])

                @block.vector
                def _(dve):
                    for i in range(NG + 1):
                        if i < NG:
                            x, _, gain = groups[i]
                            dve.wait_ge(gq_rstd, i + 1)
                            dve.scalar_tensor_tensor(out=x, in0=x, scalar=v(gain), in1=rstd[:, i, :], op0=ALU.mult, op1=ALU.mult).then_inc(gq_normed, 1)
                        if i >= 1:
                            n = i - 1
                            dve.wait_ge(swap_done, n + 1)
                            dve.tensor_tensor(columns(rot, n), ps[:, NG + n % 2, 0:tokens_of(n)].rearrange("p (c t) -> p c t", t=T),
                                              table(1, n), ALU.mult).then_inc(rope_step, 1)
                            dve.wait_ge(rope_step, n + 1)
                            dve.wait_ge(cos_done, n + 1)
                            dve.tensor_tensor(groups[n][1], columns(rot, n), columns(cosine, n), ALU.add).then_inc(rotated, 1)

                @block.gpsimd
                def _(pool):
                    pool.wait_ge(rope_loaded, 16)
                    for n in range(NG):
                        pool.wait_ge(gq_normed, n + 1)
                        if n >= 2:
                            pool.wait_ge(rotated, n - 1)
                        pool.tensor_tensor(columns(cosine, n), groups[n][1], table(0, n), ALU.mult).then_inc(cos_done, 1)
            units = []
            oT = x2H
            for c in range(C):
                for half in range(2):
                    r, kv = slice(64 * half, 64 * half + 64), 2 * (c // 4) + half
                    for qb in range(TB):
                        q0 = qb * P
                        units.append((qT[r, c, q0:q0 + P], kT[r, c // 4, :], None, [vt[:, j, kv * DH:kv * DH + DH] for j in range(4)],
                                      half, [y[r, c, q0:q0 + P] for y in oT]))
            attention(units, "gqa")
            ffn1_norm = ffn_norm_of(1, T)
            product_stage(at_o[1], oT, wide_tiles(C, T, lambda n: add_gated(1, n, 2 * C, T)), then=ffn1_norm)
        final_norm = Norm(h2[:, :, 0:T], T, lambda c, s: v("final", c), dst=x2[:, :, 0:T], early=True)
        feed_forward(1, T, ffn1_norm, final_norm)

        with ExitStack() as own, nc.Block() as block:
            final_norm.buffers(own)

            @block.scalar
            def _(act):
                final_norm.act(act, None)

            @block.vector
            def _(dve):
                final_norm.dve(dve, None)

            @block.sync
            def _(sp):
                for part in range(2):
                    c = slice(part * C // 2, part * C // 2 + C // 2)
                    sp.wait_ge(scaled_done.h, scaled_done.at(c.stop))
                    sp.dma_start(dr["out_t"][:, c, :], x2[:, c, 0:T]).then_inc(out_stored, 16)
                sp.wait_ge(out_stored, 32)



def _feature_major(a):
    return np.ascontiguousarray(a.T.reshape(-1, P, a.shape[0]).transpose(1, 0, 2))


def _column(a):
    return a.reshape(-1, P).T


def _tiles(w, width=512, per=2):
    kk, n = w.shape
    return np.ascontiguousarray(w.reshape(kk // (per * P), per, P, n // width, width).transpose(3, 0, 2, 1, 4).reshape(-1, P, per * width))


def _heads(order, width=64):
    return np.concatenate([np.arange(h * width, h * width + width) for h in order])


def _layouts(a):
    f = {n: np.asarray(x) for n, x in a.items()}
    o = {}
    consts, mix_consts, rope = const_tables()
    o["consts"], o["mix_consts"], o["rope_consts"] = consts, mix_consts, rope
    o["x_t"] = _feature_major(f["x"][0])
    o["p_t"] = _feature_major(f["p"][0, 0])
    o["ctx_t"] = _feature_major(f["ctx_2"][0])
    nsa, gqa = _heads(NSA_ORDER), _heads(GQA_ORDER)

    w = f["w_in"][0]
    hq, hf, hi, hg, nq, nkc, nvc, nks, nvs, nkw, nvw, ng = np.split(w, np.cumsum([512] * 5 + [128] * 6), axis=1)
    o["w_in_t"] = [_tiles(hf), _tiles(hq), _tiles(nq[:, nsa]), _tiles(np.concatenate([nkc, nvc, nks, nkw], axis=1)),
                   _tiles(hg), _tiles(hi), _tiles(np.concatenate([nvs, nvw, ng], axis=1), 280)]
    w1 = f["cmp_w1"][0].reshape(2, CMP_LEN, 64, 64)
    both = np.zeros((2, P, CMP_LEN, P), w1.dtype)
    both[:, 0:64, :, 0:64] = w1.transpose(0, 2, 1, 3)
    both[:, 64:, :, 64:] = w1.transpose(0, 2, 1, 3)
    o["cmp_w1_t"] = np.ascontiguousarray(both.reshape(2, P, -1, PIECE).transpose(0, 2, 1, 3).reshape(-1, P, PIECE))
    w2 = np.zeros((P, 2, P), w1.dtype)
    w2[0:64, :, 0:64] = f["cmp_w2"][0].transpose(1, 0, 2)
    w2[64:, :, 64:] = f["cmp_w2"][0].transpose(1, 0, 2)
    o["cmp_w2_t"] = w2
    o["cmp_pe_t"] = np.ascontiguousarray(np.tile(f["cmp_pe"][0].transpose(2, 0, 1), (2, 1, 1)))
    wo = f["w_out"][0]
    o["w_out_t"] = _tiles(np.concatenate([wo[:512], wo[512:][nsa]]))
    o["peer_wq_t"] = _tiles(f["peer_wq"][0])
    o["peer_keys_t"] = np.ascontiguousarray(f["peer_keys"][0].reshape(PK_SETS * PK_KEYS // PIECE, -1, P).transpose(0, 2, 1))
    u = f["peer_u"][0].reshape(PK_KEYS, PK_KEYS, C, P).transpose(1, 3, 2, 0).reshape(PK_KEYS, P, D)
    vals = f["peer_v"][0].reshape(PK_KEYS, PK_KEYS, D).transpose(1, 0, 2)
    e = np.empty((2 * PK_KEYS, P, PIECE), u.dtype)
    e[0:2], e[2:-3:2] = u[:2], u[2:]
    e[3:-2:2], e[-2:] = vals[:-2], vals[-2:]
    o["experts_t"] = e
    o["ple_gate_t"] = _tiles(f["ple_gate_w"][0])
    o["ple_proj_t"] = _tiles(f["ple_proj"][0])
    o["ada_t"] = np.concatenate([_tiles(f["ada_w_2"][i]) for i in range(LAYERS)])
    o["qkv0_t"] = _tiles(f["na_w_qkv_2"][0])
    o["o0_t"] = _tiles(f["na_w_o_2"][0])
    g = f["gqa_w_qkv_2"][0]
    kv = GQA_KV * DH
    o["qkv1_t"] = [_tiles(g[:, :D][:, gqa]), _tiles(g[:, D:D + kv], kv, 4), _tiles(g[:, D + kv:], kv, 4)]
    o["o1_t"] = _tiles(f["gqa_w_o_2"][0][gqa])
    for i in range(LAYERS):
        wi = f["ffn_w_in_2"][i].reshape(D, 2, FC // 2, 2 * P).transpose(0, 2, 1, 3).reshape(D, -1)
        o[f"ffn_in{i}_t"] = _tiles(wi)
        o[f"ffn_out{i}_t"] = np.ascontiguousarray(f["ffn_w_out_2"][i].reshape(FC, P, D))

    t = np.arange(T)
    rows = T // GRID_W
    assert rows <= NA_WIN_H
    drow = (t // GRID_W)[None, :] - (t // GRID_W)[:, None] + NA_WIN_H - 1
    start = np.clip(t % GRID_W - NA_WIN_W // 2, 0, GRID_W - NA_WIN_W)[:, None]
    inside = ((t % GRID_W)[None, :] >= start) & ((t % GRID_W)[None, :] < start + NA_WIN_W)
    dcol = np.clip((t % GRID_W)[None, :] - (t % GRID_W)[:, None] + NA_WIN_W - 1, 0, 2 * NA_WIN_W - 2)
    b = np.where(inside[None], f["na_rpb_2"][0][:, drow, dcol], np.float32(NEG))
    o["na_bias_t"] = np.ascontiguousarray(b.reshape(HEADS, TB, P, T).transpose(2, 0, 1, 3))

    vecs = {"mix_norm": _column(f["mix_norm"][0]), "lb0": _column(f["hg_lb_logits"][0]), "lb1": _column(f["hg_lb_logits"][1]),
            "hg_out": _column(f["hg_out_norm"][0]), "nsa_q": np.tile(f["nsa_q_norm"][0], 2)[:, None],
            "nsa_k": np.tile(f["nsa_k_norm"][0], (1, 2)).T, "nsa_out": _column(f["nsa_out_norm"][0][nsa]),
            "ffn_norm": _column(f["ffn_norm"][0]), "ple_norm": _column(f["ple_gate_norm"][0]),
            "mix2": _column(f["norm_mix_2"].reshape(-1)), "ffn2": _column(f["norm_ffn_2"].reshape(-1)), "final": _column(f["norm_final_2"]),
            "ada_b": _column(f["ada_b_2"].reshape(-1)), "gqa_q": np.tile(f["gqa_q_gain_2"][0], 2)[:, None],
            "gqa_k": np.tile(f["gqa_k_gain_2"][0], 2)[:, None],
            "cond": np.stack([_column(f["c_2"][0]), _column(f["c_ctx_2"])], axis=-1).reshape(P, -1)}
    o["vecs"] = np.ascontiguousarray(np.concatenate([vecs[n] for n, _ in VECS], axis=1))
    return o


def kernel(**inputs):
    import concourse.bacc as bacc
    from concourse.bass_utils import run_bass_kernel_spmd as run

    nc = bacc.Bacc("TRN2", target_bir_lowering=False, num_devices=1)
    arrays, dr = {}, {}

    def given(name, a):
        arrays[name] = np.ascontiguousarray(a)
        return nc.dram_tensor(name, arrays[name].shape, mybir.dt.from_np(arrays[name].dtype), kind="ExternalInput").ap()

    for name, a in _layouts(inputs).items():
        dr[name] = [given(f"{name}_{i}", x) for i, x in enumerate(a)] if isinstance(a, list) else given(name, a)
    dr["out_t"] = nc.dram_tensor("out_t", (P, C, T), F32, kind="ExternalOutput").ap()
    build(nc, dr)
    got = run(nc, [arrays], core_ids=[0]).results[0]["out_t"]
    return np.ascontiguousarray(got.transpose(2, 1, 0).reshape(1, T, D))
```
